# Optimizing a Trainium2 kernel written in Bass

```python
import math
import jax, jax.numpy as jnp
from jax import lax
import numpy as np

D_MODEL = 1024
BATCH = 1
SEQ = 512
DEPTH = 2

GRID_W = 64
N_HEADS = 16
N_KV_HEADS = 4
HEAD_DIM = D_MODEL // N_HEADS
GROUP = N_HEADS // N_KV_HEADS
Q_BLOCK = 128
ROPE_THETA = 10000.0
ATTN_QKV = N_HEADS * HEAD_DIM + 2 * N_KV_HEADS * HEAD_DIM
GLA_HEADS = 4
GLA_DK = D_MODEL // 2 // GLA_HEADS
GLA_DV = D_MODEL // GLA_HEADS
GLA_QK = GLA_HEADS * GLA_DK
GLA_V = GLA_HEADS * GLA_DV
GATE_RANK = 16
GATE_TAU = 16.0
GLA_CHUNK = 64
GLA_IN = 2 * GLA_QK + 2 * GLA_V + 2 * GATE_RANK
D_FF = 4 * D_MODEL
N_MIXERS = 2
N_ATTN = (DEPTH + 1) // 2
N_GLA = DEPTH // 2
EPS = 1e-6


def rmsnorm(x, g):
    x32 = x.astype(jnp.float32)
    y = x32 * lax.rsqrt(jnp.mean(x32 * x32, axis=-1, keepdims=True) + EPS)
    return (y * g.astype(jnp.float32)).astype(x.dtype)

def rope_angles(pos, dim):
    inv = ROPE_THETA ** (-jnp.arange(0, dim, 2, dtype=jnp.float32) / dim)
    ang = pos.astype(jnp.float32)[:, None] * inv[None, :]
    return jnp.cos(ang), jnp.sin(ang)

def apply_rot(x, cos, sin):
    half = x.shape[-1] // 2
    x32 = x.astype(jnp.float32)
    x1, x2 = x32[..., :half], x32[..., half:]
    c = cos[None, :, None, :]
    s = sin[None, :, None, :]
    return jnp.concatenate([x1 * c - x2 * s, x2 * c + x1 * s], axis=-1).astype(x.dtype)

def axial_rope(x, rope):
    cr, sr, cc, sc = rope
    half = HEAD_DIM // 2
    return jnp.concatenate([apply_rot(x[..., :half], cr, sr), apply_rot(x[..., half:], cc, sc)], axis=-1)

def attention_mixer(h, w_qkv, q_g, k_g, w_o, rope):
    B, S, _ = h.shape
    qkv = h @ w_qkv
    q, k, v = jnp.split(qkv, [N_HEADS * HEAD_DIM, (N_HEADS + N_KV_HEADS) * HEAD_DIM], axis=-1)
    q = rmsnorm(q.reshape(B, S, N_HEADS, HEAD_DIM), q_g)
    k = rmsnorm(k.reshape(B, S, N_KV_HEADS, HEAD_DIM), k_g)
    v = v.reshape(B, S, N_KV_HEADS, HEAD_DIM)
    q = axial_rope(q, rope)
    k = axial_rope(k, rope)
    n_blk = S // Q_BLOCK
    qb = jnp.moveaxis(q.reshape(B, n_blk, Q_BLOCK, N_KV_HEADS, GROUP, HEAD_DIM), 1, 0)
    scale = 1.0 / math.sqrt(HEAD_DIM)

    def block(qblk):
        s = jnp.einsum('bqhgd,bkhd->bhgqk', qblk, k, preferred_element_type=jnp.float32) * scale
        p = jax.nn.softmax(s, axis=-1).astype(v.dtype)
        return jnp.einsum('bhgqk,bkhd->bqhgd', p, v)

    o = lax.map(block, qb)
    o = jnp.moveaxis(o, 0, 1).reshape(B, S, N_HEADS * HEAD_DIM)
    return o @ w_o

def gla_chunked(q, k, v, logg):
    B, S, H, DK = q.shape
    DV = v.shape[-1]
    N = S // GLA_CHUNK
    to_c = lambda t: t.reshape(B, N, GLA_CHUNK, H, t.shape[-1]).transpose(0, 3, 1, 2, 4)
    q, k, v, logg = to_c(q), to_c(k), to_c(v), to_c(logg)
    b = jnp.cumsum(logg, axis=3)
    qe = q * jnp.exp(b)
    ke = k * jnp.exp(-b)
    mask = jnp.tril(jnp.ones((GLA_CHUNK, GLA_CHUNK), dtype=bool))
    a = jnp.einsum('bhncd,bhnjd->bhncj', qe, ke)
    a = jnp.where(mask, a, 0.0)
    o_intra = jnp.einsum('bhncj,bhnjv->bhncv', a, v)
    b_last = b[..., -1:, :]
    kd = k * jnp.exp(b_last - b)
    chunk_kv = jnp.einsum('bhncd,bhncv->bhndv', kd, v)
    decay = jnp.exp(b_last[..., 0, :])

    def step(state, inp):
        dec, ckv = inp
        return dec[..., None] * state + ckv, state

    init = jnp.zeros((B, H, DK, DV), jnp.float32)
    _, s_before = lax.scan(step, init, (jnp.moveaxis(decay, 2, 0), jnp.moveaxis(chunk_kv, 2, 0)))
    s_before = jnp.moveaxis(s_before, 0, 2)
    o = o_intra + jnp.einsum('bhncd,bhndv->bhncv', qe, s_before)
    return o.transpose(0, 2, 3, 1, 4).reshape(B, S, H, DV)

def gla_mixer(h, w_in, w_gate_up, b_gate, out_g, w_o):
    B, S, _ = h.shape
    f32 = jnp.float32
    proj = h @ w_in
    q, k, v, r, z = jnp.split(proj, [GLA_QK, 2 * GLA_QK, 2 * GLA_QK + GLA_V, 2 * GLA_QK + 2 * GLA_V], axis=-1)
    q = q.astype(f32).reshape(B, S, GLA_HEADS, GLA_DK) * (GLA_DK ** -0.5)
    k = k.astype(f32).reshape(B, S, GLA_HEADS, GLA_DK)
    v = v.astype(f32).reshape(B, S, GLA_HEADS, GLA_DV)
    z = z.astype(f32).reshape(B, S, 2, GATE_RANK)
    logit = jnp.einsum('bsir,ire->bsie', z, w_gate_up.astype(f32)) + b_gate.astype(f32)
    logg = (jax.nn.log_sigmoid(logit) / GATE_TAU).reshape(B, S, 2, GLA_HEADS, GLA_DK)
    o_f = gla_chunked(q, k, v, logg[:, :, 0])
    flip = lambda t: jnp.flip(t, axis=1)
    o_b = flip(gla_chunked(flip(q), flip(k), flip(v), flip(logg[:, :, 1])))
    o = rmsnorm(o_f + o_b, out_g).reshape(B, S, GLA_V)
    o = o * jax.nn.silu(r.astype(f32))
    return o.astype(h.dtype) @ w_o

def sq_relu_mlp(h, w_in, w_out):
    return jnp.square(jax.nn.relu(h @ w_in)) @ w_out

def first_inputs(seed: int = 0) -> dict:
    key = jax.random.key(seed)
    ks = jax.random.split(key, 16)
    nrm = lambda k, shape, fan_in: jax.random.normal(k, shape, jnp.float32) * (fan_in ** -0.5)
    gain = lambda k, shape: 1.0 + 0.05 * jax.random.normal(k, shape, jnp.float32)
    return {
        'x': jax.random.normal(ks[0], (BATCH, SEQ, D_MODEL), jnp.float32),
        'norm_mix': gain(ks[1], (DEPTH, D_MODEL)),
        'norm_mlp': gain(ks[2], (DEPTH, D_MODEL)),
        'attn_w_qkv': nrm(ks[3], (N_ATTN, D_MODEL, ATTN_QKV), D_MODEL),
        'attn_q_norm': gain(ks[4], (N_ATTN, HEAD_DIM)),
        'attn_k_norm': gain(ks[5], (N_ATTN, HEAD_DIM)),
        'attn_w_o': nrm(ks[6], (N_ATTN, N_HEADS * HEAD_DIM, D_MODEL), N_HEADS * HEAD_DIM),
        'gla_w_in': nrm(ks[7], (N_GLA, D_MODEL, GLA_IN), D_MODEL),
        'gla_w_gate_up': nrm(ks[8], (N_GLA, 2, GATE_RANK, GLA_QK), GATE_RANK),
        'gla_b_gate': 0.1 * jax.random.normal(ks[9], (N_GLA, 2, GLA_QK), jnp.float32),
        'gla_out_norm': gain(ks[10], (N_GLA, GLA_DV)),
        'gla_w_o': nrm(ks[11], (N_GLA, GLA_V, D_MODEL), GLA_V),
        'mlp_w_in': nrm(ks[12], (DEPTH, D_MODEL, D_FF), D_MODEL),
        'mlp_w_out': nrm(ks[13], (DEPTH, D_FF, D_MODEL), D_FF),
        'final_norm': gain(ks[14], (D_MODEL,)),
    }

def first_block(x, norm_mix, norm_mlp, attn_w_qkv, attn_q_norm, attn_k_norm, attn_w_o,
              gla_w_in, gla_w_gate_up, gla_b_gate, gla_out_norm, gla_w_o,
              mlp_w_in, mlp_w_out, final_norm):
    S = x.shape[1]
    rows = S // GRID_W
    row = jnp.repeat(jnp.arange(rows, dtype=jnp.int32), GRID_W)
    col = jnp.tile(jnp.arange(GRID_W, dtype=jnp.int32), rows)
    cr, sr = rope_angles(row, HEAD_DIM // 2)
    cc, sc = rope_angles(col, HEAD_DIM // 2)
    rope = (cr, sr, cc, sc)
    h = x
    for i in range(DEPTH):
        j = i // N_MIXERS
        hn = rmsnorm(h, norm_mix[i])
        if i % N_MIXERS == 0:
            h = h + attention_mixer(hn, attn_w_qkv[j], attn_q_norm[j], attn_k_norm[j], attn_w_o[j], rope)
        else:
            h = h + gla_mixer(hn, gla_w_in[j], gla_w_gate_up[j], gla_b_gate[j], gla_out_norm[j], gla_w_o[j])
        h = h + sq_relu_mlp(rmsnorm(h, norm_mlp[i]), mlp_w_in[i], mlp_w_out[i])
    return rmsnorm(h, final_norm)


DEPTH_2 = 1

CHUNK = 64
HEAD_DIM_2 = 64
A_HEADS = 4
A_LEFT_CHUNKS = 8
A_MAX_REL = 128
B_HEADS = 4
C_HEADS = 4
IDX_HEADS = 4
IDX_DIM = 64
TOPK_MAX = 256
N_BRANCH = 3
MIX_W = 256
D_FF_2 = 2816
CONV_W = 3
NEG = -1e30

COL_SIZES = (MIX_W, MIX_W, MIX_W,
             MIX_W, MIX_W, MIX_W, B_HEADS,
             MIX_W, HEAD_DIM_2, HEAD_DIM_2,
             IDX_HEADS * IDX_DIM, IDX_DIM, IDX_HEADS,
             N_BRANCH * D_MODEL)
N_IN = sum(COL_SIZES)


def _rmsnorm(x, g):
    xf = x.astype(jnp.float32)
    y = xf * lax.rsqrt(jnp.mean(xf * xf, axis=-1, keepdims=True) + EPS)
    return (y * g.astype(jnp.float32)).astype(x.dtype)

def _rope(x, cos, sin):
    xf = x.astype(jnp.float32)
    x1, x2 = jnp.split(xf, 2, axis=-1)
    c = cos[None, :, None, :]
    s = sin[None, :, None, :]
    return jnp.concatenate([x1 * c - x2 * s, x1 * s + x2 * c], axis=-1).astype(x.dtype)

def _blocks_to_seq(out):
    nb, b, blk, h, d = out.shape
    return out.transpose(1, 0, 2, 3, 4).reshape(b, nb * blk, h, d)

def _chunk_band_attention(q, k, v, rel_table):
    S = q.shape[1]
    dh = q.shape[-1]
    n_chunks = S // CHUNK
    pad = A_LEFT_CHUNKS * CHUNK
    band = pad + CHUNK
    kp = jnp.pad(k, ((0, 0), (pad, 0), (0, 0), (0, 0)))
    vp = jnp.pad(v, ((0, 0), (pad, 0), (0, 0), (0, 0)))
    qi = jnp.arange(CHUNK)
    kj = jnp.arange(band)
    rel = qi[:, None] + pad - kj[None, :]
    bias = rel_table[:, jnp.clip(rel, -A_MAX_REL, A_MAX_REL) + A_MAX_REL].astype(jnp.float32)
    scale = dh ** -0.5

    def one_chunk(n):
        start = n * CHUNK
        qc = lax.dynamic_slice_in_dim(q, start, CHUNK, axis=1)
        kc = lax.dynamic_slice_in_dim(kp, start, band, axis=1)
        vc = lax.dynamic_slice_in_dim(vp, start, band, axis=1)
        s = jnp.einsum('bqhd,bkhd->bhqk', qc, kc).astype(jnp.float32) * scale + bias
        valid = (start - pad + kj) >= 0
        s = jnp.where(valid[None, None, None, :], s, NEG)
        p = jax.nn.softmax(s, axis=-1).astype(v.dtype)
        return jnp.einsum('bhqk,bkhd->bqhd', p, vc)

    return _blocks_to_seq(lax.map(one_chunk, jnp.arange(n_chunks)))

def _forgetting_attention(q, k, v, log_f):
    S = q.shape[1]
    dh = q.shape[-1]
    cum = jnp.cumsum(log_f, axis=1).transpose(0, 2, 1)
    kpos = jnp.arange(S)
    scale = dh ** -0.5

    def one_block(i):
        start = i * Q_BLOCK
        qb = lax.dynamic_slice_in_dim(q, start, Q_BLOCK, axis=1)
        cq = lax.dynamic_slice_in_dim(cum, start, Q_BLOCK, axis=2)
        s = jnp.einsum('bqhd,bkhd->bhqk', qb, k).astype(jnp.float32) * scale
        s = s + cq[..., :, None] - cum[:, :, None, :]
        qpos = start + jnp.arange(Q_BLOCK)
        s = jnp.where((kpos[None, :] <= qpos[:, None])[None, None], s, NEG)
        p = jax.nn.softmax(s, axis=-1).astype(v.dtype)
        return jnp.einsum('bhqk,bkhd->bqhd', p, v)

    return _blocks_to_seq(lax.map(one_block, jnp.arange(S // Q_BLOCK)))

def _indexed_sparse_attention(q, k, v, q_idx, k_idx, w_idx):
    S = q.shape[1]
    dh = q.shape[-1]
    topk = min(TOPK_MAX, S // 4)
    chunk_k = jnp.arange(S) // CHUNK
    scale = dh ** -0.5

    def one_block(i):
        start = i * Q_BLOCK
        qb = lax.dynamic_slice_in_dim(q, start, Q_BLOCK, axis=1)
        qib = lax.dynamic_slice_in_dim(q_idx, start, Q_BLOCK, axis=1)
        wb = lax.dynamic_slice_in_dim(w_idx, start, Q_BLOCK, axis=1).astype(jnp.float32)
        logits = jnp.einsum('bqhd,bkd->bqhk', qib, k_idx).astype(jnp.float32)
        score = jnp.einsum('bqh,bqhk->bqk', wb, jax.nn.relu(logits))
        chunk_q = (start + jnp.arange(Q_BLOCK)) // CHUNK
        adm = chunk_k[None, :] <= chunk_q[:, None]
        score = jnp.where(adm[None], score, NEG)
        _, sel = lax.top_k(score, topk)
        sel_ok = chunk_k[sel] <= chunk_q[None, :, None]
        k_sel = jax.vmap(lambda kk, ii: kk[ii])(k, sel)
        v_sel = jax.vmap(lambda vv, ii: vv[ii])(v, sel)
        s = jnp.einsum('bqhd,bqkd->bhqk', qb, k_sel).astype(jnp.float32) * scale
        s = jnp.where(sel_ok[:, None], s, NEG)
        p = jax.nn.softmax(s, axis=-1).astype(v.dtype)
        return jnp.einsum('bhqk,bqkd->bqhd', p, v_sel)

    return _blocks_to_seq(lax.map(one_block, jnp.arange(S // Q_BLOCK)))

def _hybrid_mixer(h, w_in, b_gate, rel_table, b_forget, w_branch, w_out, cos, sin):
    B_, S, _ = h.shape
    z = h @ w_in
    offs = np.cumsum(np.array(COL_SIZES))[:-1].tolist()
    (qa, ka, va, qb, kb, vb, fb, qc, kc, vc, qi, ki, wi, zg) = jnp.split(z, offs, axis=-1)
    heads = lambda t, n: t.reshape(B_, S, n, -1)

    ya = _chunk_band_attention(heads(qa, A_HEADS), heads(ka, A_HEADS), heads(va, A_HEADS), rel_table)

    log_f = jax.nn.log_sigmoid(fb.astype(jnp.float32) + b_forget.astype(jnp.float32))
    yb = _forgetting_attention(heads(qb, B_HEADS), heads(kb, B_HEADS), heads(vb, B_HEADS), log_f)

    qc_r = _rope(heads(qc, C_HEADS), cos, sin)
    kc_r = _rope(kc[:, :, None, :], cos, sin)[:, :, 0, :]
    qi_r = _rope(heads(qi, IDX_HEADS), cos, sin) * (IDX_DIM ** -0.5)
    ki_r = _rope(ki[:, :, None, :], cos, sin)[:, :, 0, :]
    wi_s = wi * (IDX_HEADS ** -0.5)
    yc = _indexed_sparse_attention(qc_r, kc_r, vc, qi_r, ki_r, wi_s)

    gates = jax.nn.sigmoid(zg.reshape(B_, S, N_BRANCH, D_MODEL) + b_gate)
    merged = (gates[:, :, 0] * (ya.reshape(B_, S, MIX_W) @ w_branch[0])
              + gates[:, :, 1] * (yb.reshape(B_, S, MIX_W) @ w_branch[1])
              + gates[:, :, 2] * (yc.reshape(B_, S, MIX_W) @ w_branch[2]))
    return merged @ w_out

def _conv_ffn(h, w_up, conv_w, conv_b, w_down):
    a, g = jnp.split(h @ w_up, 2, axis=-1)
    a = lax.conv_general_dilated(a, conv_w[:, None, :], window_strides=(1,),
                                 padding=[(CONV_W - 1, 0)],
                                 dimension_numbers=('NWC', 'WIO', 'NWC'),
                                 feature_group_count=D_FF_2) + conv_b
    return (jax.nn.gelu(a) * g) @ w_down

def second_inputs(seed: int = 0) -> dict:
    key = jax.random.key(seed)
    ks = jax.random.split(key, 16)
    f32 = jnp.float32
    nrm = lambda k, shape, s: jax.random.normal(k, shape, f32) * s
    return {
        'x': nrm(ks[0], (BATCH, SEQ, D_MODEL), 1.0),
        'c': nrm(ks[1], (BATCH, D_MODEL), 1.0),
        'w_ada': nrm(ks[2], (DEPTH_2, D_MODEL, 6 * D_MODEL), D_MODEL ** -0.5),
        'b_ada': nrm(ks[3], (DEPTH_2, 6 * D_MODEL), 0.01),
        'norm_g': 1.0 + nrm(ks[4], (DEPTH_2, 4, D_MODEL), 0.05),
        'w_in': nrm(ks[5], (DEPTH_2, D_MODEL, N_IN), D_MODEL ** -0.5),
        'b_gate': nrm(ks[6], (DEPTH_2, N_BRANCH, D_MODEL), 0.01),
        'rel_table': nrm(ks[7], (DEPTH_2, A_HEADS, 2 * A_MAX_REL + 1), 0.2),
        'b_forget': jax.random.uniform(ks[8], (DEPTH_2, B_HEADS), f32, 1.0, 4.0),
        'w_branch': nrm(ks[9], (DEPTH_2, N_BRANCH, MIX_W, D_MODEL), MIX_W ** -0.5),
        'w_out': nrm(ks[10], (DEPTH_2, D_MODEL, D_MODEL), D_MODEL ** -0.5),
        'w_up': nrm(ks[11], (DEPTH_2, D_MODEL, 2 * D_FF_2), D_MODEL ** -0.5),
        'conv_w': nrm(ks[12], (DEPTH_2, CONV_W, D_FF_2), CONV_W ** -0.5),
        'conv_b': nrm(ks[13], (DEPTH_2, D_FF_2), 0.01),
        'w_down': nrm(ks[14], (DEPTH_2, D_FF_2, D_MODEL), D_FF_2 ** -0.5),
    }

def second_block(x, c, w_ada, b_ada, norm_g, w_in, b_gate, rel_table, b_forget, w_branch, w_out,
              w_up, conv_w, conv_b, w_down):
    S = x.shape[1]
    pos = jnp.arange(S, dtype=jnp.float32)
    inv_freq = ROPE_THETA ** (-jnp.arange(0, HEAD_DIM_2, 2, dtype=jnp.float32) / HEAD_DIM_2)
    ang = pos[:, None] * inv_freq[None, :]
    cos, sin = jnp.cos(ang), jnp.sin(ang)
    c_act = jax.nn.silu(c)
    for l in range(DEPTH_2):
        mod = (c_act @ w_ada[l] + b_ada[l])[:, None, :]
        sh1, sc1, g1, sh2, sc2, g2 = jnp.split(mod, 6, axis=-1)
        h = _rmsnorm(x, norm_g[l, 0]) * (1.0 + sc1) + sh1
        y = _hybrid_mixer(h, w_in[l], b_gate[l], rel_table[l], b_forget[l], w_branch[l], w_out[l], cos, sin)
        x = x + g1 * _rmsnorm(y, norm_g[l, 1])
        h = _rmsnorm(x, norm_g[l, 2]) * (1.0 + sc2) + sh2
        y = _conv_ffn(h, w_up[l], conv_w[l], conv_b[l], w_down[l])
        x = x + g2 * _rmsnorm(y, norm_g[l, 3])
    return x


def setup_inputs(seed=0):
    out = dict(first_inputs(seed))
    for name, value in second_inputs(seed + 1).items():
        if name != "x":
            out[name + "_2"] = value
    return out


def reference(
    x, norm_mix, norm_mlp, attn_w_qkv, attn_q_norm, attn_k_norm, attn_w_o, gla_w_in,
    gla_w_gate_up, gla_b_gate, gla_out_norm, gla_w_o, mlp_w_in, mlp_w_out, final_norm, c_2,
    w_ada_2, b_ada_2, norm_g_2, w_in_2, b_gate_2, rel_table_2, b_forget_2, w_branch_2, w_out_2,
    w_up_2, conv_w_2, conv_b_2, w_down_2,
):
    x = first_block(
        x, norm_mix, norm_mlp, attn_w_qkv, attn_q_norm, attn_k_norm, attn_w_o, gla_w_in,
        gla_w_gate_up, gla_b_gate, gla_out_norm, gla_w_o, mlp_w_in, mlp_w_out, final_norm,
    )
    return second_block(
        x, c_2, w_ada_2, b_ada_2, norm_g_2, w_in_2, b_gate_2, rel_table_2, b_forget_2,
        w_branch_2, w_out_2, w_up_2, conv_w_2, conv_b_2, w_down_2,
    )


_drawn_inputs = setup_inputs


def setup_inputs(seed=0):
    import zlib

    import numpy as np

    out = dict(_drawn_inputs(seed))
    spreads = {}
    factors = {'attn_q_norm': 5.477,
     'attn_k_norm': 5.869,
     'b_ada_2': 2.711,
     'b_gate_2': 27.701,
     'rel_table_2': 4.588,
     'conv_b_2': 8.0,
     'gla_b_gate': 2.755}
    for name, (base, spread) in spreads.items():
        noise = np.random.default_rng([zlib.crc32(name.encode()), seed]).standard_normal(out[name].shape)
        drawn = base * np.exp(spread * noise) if base else spread * noise
        out[name] = __import__('jax').numpy.asarray(drawn.astype(out[name].dtype))
    for name, factor in factors.items():
        out[name] = (out[name] * factor).astype(out[name].dtype)
    return out
```

```python
from contextlib import ExitStack

import numpy as np

import concourse.bass as bass
import concourse.mybir as mybir

F32 = mybir.dt.float32
F32R = mybir.dt.float32r
ALU = mybir.AluOpType
ACT = mybir.ActivationFunctionType
AX = mybir.AxisListType.X

P = 128
S = 512
D = 1024
KT = D // P
TT = S // P
EPS = 1e-6
NEG = -1e30
TAKEN = -3e38

HD = 64
D_FF = 4096
MLP_UNITS = D_FF // 256
GLA_H = 4
GLA_DK = 128
GLA_DV = 256
CH = 64
NCH = S // CH
TOPK = 128
D_FF2 = 2816
FFN_UNITS = D_FF2 // 256
TAPS = 3

N_QKV, N_PROJ, N_MLP, N_GLA, N_MIX, N_GATE = 6, 4, 2 * MLP_UNITS, 13, 10, 16
N_FFN = 3 * FFN_UNITS
B_QKV = 0
B_WO0 = B_QKV + N_QKV
B_MLP0 = B_WO0 + N_PROJ
B_GLA = B_MLP0 + N_MLP
B_WO1 = B_GLA + N_GLA
B_MLP1 = B_WO1 + N_PROJ
B_MIX = B_MLP1 + N_MLP
B_GATE = B_MIX + N_MIX
B_WOUT = B_GATE + N_GATE
B_FFN = B_WOUT + N_PROJ
N_BLOCKS = B_FFN + N_FFN
N_ADA = 6 * D // 256

PRM = {}
_at = 0
for _name, _n in (("norm_mix", 16), ("norm_mlp", 16), ("final", 8), ("qg", 1), ("kg", 1), ("gla_b", 8), ("out_g", 2),
                  ("b_ada", 48), ("norm_g", 32), ("b_gate", 24), ("b_forget", 1), ("conv", 4 * 2 * FFN_UNITS), ("c", 8),
                  ("eps", 1), ("rel_far", 4)):
    PRM[_name] = _at
    _at += _n
N_PRM = _at
IDENT, HALVES, ROT_A, ROT_B, CAUSAL, ADMIT = (P * i for i in range(6))
RESET = 6 * P
N_CON = RESET + S


def build(nc, xT_d, wb_d, ada_d, prm_d, con_d, rope_d, gup_d, rel_d, out_d):
    with ExitStack() as ctx:
        def sb(name, shape, dt=F32, scope=ctx):
            return scope.enter_context(nc.sbuf_tensor(name, shape, dt))

        def sem(name):
            return ctx.enter_context(nc.semaphore(name))

        x = sb("x", [P, KT, S])
        h_hi = sb("h_hi", [P, KT, S], F32R)
        h_lo = sb("h_lo", [P, KT, S], F32R)
        w_raw = sb("w_raw", [P, 2, 2048])
        w_hi = sb("w_hi", [P, 2, 2048], F32R)
        w_lo = sb("w_lo", [P, 2, 2048], F32R)
        con = sb("con", [P, N_CON])
        prm = sb("prm", [P, N_PRM])
        ones = sb("ones", [P, P])
        modT = sb("modT", [P, 48])
        gain2 = sb("gain2", [P, 4, KT])
        sq = sb("sq", [P, 2, 1024])
        rstd = sb("rstd", [P, S])
        cact = sb("cact", [P, KT])
        identr = sb("identr", [P, P], F32R)
        ps = ctx.enter_context(nc.psum_tensor("ps", [P, 8, S], F32))
        trow = sq[:].rearrange("p a (b s) -> p (a b) s", s=S)

        def pc(name, i=0, n=1):
            return prm[:, PRM[name] + i:PRM[name] + i + n]

        def mat(at):
            return con[:, at:at + P]

        def scoped(specs):
            with ExitStack() as scope:
                return {n: sb(n, s, d, scope) for n, s, d in specs}

        p_s = trow[:, 0:3]
        with ExitStack() as scope:
            at_ = {n: sb(n, s, d, scope) for n, s, d in [
                ("a_kh", [P, 2, S], F32R), ("a_kl", [P, 2, S], F32R), ("a_qh", [P, 8, S], F32R), ("a_ql", [P, 8, S], F32R),
                ("a_vh", [P, TT, 256], F32R), ("a_vl", [P, TT, 256], F32R),
                ("a_ph", [P, 2, S], F32R), ("a_pl", [P, 2, S], F32R),
                ("a_nmax", [P, 64], F32), ("a_sum", [P, 64], F32), ("a_rinv", [P, 64], F32)]}
            with ExitStack() as s2:
                at_.update({n: sb(n, s, F32, s2) for n, s in [
                    ("a_sq", [P, 2, 1024]), ("a_g", [P, 2, 1024]), ("a_rs", [P, 1024]), ("a_rot", [P, 1024]),
                    ("a_cos", [P, S]), ("a_sin", [P, S])]})
            with ExitStack() as s2:
                at_.update({n: sb(n, s, F32R, s2) for n, s in [("a_th", [P, 2, TT, S]), ("a_tl", [P, 2, TT, S])]})
        ml = scoped([
            ("m_hi", [P, 2, 2, S], F32R), ("m_lo", [P, 2, 2, S], F32R), ("m_r", [P, 2, 1024], F32),
            ("ada_w", [P, 2, 2048], F32), ("ada_t", [P, 2, 256], F32), ("ada_acc", [P, N_ADA, 256], F32)])
        with ExitStack() as scope:
            gl = {n: sb(n, s, F32, scope) for n, s in [
                ("g_q", [P, 2, GLA_H, S]), ("g_k", [P, 2, GLA_H, S]), ("g_v", [P, TT, D]), ("g_r", [P, KT, S]),
                ("g_a", [P, 2, TT, P]), ("g_dec", [P, 2, GLA_H, NCH]), ("g_tot", [P, GLA_H, NCH])]}
            with ExitStack() as s2:
                gl.update({n: sb(n, s, F32, s2) for n, s in [
                    ("g_x", [P, GLA_H, S]), ("g_t", [P, GLA_H, S]), ("g_z", [32, S]), ("g_up", [32, 2, S])]})
            with ExitStack() as s2:
                gl.update({n: sb(n, s, F32, s2) for n, s in [
                    ("g_s", [P, 2, NCH, GLA_DV]), ("g_kd", [P, 2, S]), ("g_kt", [P, 2, TT, P])]})
        with ExitStack() as scope:
            mx = {n: sb(n, s, d, scope) for n, s, d in [("x_yhi", [P, 6, S], F32R), ("x_ylo", [P, 6, S], F32R)]}
            with ExitStack() as s2:
                mx.update({n: sb(n, s, d, s2) for n, s, d in [
                    ("c_qh", [P, 2, S], F32R), ("c_ql", [P, 2, S], F32R), ("c_kh", [P, 1, S], F32R), ("c_kl", [P, 1, S], F32R),
                    ("c_vh", [P, TT, P], F32R), ("c_vl", [P, TT, P], F32R), ("c_wi", [P, TT, 4], F32),
                    ("x_ph", [P, 2, S], F32R), ("x_pl", [P, 2, S], F32R), ("x_th", [P, 2, S], F32R), ("x_tl", [P, 2, S], F32R),
                    ("x_m8", [P, 8], F32), ("x_f", [4, S], F32),
                    ("x_nmax", [P, 48], F32), ("x_sum", [P, 48], F32), ("x_rinv", [P, 48], F32)]})
                with ExitStack() as s3:
                    mx["x_mask"] = sb("x_mask", [P, 3, S], F32, s3)
                    mx["x_bias"] = sb("x_bias", [P, 4, 256], F32, s3)
                with ExitStack() as s3:
                    mx["x_neg"] = sb("x_neg", [P, 4, S], F32, s3)
                with ExitStack() as s3:
                    mx["pad"] = sb("x_pad", [P, 2560], F32, s3)
                    mx.update({n: sb(n, s, F32, s3) for n, s in [
                        ("x_qi", [P, 2, S]), ("x_ki", [P, 1, S]), ("x_rot", [P, 1024]), ("x_g", [P, 1024]),
                        ("x_cos", [P, S]), ("x_sin", [P, S])]})
                with ExitStack() as s3:
                    mx["pad2"] = sb("x_pad2", [P, 2560], F32, s3)
                    mx.update({n: sb(n, s, F32R, s3) for n, s in [
                        ("b_qh", [P, 2, S]), ("b_ql", [P, 2, S]), ("b_kh", [P, 2, S]), ("b_kl", [P, 2, S]),
                        ("b_vh", [P, TT, 256]), ("b_vl", [P, TT, 256])]})
            with ExitStack() as s2:
                mx.update({n: sb(n, s, d, s2) for n, s, d in [
                    ("x_mhi", [P, KT, S], F32R), ("x_mlo", [P, KT, S], F32R), ("x_gate", [P, 3, 1024], F32),
                    ("x_m", [P, 2, 1024], F32)]})
        ff = scoped([
            ("y", [P, KT, S], F32), ("f_hi", [P, 2, 2, S], F32R), ("f_lo", [P, 2, 2, S], F32R),
            ("f_c", [P, 2, 1024], F32), ("f_r", [P, 2, 1024], F32), ("f_prm", [P, 2, 8], F32)])
        y = ff["y"]

        x_in = [sem(f"x_in{c}") for c in range(4)]
        prm_in, con_in, rope_in, rope2_in, gup_in = map(sem, ("prm_in", "con_in", "rope_in", "rope2_in", "gup_in"))
        ones_set, ident_set = sem("ones_set"), sem("ident_set")
        w_in = [sem("w_in0"), sem("w_in1")]
        hi_done, split_done = sem("hi_done"), sem("split_done")
        block_done = sem("block_done")
        n_sq, n_ssq, n_std = sem("n_sq"), sem("n_ssq"), sem("n_std")
        n_row, n_hi, n_app = sem("n_row"), sem("n_hi"), sem("n_app")
        chain = sem("dve_chain")
        achain = sem("act_chain")
        out_st = sem("out_st")

        links = {"d": 0, "a": 0}

        def link(dve, ins):
            links["d"] += 1
            ins.then_inc(chain, 1)
            dve.wait_ge(chain, links["d"])

        def alink(act, ins):
            links["a"] += 1
            ins.then_inc(achain, 1)
            act.wait_ge(achain, links["a"])

        def split_hi(act, b, slot):
            act.wait_ge(w_in[slot], _land(b, slot))
            if not (isinstance(b, int) and b < 2):
                act.wait_ge(block_done, b - 1)
            act.activation(w_hi[:, slot], w_raw[:, slot], ACT.Copy).then_inc(hi_done, 1)

        def _land(b, slot):
            return 16 * (b // 2 + 1) if isinstance(b, int) else (b - slot) * 8 + 16

        def split_lo(dve, b, slot):
            dve.wait_ge(hi_done, b + 1)
            dve.tensor_tensor(w_lo[:, slot], w_raw[:, slot], w_hi[:, slot].bitcast(F32), ALU.subtract).then_inc(split_done, 1)

        def next_hi(act, b, slot):
            if not (isinstance(b, int) and b >= N_BLOCKS):
                split_hi(act, b, slot)

        def next_lo(dve, b, slot):
            if not (isinstance(b, int) and b >= N_BLOCKS):
                split_lo(dve, b, slot)

        def three(pe, out, w, h, start, stop):
            pe.matmul(out, w[0], h[0], start=start, stop=False)
            pe.matmul(out, w[0], h[1], start=False, stop=False)
            return pe.matmul(out, w[1], h[0], start=False, stop=stop)

        def wtile(slot, at):
            return w_hi[:, slot, at:at + P], w_lo[:, slot, at:at + P]

        def pe_block(pe, b, slot, hh, pair, rows=None, ntiles=2):
            pe.wait_ge(split_done, b + 1)
            for k in range(KT):
                if rows is not None:
                    pe.wait_ge(n_app, rows + k + 1)
                for n in range(ntiles):
                    last = three(pe, ps[:, 2 * pair + n, :], wtile(slot, k * 256 + n * P),
                                 (hh[0][:, k, :], hh[1][:, k, :]), k == 0, k == KT - 1)
            return last.then_inc(block_done, 1)

        def pe_token_block(pe, b, slot, pair, width=256, count=True):
            pe.wait_ge(split_done, b + 1)
            for t in range(TT):
                out = ps[:, 2 * pair + t // 2, (t % 2) * 256:(t % 2) * 256 + width]
                for k in range(KT):
                    rows = slice(t * P, (t + 1) * P)
                    w = slice(k * 256, k * 256 + width)
                    pe.matmul(out, h_hi[:, k, rows], w_hi[:, slot, w], start=k == 0, stop=False)
                    pe.matmul(out, h_lo[:, k, rows], w_hi[:, slot, w], start=False, stop=False)
                    last = pe.matmul(out, h_hi[:, k, rows], w_lo[:, slot, w], start=False, stop=k == KT - 1)
            return last.then_inc(block_done, 1) if count else last

        def pair_(i):
            return ps[:, 2 * i:2 * i + 2, :]

        HH = (h_hi, h_lo)

        def act_square(act, n, j, src):
            if j >= 2:
                act.wait_ge(n_ssq, 4 * n + j - 1)
            elif n > 0:
                act.wait_ge(n_app, 8 * n)
            act.activation(sq[:, j % 2].rearrange("p (a s) -> p a s", a=2), src[:, 2 * j:2 * j + 2, :], ACT.Square).then_inc(n_sq, 1)

        def pe_ssq(pe, n, j, bank):
            pe.wait_ge(n_sq, 4 * n + j + 1)
            for i in range(2):
                last = pe.matmul(ps[:, bank, :], ones[:], sq[:, j % 2, i * S:(i + 1) * S],
                                 start=(j == 0 and i == 0), stop=(j == 3 and i == 1))
            last.then_inc(n_ssq, 1)

        def act_std(act, n, bank):
            act.wait_ge(n_ssq, 4 * n + 4)
            alink(act, act.activation(rstd[:], ps[:, bank, :], ACT.Ln, bias=pc("eps"), scale=1.0 / D))
            act.activation(rstd[:], rstd[:], ACT.Exp, scale=-0.5).then_inc(n_std, 1)

        def dve_rstd(dve, n):
            dve.wait_ge(n_std, n + 1)

        def act_norm_h(act, n, m, bank, shift=None):
            act_std(act, n, bank)
            for k in range(KT):
                act.wait_ge(n_row, 8 * m + k + 1)
                if shift is None:
                    act.activation(h_hi[:, k, :], trow[:, k % 4], ACT.Copy).then_inc(n_hi, 1)
                else:
                    act.activation(h_hi[:, k, :], trow[:, k % 4], ACT.Identity, bias=shift[:, k:k + 1]).then_inc(n_hi, 1)

        def dve_norm_h(dve, n, m, gain, shift=None):
            dve_rstd(dve, n)
            for k in range(KT + 2):
                if k < KT:
                    if k >= 4:
                        dve.wait_ge(n_app, 8 * n + k - 3)
                    dve.scalar_tensor_tensor(out=trow[:, k % 4], in0=x[:, k, :], scalar=gain[:, k:k + 1], in1=rstd[:],
                                             op0=ALU.mult, op1=ALU.mult).then_inc(n_row, 1)
                if k >= 2:
                    i = k - 2
                    dve.wait_ge(n_hi, 8 * m + i + 1)
                    dve.wait_ge(n_row, 8 * m + i + 1)
                    hi = h_hi[:, i, :].bitcast(F32)
                    if shift is None:
                        dve.tensor_tensor(h_lo[:, i, :], trow[:, i % 4], hi, ALU.subtract).then_inc(n_app, 1)
                    else:
                        dve.scalar_tensor_tensor(out=h_lo[:, i, :], in0=trow[:, i % 4], scalar=shift[:, i:i + 1], in1=hi,
                                                 op0=ALU.add, op1=ALU.subtract).then_inc(n_app, 1)

        def dve_norm_x(dve, n, gain):
            dve_rstd(dve, n)
            for k in range(KT):
                dve.scalar_tensor_tensor(out=x[:, k, :], in0=x[:, k, :], scalar=gain[:, k:k + 1], in1=rstd[:],
                                         op0=ALU.mult, op1=ALU.mult).then_inc(n_app, 1)

        def dve_norm_add(dve, n, gain):
            dve_rstd(dve, n)
            for k in range(KT + 1):
                if k < KT:
                    if k >= 4:
                        dve.wait_ge(n_app, 8 * n + k - 3)
                    dve.scalar_tensor_tensor(out=trow[:, k % 4], in0=y[:, k, :], scalar=gain[:, k:k + 1], in1=rstd[:],
                                             op0=ALU.mult, op1=ALU.mult).then_inc(y_row, 1)
                if k >= 1:
                    i = k - 1
                    dve.wait_ge(y_row, 8 * ynorms[n] + i + 1)
                    dve.tensor_tensor(x[:, i, :], x[:, i, :], trow[:, i % 4], ALU.add).then_inc(n_app, 1)
        y_row = sem("y_row")
        ynorms = {6: 0, 8: 1}

        proj_ev = sem("proj_ev")

        def pe_proj(pe, i, b0, hh, n, bank, ready):
            for j in range(4):
                b = b0 + j
                if j == 0:
                    ready()
                if j >= 2:
                    pe.wait_ge(proj_ev, 4 * i + j - 1)
                pe_block(pe, b, b % 2, hh, j % 2)
                if j >= 1:
                    pe_ssq(pe, n, j - 1, bank)
            pe_ssq(pe, n, 3, bank)

        def act_proj(act, i, b0, n, src, bank):
            for j in range(4):
                b = b0 + j
                next_hi(act, b + 2, b % 2)
                act.wait_ge(proj_ev, 4 * i + j + 1)
                act_square(act, n, j, src)

        def dve_proj(dve, i, b0, dst, add):
            for j in range(4):
                b = b0 + j
                dve.wait_ge(block_done, b + 1)
                d = dst[:, 2 * j:2 * j + 2, :]
                if add:
                    dve.tensor_tensor(d, d, pair_(j % 2), ALU.add).then_inc(proj_ev, 1)
                else:
                    dve.tensor_copy(d, pair_(j % 2)).then_inc(proj_ev, 1)
                next_lo(dve, b + 2, b % 2)

        class Attention:

            def __init__(self, name, heads, causal, wide, nmax, total, rinv, ph, pl, th, tl):
                self.heads, self.causal, self.wide = heads, causal, wide
                self.nmax, self.total, self.rinv, self.ph, self.pl, self.th, self.tl = nmax, total, rinv, ph, pl, th, tl
                self.n = TT * heads
                self.S, self.top, self.exp, self.ri, self.hi, self.lo, self.T, self.th_c, self.tl_c, self.PV, self.oh, self.ol = (
                    sem(name + k) for k in ("_scores", "_max", "_exp", "_rinv", "_p_hi", "_p_lo", "_turned", "_t_hi", "_t_lo", "_pv", "_o_hi", "_o_lo"))

            def tiles(self, u):
                return u % TT + 1 if self.causal else TT

        def pe_attend(pe, A, u0, u1, operands, values_of, first):
            def scores(u):
                head, qt = divmod(u, TT)
                if u == u0:
                    first()
                if u >= 2:
                    pe.wait_ge(A.exp if not A.causal else A.top, u - 1)
                r = slice(64 * (head % 2), 64 * (head % 2) + 64)
                qh, ql, kh, kl = operands(head)
                q, nk = slice(qt * P, (qt + 1) * P), A.tiles(u) * P
                three(pe, ps[:, 6 + u % 2, 0:nk], (qh[r, q], ql[r, q]), (kh[r, 0:nk], kl[r, 0:nk]), True, True).then_inc(A.S, 1)

            def turn(u):
                pe.wait_ge(A.lo, u + 1)
                if u >= 2:
                    pe.wait_ge(A.th_c, u - 1)
                    pe.wait_ge(A.tl_c, u - 1)
                for part, bank in ((A.ph, 2), (A.pl, 4)):
                    for c in range(A.tiles(u)):
                        w = slice(c * P, (c + 1) * P)
                        last = pe.transpose(ps[:, bank + u % 2, w].bitcast(F32R), part[:, u % 2, w], identr[:])
                last.then_inc(A.T, 1)

            def values(u):
                head, c = divmod(u, TT)
                if c == 0 and head >= 2:
                    pe.wait_ge(A.ol, head - 1)
                if A.wide:
                    if c == 0:
                        pe.wait_ge(A.th_c, TT * head + TT)
                        pe.wait_ge(A.tl_c, TT * head + TT)
                    last = three(pe, ps[:, head % 2, :], values_of(head, c), (A.th[:, head % 2, c, :], A.tl[:, head % 2, c, :]),
                                 c == 0, c == TT - 1)
                else:
                    pe.wait_ge(A.th_c, u + 1)
                    pe.wait_ge(A.tl_c, u + 1)
                    for k in range(A.tiles(u)):
                        w = slice(k * P, (k + 1) * P)
                        last = three(pe, ps[:, head % 2, c * P:(c + 1) * P], values_of(head, k),
                                     (A.th[:, u % 2, w], A.tl[:, u % 2, w]), k == 0, k == A.tiles(u) - 1)
                last.then_inc(A.PV, 1)

            lag = 8 if A.wide else 5
            for s in range(u0, u1 + lag):
                if s < u1:
                    scores(s)
                if u0 <= s - 3 < u1:
                    turn(s - 3)
                if u0 <= s - lag < u1:
                    values(s - lag)

        def act_attend(act, A, u0, u1, source, dst):
            def probs(u):
                act.wait_ge(A.top, u + 1)
                if u >= 3 and not A.causal:
                    act.wait_ge(A.lo, u - 2)
                n = A.tiles(u) * P
                act.activation(p_s[:, u % 3, 0:n], source(u), ACT.Exp, bias=A.nmax[:, u:u + 1],
                               accum_out=A.total[:, u:u + 1]).then_inc(A.exp, 1)

            def hi(u):
                act.wait_ge(A.ri, u + 1)
                if u >= 2:
                    act.wait_ge(A.T, u - 1)
                n = A.tiles(u) * P
                act.activation(A.ph[:, u % 2, 0:n], p_s[:, u % 3, 0:n], ACT.Copy, scale=A.rinv[:, u:u + 1]).then_inc(A.hi, 1)

            def turned(u):
                act.wait_ge(A.T, u + 1)
                head, qt = divmod(u, TT)
                n = A.tiles(u)
                if A.wide:
                    if qt == 0 and head >= 2:
                        act.wait_ge(A.PV, TT * (head - 1))
                    act.activation(A.th[:, head % 2, :, qt * P:(qt + 1) * P], ps[:, 2 + u % 2, :].rearrange("p (c q) -> p c q", q=P).bitcast(F32), ACT.Copy).then_inc(A.th_c, 1)
                else:
                    if u >= 2:
                        act.wait_ge(A.PV, u - 1)
                    act.activation(A.th[:, u % 2, 0:n * P], ps[:, 2 + u % 2, 0:n * P], ACT.Copy).then_inc(A.th_c, 1)

            def out(head):
                r = slice(64 * (head % 2), 64 * (head % 2) + 64)
                act.wait_ge(A.PV, TT * (head + 1))
                act.activation(dst(head)[0][r], ps[r, head % 2, :], ACT.Copy).then_inc(A.oh, 1)

            lag = 9 if A.wide else 6
            for s in range(u0, u1 + lag):
                if s < u1:
                    probs(s)
                if u0 <= s - 1 < u1:
                    hi(s - 1)
                if u0 <= s - 4 < u1:
                    turned(s - 4)
                if u0 <= s - lag < u1 and (s - lag) % TT == TT - 1:
                    out((s - lag) // TT)

        def dve_attend(dve, A, u0, u1, top, dst):
            def rinv(u):
                dve.wait_ge(A.exp, u + 1)
                dve.reciprocal(A.rinv[:, u:u + 1], A.total[:, u:u + 1]).then_inc(A.ri, 1)

            def lo(u):
                dve.wait_ge(A.hi, u + 1)
                dve.wait_ge(A.ri, u + 1)
                if u >= 2:
                    dve.wait_ge(A.T, u - 1)
                n = A.tiles(u) * P
                dve.scalar_tensor_tensor(out=A.pl[:, u % 2, 0:n], in0=p_s[:, u % 3, 0:n], scalar=A.rinv[:, u:u + 1],
                                         in1=A.ph[:, u % 2, 0:n].bitcast(F32), op0=ALU.mult, op1=ALU.subtract).then_inc(A.lo, 1)

            def turned(u):
                dve.wait_ge(A.T, u + 1)
                head, qt = divmod(u, TT)
                n = A.tiles(u)
                if A.wide:
                    if qt == 0 and head >= 2:
                        dve.wait_ge(A.PV, TT * (head - 1))
                    dve.tensor_copy(A.tl[:, head % 2, :, qt * P:(qt + 1) * P], ps[:, 4 + u % 2, :].rearrange("p (c q) -> p c q", q=P)).then_inc(A.tl_c, 1)
                else:
                    if u >= 2:
                        dve.wait_ge(A.PV, u - 1)
                    dve.tensor_copy(A.tl[:, u % 2, 0:n * P], ps[:, 4 + u % 2, 0:n * P]).then_inc(A.tl_c, 1)

            def out(head):
                r = slice(64 * (head % 2), 64 * (head % 2) + 64)
                dve.wait_ge(A.oh, head + 1)
                hi, low = dst(head)
                dve.tensor_tensor(low[r], ps[r, head % 2, :], hi[r].bitcast(F32), ALU.subtract).then_inc(A.ol, 1)

            lag = 9 if A.wide else 6
            for s in range(u0, u1 + lag):
                if s < u1:
                    top(s)
                if u0 <= s - 1 < u1:
                    rinv(s - 1)
                if u0 <= s - 2 < u1:
                    lo(s - 2)
                if u0 <= s - 4 < u1:
                    turned(s - 4)
                if u0 <= s - lag < u1 and (s - lag) % TT == TT - 1:
                    out((s - lag) // TT)

        A1 = Attention("a", 16, False, True, at_["a_nmax"], at_["a_sum"], at_["a_rinv"], at_["a_ph"], at_["a_pl"], at_["a_th"], at_["a_tl"])
        a_v_hi, a_v_lo, a_raw, a_aux, a_rs, a_rows, a_qhi, a_ready = map(sem, (
            "a_v_hi", "a_v_lo", "a_raw", "a_aux", "a_rs_s", "a_rows", "a_qhi", "a_ready"))
        AUX = {0: 0, 2: 1, 3: 2, 4: 3, 5: 4}
        AUX_AFTER = {1: [0], 3: [2], 4: [3], 5: [4, 5]}
        two = lambda ap: ap.rearrange("p (a s) -> p a s", a=2)

        def attn_pe(pe):
            def aux(j):
                a = AUX[j]
                pe.wait_ge(a_raw, a + 1)
                if a >= 1:
                    pe.wait_ge(a_rows, a)
                for i in range(2):
                    pe.matmul(ps[:, 4 + i, :], mat(HALVES), at_["a_sq"][:, a % 2, i * S:(i + 1) * S], start=True, stop=True)
                for i in range(2):
                    last = pe.matmul(ps[:, 6 + i, :], mat(ROT_A), at_["a_g"][:, a % 2, i * S:(i + 1) * S], start=True, stop=True)
                last.then_inc(a_aux, 1)

            for j in range(N_QKV):
                b = B_QKV + j
                if j == 1:
                    pe_token_block(pe, b, b % 2, 1)
                else:
                    if j == 2:
                        pe.wait_ge(a_raw, 1)
                    if j == 3:
                        pe.wait_ge(a_v_lo, 1)
                    if j >= 4:
                        pe.wait_ge(a_raw, AUX[j - 2] + 1)
                    pe_block(pe, b, b % 2, HH, j % 2, rows=0 if j == 0 else None)
                for i in AUX_AFTER.get(j, []):
                    aux(i)
            pe_attend(pe, A1, 0, A1.n,
                      lambda h: (at_["a_qh"][:, h // 2], at_["a_ql"][:, h // 2], at_["a_kh"][:, h // 8], at_["a_kl"][:, h // 8]),
                      lambda h, c: (at_["a_vh"][:, c, P * (h // 8):P * (h // 8) + P], at_["a_vl"][:, c, P * (h // 8):P * (h // 8) + P]),
                      lambda: pe.wait_ge(a_ready, 5))

        def attn_act(act):
            def root(j):
                a = AUX[j]
                act.wait_ge(a_aux, a + 1)
                if a >= 1:
                    act.wait_ge(a_rows, a)
                alink(act, act.activation(two(at_["a_rs"][:]), ps[:, 4:6, :], ACT.Ln, bias=pc("eps"), scale=1.0 / HD))
                act.activation(at_["a_rs"][:], at_["a_rs"][:], ACT.Exp, scale=-0.5).then_inc(a_rs, 1)

            def q_hi(j):
                a = AUX[j]
                act.wait_ge(a_rows, a + 1)
                dst = at_["a_kh"][:] if a == 0 else at_["a_qh"][:, 2 * a - 2:2 * a]
                act.activation(dst, two(at_["a_rot"][:]), ACT.Copy).then_inc(a_qhi, 1)

            for j in range(N_QKV):
                b = B_QKV + j
                act.wait_ge(block_done, b + 1)
                if j == 1:
                    act.activation(at_["a_vh"][:], ps[:, 2:4, :].rearrange("p a (b n) -> p (a b) n", n=256), ACT.Copy).then_inc(a_v_hi, 1)
                else:
                    a = AUX[j]
                    if a >= 2:
                        act.wait_ge(a_aux, a - 1)
                        act.wait_ge(a_ready, a - 1)
                    act.activation(two(at_["a_sq"][:, a % 2]), pair_(j % 2), ACT.Square)
                    act.activation(two(at_["a_g"][:, a % 2]), pair_(j % 2), ACT.Copy,
                                   scale=pc("kg" if j == 0 else "qg")).then_inc(a_raw, 1)
                next_hi(act, b + 2, b % 2)
                for i in AUX_AFTER.get(j, []):
                    root(i)
                    q_hi(i)
            act_attend(act, A1, 0, A1.n, lambda u: ps[:, 6 + u % 2, :], lambda h: (h_hi[:, h // 2], h_lo[:, h // 2]))

        def attn_dve(dve):
            def rope(j):
                a = AUX[j]
                dve.wait_ge(a_aux, a + 1)
                if a == 0:
                    dve.wait_ge(rope_in, 32)
                if a >= 1:
                    dve.wait_ge(a_qhi, a)
                for i in range(2):
                    g = at_["a_g"][:, a % 2, i * S:(i + 1) * S]
                    dve.tensor_tensor(g, g, at_["a_cos"][:], ALU.mult)
                    ins = dve.tensor_tensor(at_["a_rot"][:, i * S:(i + 1) * S], ps[:, 6 + i, :], at_["a_sin"][:], ALU.mult)
                link(dve, ins)
                link(dve, dve.tensor_tensor(at_["a_rot"][:], at_["a_rot"][:], at_["a_g"][:, a % 2], ALU.add))
                dve.wait_ge(a_rs, a + 1)
                dve.scalar_tensor_tensor(out=at_["a_rot"][:], in0=at_["a_rot"][:], scalar=1.0 if j == 0 else HD ** -0.5,
                                         in1=at_["a_rs"][:], op0=ALU.mult, op1=ALU.mult).then_inc(a_rows, 1)
                dve.wait_ge(a_rows, a + 1)
                dve.wait_ge(a_qhi, a + 1)
                hi = at_["a_kh"][:] if a == 0 else at_["a_qh"][:, 2 * a - 2:2 * a]
                lo = at_["a_kl"][:] if a == 0 else at_["a_ql"][:, 2 * a - 2:2 * a]
                dve.tensor_tensor(lo, two(at_["a_rot"][:]), hi.bitcast(F32), ALU.subtract).then_inc(a_ready, 1)
                dve.wait_ge(a_ready, a + 1)

            for j in range(N_QKV):
                b = B_QKV + j
                if j == 1:
                    dve.wait_ge(a_v_hi, 1)
                    dve.tensor_tensor(at_["a_vl"][:], ps[:, 2:4, :].rearrange("p a (b n) -> p (a b) n", n=256),
                                      at_["a_vh"][:].bitcast(F32), ALU.subtract).then_inc(a_v_lo, 1)
                next_lo(dve, b + 2, b % 2)
                for i in AUX_AFTER.get(j, []):
                    rope(i)

            def top(u):
                dve.wait_ge(A1.S, u + 1)
                dve.tensor_reduce(A1.nmax[:, u:u + 1], ps[:, 6 + u % 2, :], AX, ALU.max, negate=True).then_inc(A1.top, 1)
            dve_attend(dve, A1, 0, A1.n, top, lambda h: (h_hi[:, h // 2], h_lo[:, h // 2]))

        m_relu, m_sq, m_hi, m_lo, m_out, m_add = map(sem, ("m_relu", "m_sq", "m_hi_s", "m_lo_s", "m_out", "m_add"))

        def mlp_in(pe, i, u, par, b, slot, rows=None):
            c = MLP_UNITS * i + u
            if not (isinstance(u, int) and u < 2):
                pe.wait_ge(m_relu, c - 1)
            pe_block(pe, b, slot, HH, par, rows=rows)

        def mlp_out(pe, i, u, par, b, slot, after=None):
            c = MLP_UNITS * i + u
            pe.wait_ge(m_lo, c + 1)
            pe.wait_ge(split_done, b + 1)
            for q in range(4):
                if not (isinstance(u, int) and u == 0 and q < 2):
                    pe.wait_ge(m_add, 4 * c + q - 1)
                for k in range(2):
                    for n in range(2):
                        last = three(pe, ps[:, 4 + 2 * (q % 2) + n, :], wtile(slot, k * 1024 + (2 * q + n) * P),
                                     (ml["m_hi"][:, par, k, :], ml["m_lo"][:, par, k, :]), k == 0, k == 1)
                last.then_inc(m_out if q < 3 else block_done, 1)
                if after is not None:
                    after(q)

        def mlp_pe(pe, i, b0, n, after_norm=None):
            mlp_in(pe, i, 0, 0, b0, b0 % 2, rows=8 * (n - 1))

            def turn(it):
                for d in (1, 2):
                    mlp_in(pe, i, it * 2 + d, d % 2, it * 4 + (b0 + 2 * d - 1), (b0 + 1) % 2)
                    mlp_out(pe, i, it * 2 + (d - 1), (d - 1) % 2, it * 4 + (b0 + 2 * d), b0 % 2)

            turn(0)
            with pe.Fori(1, (MLP_UNITS - 2) // 2) as it:
                turn(it)
            u = MLP_UNITS - 1
            mlp_in(pe, i, u, u % 2, b0 + 2 * u - 1, (b0 + 1) % 2)
            mlp_out(pe, i, u - 1, (u - 1) % 2, b0 + 2 * u, b0 % 2)

            def after(q):
                if q >= 2:
                    pe_ssq(pe, n, q - 2, 2 * 1)
            mlp_out(pe, i, u, u % 2, b0 + 2 * u + 1, (b0 + 1) % 2, after=after)
            pe_ssq(pe, n, 2, 2)
            pe_ssq(pe, n, 3, 2)

        def mlp_act_in(act, i, u, par, b, slot, more=True):
            c = MLP_UNITS * i + u
            act.wait_ge(block_done, b + 1)
            if not (isinstance(u, int) and i == 0 and u < 2):
                act.wait_ge(m_lo, c - 1)
            act.activation(ml["m_r"][:, par].rearrange("p (a s) -> p a s", a=2), pair_(par), ACT.Relu).then_inc(m_relu, 1)
            split_hi(act, b + 2, slot)
            act.wait_ge(m_sq, c + 1)
            act.activation(ml["m_hi"][:, par], ml["m_r"][:, par].rearrange("p (a s) -> p a s", a=2), ACT.Copy).then_inc(m_hi, 1)
            if more:
                split_hi(act, b + 3, 1 - slot)

        def mlp_act(act, i, b0, n):
            mlp_act_in(act, i, 0, 0, b0, b0 % 2, more=False)

            def turn(it):
                for d in (1, 2):
                    mlp_act_in(act, i, it * 2 + d, d % 2, it * 4 + (b0 + 2 * d - 1), (b0 + 1) % 2)

            turn(0)
            with act.Fori(1, (MLP_UNITS - 2) // 2) as it:
                turn(it)
            u = MLP_UNITS - 1
            mlp_act_in(act, i, u, u % 2, b0 + 2 * u - 1, (b0 + 1) % 2)
            for q in range(4):
                act.wait_ge(m_add, 4 * (MLP_UNITS * i + u) + q + 1)
                act_square(act, n, q, x)
            next_hi(act, b0 + 2 * u + 3, (b0 + 1) % 2)

        def mlp_dve_add(dve, i, u, q, b):
            c = MLP_UNITS * i + u
            if q < 3:
                dve.wait_ge(m_out, 3 * c + q + 1)
            else:
                dve.wait_ge(block_done, b + 1)
            if not (isinstance(u, int) and u == 0 and i == 0):
                dve.wait_ge(m_add, 4 * c + q - 3)
            xd = x[:, 2 * q:2 * q + 2, :]
            dve.tensor_tensor(xd, xd, pair_(2 + q % 2), ALU.add).then_inc(m_add, 1)

        def mlp_dve_in(dve, i, u, par, b, slot, prev=True):
            c = MLP_UNITS * i + u
            dve.wait_ge(m_relu, c + 1)
            r = ml["m_r"][:, par]
            dve.tensor_tensor(r, r, r, ALU.mult).then_inc(m_sq, 1)
            if prev:
                mlp_dve_add(dve, i, u - 1, 0, b + 1)
            split_lo(dve, b + 2, slot)
            if prev:
                mlp_dve_add(dve, i, u - 1, 1, b + 1)
            dve.wait_ge(m_hi, c + 1)
            dve.tensor_tensor(ml["m_lo"][:, par], r.rearrange("p (a s) -> p a s", a=2), ml["m_hi"][:, par].bitcast(F32),
                              ALU.subtract).then_inc(m_lo, 1)
            if prev:
                mlp_dve_add(dve, i, u - 1, 2, b + 1)
                mlp_dve_add(dve, i, u - 1, 3, b + 1)
                split_lo(dve, b + 3, 1 - slot)

        def mlp_dve(dve, i, b0):
            mlp_dve_in(dve, i, 0, 0, b0, b0 % 2, prev=False)

            def turn(it):
                for d in (1, 2):
                    mlp_dve_in(dve, i, it * 2 + d, d % 2, it * 4 + (b0 + 2 * d - 1), (b0 + 1) % 2)

            turn(0)
            with dve.Fori(1, (MLP_UNITS - 2) // 2) as it:
                turn(it)
            u = MLP_UNITS - 1
            mlp_dve_in(dve, i, u, u % 2, b0 + 2 * u - 1, (b0 + 1) % 2)
            for q in range(4):
                mlp_dve_add(dve, i, u, q, b0 + 2 * u + 1)
            next_lo(dve, b0 + 2 * u + 3, (b0 + 1) % 2)

        g_ev, g_ev2, g_log, g_xr, g_x2, g_b, g_e1, g_e2, g_qk = map(sem, (
            "g_ev", "g_ev2", "g_logits", "g_x_ready", "g_soft", "g_cum", "g_exp", "g_expn", "g_qk"))
        g_aT, g_ac, g_az, g_am, g_kd, g_kT, g_kc, g_ckv, g_st, g_O, g_sq, g_ss, g_rt, g_oh, g_ol, g_row = map(sem, (
            "g_aT", "g_a_copied", "g_a_zero", "g_a_masked", "g_kd_s", "g_kT", "g_kt_s", "g_ckv", "g_states", "g_O", "g_sq",
            "g_ss", "g_root", "g_o_hi", "g_o_lo", "g_row"))
        INV_TAU = 1.0 / 16.0
        chunks = lambda ap: ap.rearrange("p h (n c) -> p (h n) c", c=CH)

        def qk(t, d):
            return gl[t][:, 1 - d]

        def chunks_of(d):
            return list(range(NCH - 1)) if d == 0 else list(range(NCH - 1, 0, -1))

        def chunk_bank(d, n):
            return ps[:, 4 * (1 - d) + 2 * (n % 2) + n // 4, ((n // 2) % 2) * 256:((n // 2) % 2) * 256 + 256]

        def gla_pe(pe, b0, rows):
            def logits(d):
                if d == 0:
                    pe.wait_ge(gup_in, 16)
                    pe.wait_ge(g_ev, 1)
                else:
                    pe.wait_ge(g_xr, GLA_H)
                for h in range(GLA_H):
                    last = pe.matmul(ps[:, 4 + h, :], gl["g_up"][:, d, h * P:(h + 1) * P], gl["g_z"][:], start=True, stop=True)
                last.then_inc(g_log, 1)

            for j in range(N_GLA):
                b = b0 + j
                if j == 1:
                    pe.wait_ge(mod_set, 1)
                if j >= 2:
                    pe.wait_ge(g_ev, j - 1)
                if 5 <= j < 9:
                    pe_token_block(pe, b, b % 2, j % 2)
                else:
                    pe_block(pe, b, b % 2, HH, j % 2, rows=rows if j == 0 else None, ntiles=1 if j == 0 else 2)
                if j == 1:
                    logits(0)
                if j == 3:
                    logits(1)
            pe.wait_ge(g_ev, N_GLA)

            for h in range(GLA_H):
                for d in range(2):
                    e = 2 * h + d
                    pe.wait_ge(g_qk, 2)
                    if h >= 1:
                        pe.wait_ge(g_st, 2 * h)
                    for t in range(TT):
                        w = slice(t * P, (t + 1) * P)
                        last = pe.matmul(ps[:, 2 * d, w], qk("g_k", d)[:, h, w], qk("g_q", d)[:, h, w], start=True, stop=True)
                    last.then_inc(g_aT, 1)
                    pe.wait_ge(g_kd, e + 1)
                    for t in range(TT):
                        w = slice(t * P, (t + 1) * P)
                        last = pe.transpose(ps[:, 2 * d + 1, w], gl["g_kd"][:, d, w], mat(IDENT))
                    last.then_inc(g_kT, 1)
                for d in range(2):
                    e = 2 * h + d
                    pe.wait_ge(g_kc, e + 1)
                    if d == 0 and h >= 1:
                        pe.wait_ge(g_ol, 2 * h)
                    if d == 1:
                        pe.wait_ge(g_ac, e + 1)
                    for n in chunks_of(d):
                        r = slice(CH * (n % 2), CH * (n % 2) + CH)
                        last = pe.matmul(chunk_bank(d, n),
                                         gl["g_kt"][r, d, n // 2, :], gl["g_v"][r, n // 2, h * 256:h * 256 + 256], start=True, stop=True)
                    last.then_inc(g_ckv, 1)
                pe.wait_ge(g_am, 2 * (h + 1))
                pe.wait_ge(g_st, 2 * h + 2)
                for i in range(2):
                    vcol = slice(h * 256 + i * P, h * 256 + (i + 1) * P)
                    for t in range(TT):
                        todo = [(gl["g_v"][:, t, vcol], gl["g_a"][:, d, t, :], t * P, P) for d in range(2)]
                        for n in (2 * t, 2 * t + 1):
                            for d in range(2):
                                if n != (0 if d == 0 else NCH - 1):
                                    todo.append((gl["g_s"][:, d, n, i * P:(i + 1) * P], qk("g_q", d)[:, h, n * CH:(n + 1) * CH], n * CH, CH))
                        for z, (l, r, at, wd) in enumerate(todo):
                            last = pe.matmul(ps[:, 4 + i, at:at + wd], l, r, start=z == 0, stop=z == len(todo) - 1)
                last.then_inc(g_O, 1)
                pe.wait_ge(g_sq, h + 1)
                for i in range(2):
                    last = pe.matmul(ps[:, 6, :], ones[:], sq[:, 0, i * S:(i + 1) * S], start=i == 0, stop=i == 1)
                last.then_inc(g_ss, 1)

        def gla_act(act, b0):
            def gates(d):
                for h in range(GLA_H):
                    if h == 0:
                        act.wait_ge(g_log, d + 1)
                        if d == 1:
                            act.wait_ge(g_qk, 1)
                    act.activation(gl["g_x"][:, h, :], ps[:, 4 + h, :], ACT.Identity, bias=pc("gla_b", 4 * d + h)).then_inc(g_xr, 1)
                act.wait_ge(g_xr, GLA_H * (d + 1))
                t = gl["g_t"][:]
                alink(act, act.activation(t, gl["g_x"][:], ACT.Abs))
                alink(act, act.activation(t, t, ACT.Exp, scale=-1.0))
                act.activation(t, t, ACT.Ln, bias=1.0).then_inc(g_x2, 1)

            def exps(d):
                act.wait_ge(g_b, d + 1)
                act.activation(gl["g_dec"][:, d], gl["g_tot"][:], ACT.Exp, scale=INV_TAU)
                act.activation(gl["g_x"][:], gl["g_t"][:], ACT.Exp, scale=INV_TAU).then_inc(g_e1, 1)
                act.wait_ge(g_e1, d + 1)
                act.activation(gl["g_t"][:], gl["g_t"][:], ACT.Exp, scale=-INV_TAU).then_inc(g_e2, 1)

            for j in range(N_GLA):
                b = b0 + j
                act.wait_ge(block_done, b + 1)
                if j == 0:
                    act.activation(gl["g_z"][:], ps[0:32, 0, :], ACT.Copy).then_inc(g_ev, 1)
                elif j < 5:
                    t, i = ("g_q", 2 * (j - 1)) if j < 3 else ("g_k", 2 * (j - 3))
                    act.activation(gl[t][:, 0, i:i + 2, :], pair_(j % 2), ACT.Copy, scale=GLA_DK ** -0.5 if j < 3 else 1.0).then_inc(g_ev, 1)
                elif j < 9:
                    c = 256 * (j - 5)
                    act.activation(gl["g_v"][:, :, c:c + 256], pair_(j % 2).rearrange("p a (b n) -> p (a b) n", n=256), ACT.Copy).then_inc(g_ev, 1)
                else:
                    i = 2 * (j - 9)
                    act.activation(gl["g_r"][:, i:i + 2, :], pair_(j % 2), ACT.Silu).then_inc(g_ev, 1)
                next_hi(act, b + 2, b % 2)
                if j == 1:
                    gates(0)
                if j == 4:
                    exps(0)
                if j == 5:
                    gates(1)
                if j == 7:
                    exps(1)
            for h in range(GLA_H):
                for d in range(2):
                    act.wait_ge(g_kT, 2 * h + d + 1)
                    if h >= 1:
                        act.wait_ge(g_ckv, 2 * h)
                    act.activation(gl["g_kt"][:, d], ps[:, 2 * d + 1, :].rearrange("p (t k) -> p t k", t=TT), ACT.Copy).then_inc(g_kc, 1)
                act.wait_ge(g_O, h + 1)
                if h == 0:
                    act.wait_ge(n_app, 8 * 3)
                else:
                    act.wait_ge(g_ol, 2 * h)
                act.activation(two(sq[:, 0]), ps[:, 4:6, :], ACT.Square).then_inc(g_sq, 1)
                act.wait_ge(g_ss, h + 1)
                alink(act, act.activation(rstd[:], ps[:, 6, :], ACT.Ln, bias=pc("eps"), scale=1.0 / GLA_DV))
                act.activation(rstd[:], rstd[:], ACT.Exp, scale=-0.5).then_inc(g_rt, 1)
                for i in range(2):
                    act.wait_ge(g_row, 2 * h + i + 1)
                    act.activation(h_hi[:, 2 * h + i, :], gl["g_r"][:, 2 * h + i, :], ACT.Copy).then_inc(g_oh, 1)

        def gla_dve(dve, b0):
            def cumulate(d):
                dve.wait_ge(g_x2, d + 1)
                x_, t = gl["g_x"][:], gl["g_t"][:]
                link(dve, dve.scalar_tensor_tensor(out=x_, in0=x_, scalar=0.0, in1=t, op0=ALU.min, op1=ALU.subtract))
                for h in range(GLA_H):
                    ins = dve.tensor_tensor_scan(gl["g_t"][:, h, :], con[:, RESET:RESET + S], gl["g_x"][:, h, :], 0.0, ALU.mult, ALU.add)
                link(dve, ins)
                ends = gl["g_t"][:].rearrange("p h (n c) -> p h n c", c=CH)[:, :, :, CH - 1]
                if d == 1:
                    dve.wait_ge(g_e1, 1)
                ins = dve.tensor_copy(gl["g_tot"][:], ends)
                if d == 0:
                    ins.then_inc(g_b, 1)
                else:
                    link(dve, ins)
                    link(dve, dve.tensor_tensor(t, x_, t, ALU.subtract))
                    tot = gl["g_tot"][:].rearrange("p h n -> p (h n)").unsqueeze(2).to_broadcast([P, GLA_H * NCH, CH])
                    dve.tensor_tensor(chunks(gl["g_t"][:]), chunks(gl["g_t"][:]), tot, ALU.add).then_inc(g_b, 1)

            def scaled(d):
                dve.wait_ge(g_e2, d + 1)
                dve.tensor_tensor(qk("g_q", d), gl["g_q"][:, 0], gl["g_x"][:], ALU.mult)
                dve.tensor_tensor(qk("g_k", d), gl["g_k"][:, 0], gl["g_t"][:], ALU.mult).then_inc(g_qk, 1)

            for j in range(N_GLA):
                b = b0 + j
                next_lo(dve, b + 2, b % 2)
                if j == 1:
                    cumulate(0)
                if j == 4:
                    dve.wait_ge(g_ev, 5)
                    scaled(0)
                if j == 5:
                    cumulate(1)
                if j == 7:
                    dve.wait_ge(g_qk, 1)
                    scaled(1)
            dve.wait_ge(g_qk, 2)
            dve.memset(gl["g_a"][:], 0.0).then_inc(g_az, 1)
            dve.wait_ge(g_az, 1)
            for h in range(GLA_H):
                for d in range(2):
                    e = 2 * h + d
                    if h >= 1:
                        dve.wait_ge(g_kT, 2 * h)
                    dec = gl["g_dec"][:, d, h, :].unsqueeze(2).to_broadcast([P, NCH, CH])
                    dve.tensor_tensor(gl["g_kd"][:, d].rearrange("p (n c) -> p n c", c=CH),
                                      qk("g_k", d)[:, h, :].rearrange("p (n c) -> p n c", c=CH), dec, ALU.mult).then_inc(g_kd, 1)
                for d in range(2):
                    e = 2 * h + d
                    dve.wait_ge(g_aT, e + 1)
                    if h >= 1:
                        dve.wait_ge(g_O, h)
                        dve.wait_ge(g_am, 2 * h)
                    for r in (slice(0, CH), slice(CH, P)):
                        ins = dve.tensor_copy(gl["g_a"][r, d, :, r], ps[r, 2 * d, :].rearrange("p (t c) -> p t c", t=TT)[:, :, r])
                    ins.then_inc(g_ac, 1)
                for d in range(2):
                    e = 2 * h + d
                    dve.wait_ge(g_ckv, e + 1)
                    prev = None
                    for n in chunks_of(d):
                        to = n + 1 if d == 0 else n - 1
                        add = chunk_bank(d, n)
                        if prev is None:
                            ins = dve.tensor_copy(gl["g_s"][:, d, to, :], add)
                        else:
                            ins = dve.scalar_tensor_tensor(out=gl["g_s"][:, d, to, :], in0=gl["g_s"][:, d, prev, :],
                                                           scalar=gl["g_dec"][:, d, h, n:n + 1], in1=add, op0=ALU.mult, op1=ALU.add)
                        prev = to
                        if n == chunks_of(d)[-1]:
                            ins.then_inc(g_st, 1)
                        else:
                            link(dve, ins)
                dve.wait_ge(g_rt, h + 1)
                for i in range(2):
                    t = sq[:, 1, i * S:(i + 1) * S]
                    if h == 0 and i == 0:
                        dve.wait_ge(n_app, 24)
                    ins = dve.scalar_tensor_tensor(out=t, in0=ps[:, 4 + i, :], scalar=pc("out_g", i), in1=rstd[:], op0=ALU.mult, op1=ALU.mult)
                link(dve, ins)
                for i in range(2):
                    r = gl["g_r"][:, 2 * h + i, :]
                    dve.tensor_tensor(r, r, sq[:, 1, i * S:(i + 1) * S], ALU.mult).then_inc(g_row, 1)
                for i in range(2):
                    f = 2 * h + i
                    dve.wait_ge(g_oh, f + 1)
                    dve.wait_ge(g_row, f + 1)
                    dve.tensor_tensor(h_lo[:, f, :], gl["g_r"][:, f, :], h_hi[:, f, :].bitcast(F32), ALU.subtract).then_inc(g_ol, 1)

        def gla_pool(pool):
            for h in range(GLA_H):
                for d in range(2):
                    pool.wait_ge(g_ac, 2 * h + d + 1)
                    sign = 1 if d == 0 else -1
                    v = gl["g_a"][:, d]
                    pool.affine_select(out=v, in_=v, compare_op=ALU.is_ge, fill=0.0, base=0, pattern=[[0, TT], [sign, P]],
                                       channel_multiplier=-sign).then_inc(g_am, 1)

        ada_in, ada_row, ada_used, ada_sum, mod_set = [sem("ada_in0"), sem("ada_in1")], sem("ada_row"), sem("ada_used"), sem("ada_sum"), sem("mod_set")
        c_set, ada_acc_s = sem("c_set"), sem("ada_acc_s")

        def ada_pool(pool):
            pool.wait_ge(c_set, 1)
            for j in range(N_ADA):
                pool.wait_ge(ada_in[j % 2], 16 * (j // 2 + 1))
                for k in range(KT):
                    w = ml["ada_w"][:, j % 2, k * 256:(k + 1) * 256]
                    i = KT * j + k
                    if i >= 2:
                        pool.wait_ge(ada_acc_s, i - 1)
                    pool.tensor_scalar(ml["ada_t"][:, k % 2], w, cact[:, k:k + 1], None, ALU.mult).then_inc(ada_row, 1)
                    pool.wait_ge(ada_row, i + 1)
                    acc = ml["ada_acc"][:, j]
                    if k == 0:
                        ins = pool.tensor_copy(acc, ml["ada_t"][:, k % 2])
                    else:
                        pool.wait_ge(ada_acc_s, i)
                        ins = pool.tensor_tensor(acc, acc, ml["ada_t"][:, k % 2], ALU.add)
                    ins.then_inc(ada_acc_s, 1)

        def ada_pe(pe):
            pe.wait_ge(ada_acc_s, KT * N_ADA)
            for j in range(2 * N_ADA):
                last = pe.matmul(ps[:, 3, j:j + 1], ml["ada_acc"][:, j // 2, (j % 2) * P:(j % 2) * P + P], ones[:, 0:1], start=True, stop=True)
            last.then_inc(ada_sum, 1)

        def ada_dve(dve):
            dve.wait_ge(ada_sum, 1)
            link(dve, dve.tensor_tensor(modT[:], ps[:, 3, 0:48], pc("b_ada", 0, 48), ALU.add))
            for i, (at, one) in enumerate(((8, 1.0), (16, 0.0), (32, 1.0), (40, 0.0))):
                last = dve.scalar_tensor_tensor(out=gain2[:, i, :], in0=modT[:, at:at + 8], scalar=one, in1=pc("norm_g", 8 * i, 8),
                                                op0=ALU.add, op1=ALU.mult)
            last.then_inc(mod_set, 1)
            dve.wait_ge(mod_set, 1)

        X = Attention("x", 12, True, False, mx["x_nmax"], mx["x_sum"], mx["x_rinv"], mx["x_ph"], mx["x_pl"], mx["x_th"], mx["x_tl"])
        x_raw, x_aux, x_rot, x_chi, x_ready, x_hi, x_ev = map(sem, ("x_raw", "x_aux", "x_rot_s", "x_c_hi", "x_c_ready", "x_hi_ev", "x_ev"))
        i_S, i_relu, i_acc, f_raw, f_soft, f_row, f_pe, f_neg, bias_in = map(sem, (
            "i_scores", "i_relu", "i_acc", "f_raw", "f_soft", "f_row", "f_pe", "f_neg", "bias_in"))
        SCORES = [(qt, h) for qt in range(1, TT) for h in range(4)]
        CUM = trow[0:4, 3]

        def x_operands(head):
            t = (head % 4) // 2
            if head < 4:
                return mx["c_qh"][:, t], mx["c_ql"][:, t], mx["c_kh"][:, 0], mx["c_kl"][:, 0]
            return mx["b_qh"][:, t], mx["b_ql"][:, t], mx["b_kh"][:, t], mx["b_kl"][:, t]

        def x_values(head, c):
            if head < 4:
                return mx["c_vh"][:, c], mx["c_vl"][:, c]
            w = slice(P * ((head % 4) // 2), P * ((head % 4) // 2) + P)
            return mx["b_vh"][:, c, w], mx["b_vl"][:, c, w]

        def x_dst(head):
            t = (head % 4) // 2 + {0: 4, 1: 0, 2: 2}[head // 4]
            return mx["x_yhi"][:, t], mx["x_ylo"][:, t]

        def mix_pe(pe, b0):
            def rotate(a):
                pe.wait_ge(x_raw, a + 1)
                if a >= 1:
                    pe.wait_ge(x_rot, a)
                for i in range(2):
                    last = pe.matmul(ps[:, 4 + i, :], mat(ROT_B), mx["x_g"][:, i * S:(i + 1) * S], start=True, stop=True)
                last.then_inc(x_aux, 1)

            def blk(j):
                b = b0 + j
                if 2 <= j < 5:
                    pe.wait_ge(x_raw, j - 1)
                elif j >= 5:
                    pe.wait_ge(x_ev, j - 4)
                if j == 3:
                    pe_token_block(pe, b, b % 2, 1, width=136, count=False)
                    for k in range(KT):
                        last = three(pe, ps[:, 6, :], wtile(b % 2, k * 256 + P), (h_hi[:, k, :], h_lo[:, k, :]), k == 0, k == KT - 1)
                    last.then_inc(block_done, 1)
                elif j in (6, 9):
                    pe_token_block(pe, b, b % 2, j % 2)
                else:
                    pe_block(pe, b, b % 2, HH, j % 2, rows=40 if j == 0 else None)

            def negative(h):
                pe.wait_ge(f_row, h + 1)
                pe.matmul(ps[:, 4 + h, :], ones[0:4, :], mx["x_f"][:], start=True, stop=True).then_inc(f_pe, 1)

            blk(0)
            blk(1)
            rotate(0)
            blk(2)
            rotate(1)
            blk(3)
            rotate(2)
            pe.wait_ge(x_rot, 3)
            pe.wait_ge(f_raw, 1)
            for i, (qt, h) in enumerate(SCORES):
                if i >= 4:
                    pe.wait_ge(i_relu, i - 3)
                r = slice(64 * (h % 2), 64 * (h % 2) + 64)
                pe.matmul(ps[:, 4 + i % 4, 0:(qt + 1) * P], mx["x_qi"][r, h // 2, qt * P:(qt + 1) * P], mx["x_ki"][r, 0, 0:(qt + 1) * P],
                          start=True, stop=True).then_inc(i_S, 1)
            blk(4)
            blk(5)
            blk(6)
            pe.wait_ge(x_ev, 4)
            pe.wait_ge(i_relu, len(SCORES))
            pe_attend(pe, X, 0, 8 * TT, x_operands, x_values, lambda: pe.wait_ge(x_ready, 2))
            pe.wait_ge(X.ol, 8)
            blk(7)
            negative(0)
            negative(1)
            blk(8)
            negative(2)
            negative(3)
            blk(9)
            pe.wait_ge(x_ev, 7)
            pe.wait_ge(f_neg, 4)
            pe_attend(pe, X, 8 * TT, 12 * TT, x_operands, x_values, lambda: None)

        def mix_act(act, b0):
            def tokens(i, n0, n1):
                return pair_(i).rearrange("p a (b n) -> p (a b) n", n=256)[:, :, n0:n1]

            for j in range(N_MIX):
                b = b0 + j
                if j == 7:
                    act_attend(act, X, 0, 8 * TT, lambda u: p_s[:, u % 3, 0:X.tiles(u) * P], x_dst)
                act.wait_ge(block_done, b + 1)
                if j < 3:
                    if j >= 1:
                        act.wait_ge(x_rot, j)
                    act.activation(two(mx["x_g"][:]), pair_(j % 2), ACT.Copy).then_inc(x_raw, 1)
                elif j == 3:
                    act.activation(mx["c_vh"][:], tokens(1, 0, P), ACT.Copy)
                    act.activation(mx["c_wi"][:], tokens(1, 132, 136), ACT.Copy, scale=0.5).then_inc(x_hi, 1)
                    act.activation(mx["x_f"][:], ps[0:4, 6, :], ACT.Identity, bias=pc("b_forget")[0:4]).then_inc(f_raw, 1)
                    act.wait_ge(f_raw, 1)
                    alink(act, act.activation(CUM, mx["x_f"][:], ACT.Abs))
                    alink(act, act.activation(CUM, CUM, ACT.Exp, scale=-1.0))
                    act.activation(CUM, CUM, ACT.Ln, bias=1.0).then_inc(f_soft, 1)
                elif j in (6, 9):
                    act.activation(mx["b_vh"][:], tokens(j % 2, 0, 256), ACT.Copy).then_inc(x_hi, 1)
                else:
                    if j == 4:
                        act.wait_ge(x_ready, 2)
                    act.activation(mx["b_kh" if j in (4, 7) else "b_qh"][:], pair_(j % 2), ACT.Copy).then_inc(x_hi, 1)
                next_hi(act, b + 2, b % 2)
                if j in (1, 3):
                    a = 0 if j == 1 else 2
                    act.wait_ge(x_rot, a + 1)
                    act.activation(mx["c_kh"][:] if a == 0 else mx["c_qh"][:],
                                   two(mx["x_rot"][:])[:, 0:1 if a == 0 else 2, :], ACT.Copy).then_inc(x_chi, 1)
                if j == 3:
                    for i, (qt, h) in enumerate(SCORES):
                        act.wait_ge(i_S, i + 1)
                        if i >= 3:
                            act.wait_ge(i_acc, i - 2)
                        n = (qt + 1) * P
                        act.activation(trow[:, i % 3, 0:n], ps[:, 4 + i % 4, 0:n], ACT.Relu, scale=HD ** -0.5).then_inc(i_relu, 1)
                if j in (7, 8):
                    for h in ((0, 1) if j == 7 else (2, 3)):
                        act.wait_ge(f_pe, h + 1)
                        act.activation(mx["x_neg"][:, h, :], ps[:, 4 + h, :], ACT.Copy, scale=-1.0).then_inc(f_neg, 1)
            act_attend(act, X, 8 * TT, 12 * TT, lambda u: p_s[:, u % 3, 0:X.tiles(u) * P], x_dst)

        def mix_dve(dve, b0):
            def tokens(i, n0, n1):
                return pair_(i).rearrange("p a (b n) -> p (a b) n", n=256)[:, :, n0:n1]

            def rope(a):
                dve.wait_ge(x_aux, a + 1)
                if a == 0:
                    dve.wait_ge(rope2_in, 32)
                if a == 2:
                    dve.wait_ge(x_ready, 1)
                for i in range(2):
                    g = mx["x_g"][:, i * S:(i + 1) * S]
                    dve.tensor_tensor(g, g, mx["x_cos"][:], ALU.mult)
                    ins = dve.tensor_tensor(mx["x_rot"][:, i * S:(i + 1) * S], ps[:, 4 + i, :], mx["x_sin"][:], ALU.mult)
                link(dve, ins)
                dst = mx["x_qi"][:] if a == 1 else two(mx["x_rot"][:])
                dve.tensor_tensor(dst, two(mx["x_rot"][:]), two(mx["x_g"][:]), ALU.add).then_inc(x_rot, 1)
                dve.wait_ge(x_rot, a + 1)
                if a != 1:
                    if a == 0:
                        link(dve, dve.tensor_copy(mx["x_ki"][:, 0, :], mx["x_rot"][:, S:2 * S]))
                    dve.wait_ge(x_chi, 1 if a == 0 else 2)
                    hi, lo, n = (mx["c_kh"], mx["c_kl"], 1) if a == 0 else (mx["c_qh"], mx["c_ql"], 2)
                    dve.tensor_tensor(lo[:], two(mx["x_rot"][:])[:, 0:n, :], hi[:].bitcast(F32), ALU.subtract).then_inc(x_ready, 1)
                    dve.wait_ge(x_ready, 1 if a == 0 else 2)

            def index_scores():
                for i, (qt, h) in enumerate(SCORES):
                    n = (qt + 1) * P
                    sc = mx["x_mask"][:, qt - 1, 0:n]
                    w = mx["c_wi"][:, qt, h:h + 1]
                    dve.wait_ge(i_relu, i + 1)
                    if h == 0:
                        dve.tensor_scalar(sc, trow[:, i % 3, 0:n], w, None, ALU.mult).then_inc(i_acc, 1)
                    else:
                        dve.scalar_tensor_tensor(out=sc, in0=trow[:, i % 3, 0:n], scalar=w, in1=sc, op0=ALU.mult, op1=ALU.add).then_inc(i_acc, 1)
                    dve.wait_ge(i_acc, i + 1)
                    if h == 3:
                        link(dve, dve.tensor_tensor(sc[:, n - P:n], sc[:, n - P:n], mat(ADMIT), ALU.add))

            def top_k(qt):
                sc = mx["x_mask"][:, qt - 1, 0:(qt + 1) * P]
                for _ in range(TOPK // 8):
                    link(dve, dve.max(mx["x_m8"][:], sc))
                    link(dve, dve.match_replace(sc, mx["x_m8"][:], sc, TAKEN))
                link(dve, dve.tensor_scalar(sc, sc, TAKEN, NEG, ALU.not_equal, ALU.mult))

            def top(u):
                head, qt = divmod(u, TT)
                h, n = head % 4, X.tiles(u) * P
                s_, sc = ps[:, 6 + u % 2, 0:n], p_s[:, u % 3, 0:n]
                dve.wait_ge(X.S, u + 1)
                if u >= 3:
                    dve.wait_ge(X.lo, u - 2)
                scaled = lambda lo, hi, add: dve.scalar_tensor_tensor(out=sc[:, lo:hi], in0=s_[:, lo:hi], scalar=HD ** -0.5, in1=add,
                                                                      op0=ALU.mult, op1=ALU.add)
                if head < 4:
                    ins = scaled(0, n, mat(ADMIT) if qt == 0 else mx["x_mask"][:, qt - 1, 0:n])
                elif head < 8:
                    if qt == 0:
                        ins = scaled(0, n, mx["x_bias"][:, h, P:2 * P])
                    else:
                        ins = scaled(n - 2 * P, n, mx["x_bias"][:, h, :])
                        if n > 2 * P:
                            ins = dve.tensor_scalar(sc[:, 0:n - 2 * P], s_[:, 0:n - 2 * P], HD ** -0.5, pc("rel_far", h), ALU.mult, ALU.add)
                else:
                    link(dve, scaled(0, n, mx["x_neg"][:, h, 0:n]))
                    ins = dve.tensor_tensor(sc[:, n - P:n], sc[:, n - P:n], mat(CAUSAL), ALU.add)
                link(dve, ins)
                dve.tensor_reduce(X.nmax[:, u:u + 1], sc, AX, ALU.max, negate=True).then_inc(X.top, 1)

            for j in range(N_MIX):
                b = b0 + j
                if j == 7:
                    dve.wait_ge(bias_in, 16)
                    for h in range(4):
                        ins = dve.tensor_tensor(mx["x_bias"][:, h, P:2 * P], mx["x_bias"][:, h, P:2 * P], mat(ADMIT), ALU.add)
                    link(dve, ins)
                    dve_attend(dve, X, 0, 8 * TT, top, x_dst)
                if j < 3:
                    pass
                elif j == 3:
                    dve.wait_ge(x_hi, 1)
                    dve.tensor_tensor(mx["c_vl"][:], tokens(1, 0, P), mx["c_vh"][:].bitcast(F32), ALU.subtract).then_inc(x_ev, 1)
                else:
                    dve.wait_ge(x_hi, j - 2)
                    if j in (6, 9):
                        dve.tensor_tensor(mx["b_vl"][:], tokens(j % 2, 0, 256), mx["b_vh"][:].bitcast(F32), ALU.subtract).then_inc(x_ev, 1)
                    else:
                        k = "b_k" if j in (4, 7) else "b_q"
                        dve.tensor_tensor(mx[k + "l"][:], pair_(j % 2), mx[k + "h"][:].bitcast(F32), ALU.subtract).then_inc(x_ev, 1)
                if j in (1, 2, 3):
                    rope(j - 1)
                next_lo(dve, b + 2, b % 2)
                if j == 3:
                    dve.wait_ge(f_soft, 1)
                    f = mx["x_f"][:]
                    link(dve, dve.scalar_tensor_tensor(out=f, in0=f, scalar=0.0, in1=CUM, op0=ALU.min, op1=ALU.subtract))
                    for t in range(TT):
                        w = slice(t * P, (t + 1) * P)
                        link(dve, dve.tensor_tensor_scan(CUM[:, w], ones[0:4, :], f[:, w], 0.0 if t == 0 else CUM[:, t * P - 1:t * P], ALU.mult, ALU.add))
                    index_scores()
                if j in (4, 5, 6):
                    top_k(j - 3)
                if j in (7, 8):
                    for h in ((0, 1) if j == 7 else (2, 3)):
                        if h >= 1:
                            dve.wait_ge(f_pe, h)
                        dve.tensor_scalar(mx["x_f"][:], CUM, mat(IDENT)[0:4, h:h + 1], None, ALU.mult).then_inc(f_row, 1)
            dve_attend(dve, X, 8 * TT, 12 * TT, top, x_dst)

        t_sig, t_use, t_sum, t_hi, t_lo = map(sem, ("t_gate", "t_used", "t_merged", "t_hi", "t_lo"))

        def merge_pe(pe, b0):
            pe.wait_ge(X.ol, 12)
            for p in range(4):
                for br in range(3):
                    b, i = b0 + 4 * p + br, 6 * p + br
                    if i >= 2:
                        if br < 2:
                            pe.wait_ge(t_use, 3 * p - 1 + br)
                        else:
                            pe.wait_ge(t_sig, 3 * p + 1)
                    pe_block(pe, b, b % 2, HH, i % 2)
                b = b0 + 4 * p + 3
                pe.wait_ge(split_done, b + 1)
                for br in range(3):
                    i = 6 * p + 3 + br
                    if br < 2:
                        pe.wait_ge(t_sig, 3 * p + 2 + br)
                    else:
                        pe.wait_ge(t_use, 3 * p + 1)
                    for k in range(2):
                        for n in range(2):
                            last = three(pe, ps[:, 2 * (i % 2) + n, :], wtile(b % 2, (2 * br + k) * 256 + n * P),
                                         (mx["x_yhi"][:, 2 * br + k, :], mx["x_ylo"][:, 2 * br + k, :]), k == 0, k == 1)
                    last.then_inc(t_br if br < 2 else block_done, 1)
        t_br = sem("t_branch")

        def merge_act(act, b0):
            for p in range(4):
                for br in range(3):
                    b = b0 + 4 * p + br
                    act.wait_ge(block_done, b + 1)
                    if p >= 1:
                        act.wait_ge(t_sum, p)
                    for n in range(2):
                        ins = act.activation(mx["x_gate"][:, br, n * S:(n + 1) * S], ps[:, 2 * (br % 2) + n, :], ACT.Sigmoid,
                                             bias=pc("b_gate", 8 * br + 2 * p + n))
                    ins.then_inc(t_sig, 1)
                    next_hi(act, b + 2, b % 2)
                act.wait_ge(t_sum, p + 1)
                act.activation(mx["x_mhi"][:, 2 * p:2 * p + 2, :], two(mx["x_m"][:, p % 2]), ACT.Copy).then_inc(t_hi, 1)
                next_hi(act, b0 + 4 * p + 5, (b0 + 1) % 2)

        def merge_dve(dve, b0):
            for p in range(4):
                for br in range(3):
                    next_lo(dve, b0 + 4 * p + br + 2, (b0 + br) % 2)
                m = mx["x_m"][:, p % 2]
                for br in range(3):
                    if br < 2:
                        dve.wait_ge(t_br, 2 * p + br + 1)
                    else:
                        dve.wait_ge(block_done, b0 + 4 * p + 4)
                    dve.wait_ge(t_sig, 3 * p + br + 1)
                    if br == 0 and p >= 2:
                        dve.wait_ge(t_lo, p - 1)
                        dve.wait_ge(t_hi, p - 1)
                    g = mx["x_gate"][:, br]
                    out = m if br == 0 else g
                    dve.tensor_tensor(two(out), two(g), pair_((br + 1) % 2), ALU.mult).then_inc(t_use, 1)
                    dve.wait_ge(t_use, 3 * p + br + 1)
                    if br >= 1:
                        ins = dve.tensor_tensor(m, m, g, ALU.add)
                        if br == 1:
                            link(dve, ins)
                ins.then_inc(t_sum, 1)
                dve.wait_ge(t_hi, p + 1)
                dve.tensor_tensor(mx["x_mlo"][:, 2 * p:2 * p + 2, :], two(m), mx["x_mhi"][:, 2 * p:2 * p + 2, :].bitcast(F32),
                                  ALU.subtract).then_inc(t_lo, 1)
                next_lo(dve, b0 + 4 * p + 5, (b0 + 1) % 2)

        f_pr, f_ce, f_t1, f_conv, f_ge, f_gm, f_hs, f_ls, f_out, f_add, y_zero = map(sem, (
            "f_params", "f_current", "f_tap1", "f_conv", "f_gelu", "f_gated", "f_h_hi", "f_h_lo", "f_out", "f_added", "y_zero"))

        def ffn_up(pe, u, b, slot, rows=None):
            for which, pair in ((0, 0), (1, 1)):
                if not (isinstance(u, int) and u == 0):
                    pe.wait_ge((f_conv, f_gm)[which], u)
                pe_block(pe, b + which, (slot + which) % 2, HH, pair, rows=rows if which == 0 else None)

        def ffn_down(pe, u, b, slot, after=None):
            pe.wait_ge(f_ls, u + 1)
            pe.wait_ge(split_done, b + 1)
            for q in range(4):
                if not (isinstance(u, int) and u == 0 and q < 2):
                    pe.wait_ge(f_add, u * 4 + (q - 1))
                for k in range(2):
                    for n in range(2):
                        last = three(pe, ps[:, 4 + 2 * (q % 2) + n, :], wtile(slot, k * 1024 + (2 * q + n) * P),
                                     (ff["f_hi"][:, f_par(u), k, :], ff["f_lo"][:, f_par(u), k, :]), k == 0, k == 1)
                last.then_inc(f_out if q < 3 else block_done, 1)
                if after is not None:
                    after(q)

        par_now = [0]

        def f_par(u):
            return u % 2 if isinstance(u, int) else par_now[0]

        LOOPED = FFN_UNITS - 3

        def ffn_pe(pe, b0, n):
            ffn_up(pe, 0, b0, b0 % 2, rows=56)

            def unit(u, b, d):
                ffn_up(pe, u, b, (b0 + 3 * d - 1) % 2)
                par_now[0] = (d - 1) % 2
                ffn_down(pe, u - 1, b + 2, (b0 + 3 * d + 1) % 2)

            unit(1, b0 + 2, 1)
            with pe.Fori(0, LOOPED // 2) as it:
                for d in (2, 3):
                    unit(it * 2 + d, it * 6 + (b0 + 3 * d - 1), d)
            unit(FFN_UNITS - 1, b0 + 3 * FFN_UNITS - 4, FFN_UNITS - 1)
            ffn_down(pe, FFN_UNITS - 1, b0 + 3 * FFN_UNITS - 1, (b0 + 3 * FFN_UNITS - 1) % 2,
                     after=lambda q: pe_ssq(pe, n, q - 2, 2) if q >= 2 else None)
            pe_ssq(pe, n, 2, 2)
            pe_ssq(pe, n, 3, 2)

        def ffn_act(act, b0, n):
            def unit(u, b, d, first=False, last=False):
                slot = (b0 if first else b0 + 3 * d - 1) % 2
                p_ = d % 2
                act.wait_ge(block_done, b + 1)
                act.wait_ge(f_pr, u + 1)
                if not (isinstance(u, int) and u < 2):
                    act.wait_ge(f_gm, u - 1)
                for i in range(2):
                    ins = act.activation(ff["f_c"][:, p_, i * S:(i + 1) * S], ps[:, i, :], ACT.Identity,
                                         bias=ff["f_prm"][:, p_, 4 * i + 3:4 * i + 4], scale=ff["f_prm"][:, p_, 4 * i + 2:4 * i + 3])
                ins.then_inc(f_ce, 1)
                split_hi(act, b + 2, slot)
                act.wait_ge(f_conv, u + 1)
                act.activation(ff["f_c"][:, p_], ff["f_c"][:, p_], ACT.Gelu_apprx_tanh).then_inc(f_ge, 1)
                split_hi(act, b + 3, 1 - slot)
                act.wait_ge(f_gm, u + 1)
                act.activation(ff["f_hi"][:, p_], two(ff["f_r"][:, p_]), ACT.Copy).then_inc(f_hs, 1)
                if not first and not last:
                    split_hi(act, b + 4, slot)

            unit(0, b0, 0, first=True)
            unit(1, b0 + 2, 1)
            with act.Fori(0, LOOPED // 2) as it:
                for d in (2, 3):
                    unit(it * 2 + d, it * 6 + (b0 + 3 * d - 1), d)
            u = FFN_UNITS - 1
            unit(u, b0 + 3 * u - 1, u, last=True)
            for q in range(4):
                act.wait_ge(f_add, 4 * u + q + 1)
                act_square(act, n, q, y)

        def ffn_dve(dve, b0):
            def params(u, d):
                at = PRM["conv"]
                src = prm[:, at + 8 * u:at + 8 * u + 8] if isinstance(u, int) else prm[:, bass.ds(u * 8 + at, 8)]
                dve.tensor_scalar(ff["f_prm"][:, d % 2, :], src, 1.0, None, ALU.mult).then_inc(f_pr, 1)

            def add(u, q, b):
                if q < 3:
                    dve.wait_ge(f_out, u * 3 + (q + 1))
                else:
                    dve.wait_ge(block_done, b + 1)
                if not (isinstance(u, int) and u == 0):
                    dve.wait_ge(f_add, u * 4 + (q - 3))
                yd = y[:, 2 * q:2 * q + 2, :]
                dve.tensor_tensor(yd, yd, pair_(2 + q % 2), ALU.add).then_inc(f_add, 1)

            def unit(u, b, d, first=False, last=False):
                slot = (b0 if first else b0 + 3 * d - 1) % 2
                p_ = d % 2
                dve.wait_ge(f_ce, u + 1)
                for tap, shift, s_ in ((1, 1, f_t1), (0, 2, f_conv)):
                    for i in range(2):
                        c = ff["f_c"][:, p_, i * S + shift:(i + 1) * S]
                        ins = dve.scalar_tensor_tensor(out=c, in0=ps[:, i, 0:S - shift], scalar=ff["f_prm"][:, p_, 4 * i + tap:4 * i + tap + 1],
                                                       in1=c, op0=ALU.mult, op1=ALU.add)
                    ins.then_inc(s_, 1)
                    dve.wait_ge(s_, u + 1)
                if not last:
                    params(u + 1, d + 1)
                    dve.wait_ge(f_pr, u + 2)
                split_lo(dve, b + 2, slot)
                dve.wait_ge(block_done, b + 2)
                dve.wait_ge(f_ge, u + 1)
                if not (isinstance(u, int) and u < 2):
                    dve.wait_ge(f_ls, u - 1)
                dve.tensor_tensor(two(ff["f_r"][:, p_]), two(ff["f_c"][:, p_]), pair_(1), ALU.mult).then_inc(f_gm, 1)
                if not first:
                    add(u - 1, 0, b + 2)
                split_lo(dve, b + 3, 1 - slot)
                if not first:
                    add(u - 1, 1, b + 2)
                dve.wait_ge(f_hs, u + 1)
                dve.wait_ge(f_gm, u + 1)
                dve.tensor_tensor(ff["f_lo"][:, p_], two(ff["f_r"][:, p_]), ff["f_hi"][:, p_].bitcast(F32), ALU.subtract).then_inc(f_ls, 1)
                if not first:
                    add(u - 1, 2, b + 2)
                    add(u - 1, 3, b + 2)
                    if not last:
                        split_lo(dve, b + 4, slot)

            params(0, 0)
            dve.wait_ge(f_pr, 1)
            dve.memset(y[:], 0.0).then_inc(y_zero, 1)
            dve.wait_ge(y_zero, 1)
            unit(0, b0, 0, first=True)
            unit(1, b0 + 2, 1)
            with dve.Fori(0, LOOPED // 2) as it:
                for d in (2, 3):
                    unit(it * 2 + d, it * 6 + (b0 + 3 * d - 1), d)
            u = FFN_UNITS - 1
            unit(u, b0 + 3 * u - 1, u, last=True)
            for q in range(4):
                add(u, q, b0 + 3 * u + 2)

        def renorm_squares(act, n, src):
            for j in range(4):
                act.wait_ge(n_app, 8 * (n - 1) + 2 * j + 2)
                act_square(act, n, j, src)

        def pe_sums(pe, n, bank):
            for j in range(4):
                pe_ssq(pe, n, j, bank)

        env = dict(locals())
        block = ctx.enter_context(nc.Block())
        program(nc, block, env)


def program(nc, block, e):
    x, out_d = e["x"], e["out_d"]
    gain = lambda name, i: e["prm"][:, PRM[name] + 8 * i:PRM[name] + 8 * i + 8]
    shift = lambda i: e["modT"][:, 24 * i:24 * i + 8]

    @block.sync
    def _(sp):
        xt = e["xT_d"].rearrange("(k p) s -> p k s", p=P)
        sp.dma_start(e["prm"][:], e["prm_d"]).then_inc(e["prm_in"], 16)
        for c in range(4):
            sp.dma_start(x[:, 2 * c:2 * c + 2, :], xt[:, 2 * c:2 * c + 2, :]).then_inc(e["x_in"][c], 16)
        for b in range(2):
            sp.dma_start(e["w_raw"][:, b], e["wb_d"][b]).then_inc(e["w_in"][b], 16)
        sp.dma_start(e["con"][:], e["con_d"]).then_inc(e["con_in"], 16)
        sp.dma_start(e["at_"]["a_cos"][:], e["rope_d"][0]).then_inc(e["rope_in"], 16)
        sp.dma_start(e["at_"]["a_sin"][:], e["rope_d"][1]).then_inc(e["rope_in"], 16)

        def load(b, slot):
            sp.wait_ge(e["split_done"], b - 1)
            sp.dma_start(e["w_raw"][:, slot], e["wb_d"][b]).then_inc(e["w_in"][slot], 16)

        def loads(b0, b1):
            with sp.Fori(0, (b1 - b0) // 2) as it:
                load(it * 2 + b0, b0 % 2)
                load(it * 2 + (b0 + 1), (b0 + 1) % 2)
            if (b1 - b0) % 2:
                load(b1 - 1, (b1 - 1) % 2)
        loads(2, B_MLP0 + 2)
        sp.wait_ge(e["A1"].ol, 16)
        def load_ada(j, slot):
            sp.dma_start(e["ml"]["ada_w"][:, slot], e["ada_d"][j]).then_inc(e["ada_in"][slot], 16)

        for d in range(2):
            load(B_MLP0 + 2 + d, (B_MLP0 + d) % 2)
            load_ada(d, d)
        with sp.Fori(0, N_ADA // 2 - 1) as it:
            for d in range(2):
                load(it * 2 + (B_MLP0 + 4 + d), (B_MLP0 + d) % 2)
                sp.wait_ge(e["ada_acc_s"], it * (2 * KT) + KT * (d + 1))
                load_ada(it * 2 + (2 + d), d)
        loads(B_MLP0 + 2 + N_ADA, B_GLA + 2)
        sp.wait_ge(e["m_add"], 4 * MLP_UNITS)
        sp.wait_ge(e["ada_sum"], 1)
        sp.dma_start(e["gl"]["g_up"][:], e["gup_d"]).then_inc(e["gup_in"], 16)
        loads(B_GLA + 2, B_MLP1 + 2)
        loads(B_MLP1 + 2, B_MIX + 2)
        sp.wait_ge(e["n_app"], 40)
        sp.dma_start(e["mx"]["x_cos"][:], e["rope_d"][2]).then_inc(e["rope2_in"], 16)
        sp.dma_start(e["mx"]["x_sin"][:], e["rope_d"][3]).then_inc(e["rope2_in"], 16)
        sp.dma_start(e["mx"]["x_bias"][:], e["rel_d"]).then_inc(e["bias_in"], 16)
        loads(B_MIX + 2, B_FFN + 2)
        loads(B_FFN + 2, N_BLOCKS)
        od = out_d.rearrange("(k p) s -> p k s", p=P)
        for j in range(4):
            sp.wait_ge(e["n_app"], 8 * 8 + 2 * j + 2)
            sp.dma_start(od[:, 2 * j:2 * j + 2, :], x[:, 2 * j:2 * j + 2, :]).then_inc(e["out_st"], 16)
        sp.wait_ge(e["out_st"], 64)

    @block.gpsimd
    def _(pool):
        pool.memset(e["ones"][:], 1.0).then_inc(e["ones_set"], 1)
        e["ada_pool"](pool)
        e["gla_pool"](pool)

    @block.scalar
    def _(act):
        act.wait_ge(e["prm_in"], 16)
        act.activation(e["cact"][:], e["pc"]("c", 0, 8), ACT.Silu).then_inc(e["c_set"], 1)
        act.preload_act_table_set("natural_log_exp_and_others")
        for j in range(4):
            act.wait_ge(e["x_in"][j], 16)
            e["act_square"](act, 0, j, x)
        e["split_hi"](act, 0, 0)
        e["act_norm_h"](act, 0, 0, 2)
        e["split_hi"](act, 1, 1)
        e["attn_act"](act)
        e["act_proj"](act, 0, B_WO0, 1, x, 6)
        e["act_norm_h"](act, 1, 1, 6)
        e["mlp_act"](act, 0, B_MLP0, 2)
        act.preload_act_table_set("natural_log_exp_and_others")
        e["act_norm_h"](act, 2, 2, 2)
        e["gla_act"](act, B_GLA)
        e["act_proj"](act, 1, B_WO1, 3, x, 6)
        e["act_norm_h"](act, 3, 3, 6)
        e["mlp_act"](act, 1, B_MLP1, 4)
        act.preload_act_table_set("natural_log_exp_and_others")
        e["act_std"](act, 4, 2)
        e["renorm_squares"](act, 5, x)
        e["act_norm_h"](act, 5, 4, 2, shift(0))
        e["mix_act"](act, B_MIX)
        e["merge_act"](act, B_GATE)
        e["act_proj"](act, 2, B_WOUT, 6, e["y"], 6)
        act.preload_act_table_set("natural_log_exp_and_others")
        e["act_std"](act, 6, 6)
        e["renorm_squares"](act, 7, x)
        e["act_norm_h"](act, 7, 5, 2, shift(1))
        e["ffn_act"](act, B_FFN, 8)
        e["act_std"](act, 8, 2)

    @block.vector
    def _(dve):
        e["split_lo"](dve, 0, 0)
        for j in range(4):
            dve.wait_ge(e["x_in"][j], 16)
        e["dve_norm_h"](dve, 0, 0, gain("norm_mix", 0))
        e["split_lo"](dve, 1, 1)
        dve.wait_ge(e["con_in"], 16)
        dve.tensor_copy(e["identr"][:], e["mat"](IDENT)).then_inc(e["ident_set"], 1)
        e["attn_dve"](dve)
        e["dve_proj"](dve, 0, B_WO0, x, True)
        e["dve_norm_h"](dve, 1, 1, gain("norm_mlp", 0))
        e["mlp_dve"](dve, 0, B_MLP0)
        e["dve_norm_h"](dve, 2, 2, gain("norm_mix", 1))
        e["ada_dve"](dve)
        e["gla_dve"](dve, B_GLA)
        e["dve_proj"](dve, 1, B_WO1, x, True)
        e["dve_norm_h"](dve, 3, 3, gain("norm_mlp", 1))
        e["mlp_dve"](dve, 1, B_MLP1)
        e["dve_norm_x"](dve, 4, gain("final", 0))
        e["dve_norm_h"](dve, 5, 4, e["gain2"][:, 0], shift(0))
        e["mix_dve"](dve, B_MIX)
        e["merge_dve"](dve, B_GATE)
        e["dve_proj"](dve, 2, B_WOUT, e["y"], False)
        e["dve_norm_add"](dve, 6, e["gain2"][:, 1])
        e["dve_norm_h"](dve, 7, 5, e["gain2"][:, 2], shift(1))
        e["ffn_dve"](dve, B_FFN)
        e["dve_norm_add"](dve, 8, e["gain2"][:, 3])

    @block.tensor
    def _(pe):
        pe.wait_ge(e["ones_set"], 1)
        e["pe_sums"](pe, 0, 2)
        pe.wait_ge(e["con_in"], 16)
        pe.wait_ge(e["ident_set"], 1)
        e["attn_pe"](pe)
        e["pe_proj"](pe, 0, B_WO0, e["HH"], 1, 6, lambda: pe.wait_ge(e["A1"].ol, 16))
        e["mlp_pe"](pe, 0, B_MLP0, 2)
        e["ada_pe"](pe)
        e["gla_pe"](pe, B_GLA, 16)
        e["pe_proj"](pe, 1, B_WO1, e["HH"], 3, 6, lambda: pe.wait_ge(e["g_ol"], 8))
        e["mlp_pe"](pe, 1, B_MLP1, 4)
        e["pe_sums"](pe, 5, 2)
        e["mix_pe"](pe, B_MIX)
        e["merge_pe"](pe, B_GATE)
        e["pe_proj"](pe, 2, B_WOUT, (e["mx"]["x_mhi"], e["mx"]["x_mlo"]), 6, 6, lambda: pe.wait_ge(e["t_lo"], 4))
        e["pe_sums"](pe, 7, 2)
        e["ffn_pe"](pe, B_FFN, 8)


def pack_block(w):
    return w.reshape(KT, P, 256).transpose(1, 0, 2).reshape(P, 2048)


def pack_wide(w):
    return w.reshape(2, P, 1024).transpose(1, 0, 2).reshape(P, 2048)


def columns(v):
    return v.reshape(-1, P).T


def zeros(*shape):
    return np.zeros(shape, np.float32)


def weight_blocks(i):
    out = []
    cols = lambda w, order=None: [pack_block(w[:, 256 * j:256 * j + 256]) for j in range(w.shape[1] // 256)]
    w = i["attn_w_qkv"][0]
    heads = [8 * (t // 4) + 4 * par + t % 4 for t in range(8) for par in range(2)]
    wq = np.concatenate([w[:, 64 * h:64 * h + 64] for h in heads], 1)
    out += [pack_block(w[:, 1024:1280]), pack_block(w[:, 1280:1536])] + cols(wq)
    out += cols(i["attn_w_o"][0].reshape(16, HD, D)[heads].reshape(D, D))

    def mlp(w1, w2):
        a = cols(w1)
        b = [pack_wide(w2[256 * u:256 * u + 256]) for u in range(MLP_UNITS)]
        seq = [a[0]]
        for u in range(1, MLP_UNITS):
            seq += [a[u], b[u - 1]]
        return seq + [b[-1]]

    out += mlp(i["mlp_w_in"][0], i["mlp_w_out"][0])
    w = i["gla_w_in"][0]
    z = np.concatenate([w[:, 3072:3104], zeros(D, 224)], 1)
    out += [pack_block(z)] + cols(w[:, 0:1024]) + cols(w[:, 1024:2048]) + cols(w[:, 2048:3072])
    out += cols(i["gla_w_o"][0])
    out += mlp(i["mlp_w_in"][1], i["mlp_w_out"][1])
    w = i["w_in_2"][0]
    c = lambda a, n=256: w[:, a:a + n]
    small = np.concatenate([c(1860, 64), c(1860, 64), c(1536, 4), c(2244, 4), zeros(D, 120)], 1)
    dup = np.concatenate([c(1796, 64)] * 2 + [c(2180, 64)] * 2, 1)
    out += [pack_block(v) for v in (dup, c(1924), c(1540), small, c(256), c(0), c(512), c(1024), c(768), c(1280))]
    for p in range(4):
        for br in range(3):
            out.append(pack_block(c(2248 + 1024 * br + 256 * p)))
        wbr = np.concatenate([i["w_branch_2"][0, br][:, 256 * p:256 * p + 256] for br in range(3)] + [zeros(256, 256)], 0)
        out.append(pack_block(wbr))
    out += cols(i["w_out_2"][0])
    up = i["w_up_2"][0]
    a, g = cols(up[:, :D_FF2]), cols(up[:, D_FF2:])
    dn = [pack_wide(i["w_down_2"][0][256 * u:256 * u + 256]) for u in range(FFN_UNITS)]
    out += [a[0], g[0]]
    for u in range(1, FFN_UNITS):
        out += [a[u], g[u], dn[u - 1]]
    out.append(dn[-1])
    return np.stack(out)


def small_parameters(i):
    halves = lambda v: np.concatenate([v, v])[:, None]
    pad = lambda v: np.concatenate([v, zeros(P - len(v))])[:, None]
    conv = np.concatenate([i["conv_w_2"][0], i["conv_b_2"]], 0)
    conv = conv.reshape(4, FFN_UNITS, 2, P).transpose(3, 1, 2, 0).reshape(P, -1)
    parts = [columns(i["norm_mix"].reshape(-1)), columns(i["norm_mlp"].reshape(-1)), columns(i["final_norm"]),
             halves(i["attn_q_norm"][0]), halves(i["attn_k_norm"][0]), columns(i["gla_b_gate"].reshape(-1)),
             columns(i["gla_out_norm"].reshape(-1)), columns(i["b_ada_2"].reshape(-1)), columns(i["norm_g_2"].reshape(-1)),
             columns(i["b_gate_2"].reshape(-1)), pad(i["b_forget_2"][0]), conv, columns(i["c_2"].reshape(-1)),
             np.full((P, 1), EPS, np.float32), np.tile(i["rel_table_2"][0, :, -1][None], (P, 1))]
    return np.ascontiguousarray(np.concatenate(parts, 1))


def constants():
    con = zeros(P, N_CON)
    r = np.arange(P)
    con[:, IDENT:IDENT + P] = np.eye(P)
    con[:, HALVES:HALVES + P] = (r[:, None] // 64 == r[None] // 64)
    for at, half in ((ROT_A, 16), (ROT_B, 32)):
        for m in range(P):
            if m % (2 * half) < half:
                con[m + half, at + m] = -1.0
            else:
                con[m - half, at + m] = 1.0
    con[:, CAUSAL:CAUSAL + P] = np.where(r[None] <= r[:, None], 0.0, NEG)
    con[:, ADMIT:ADMIT + P] = np.where(r[None] // CH <= r[:, None] // CH, 0.0, NEG)
    con[:, RESET:RESET + S] = (np.arange(S) % CH != 0)
    return con


def rope_tables():
    f = np.float32
    theta = f(10000.0)
    t, d = np.arange(S), np.arange(P) % 64
    inv = theta ** (-np.arange(0, 32, 2, dtype=f) / f(32))
    pos = np.where((d < 32)[:, None], (t // 64)[None], (t % 64)[None]).astype(f)
    ang = pos * inv[d % 16][:, None]
    inv2 = theta ** (-np.arange(0, 64, 2, dtype=f) / f(64))
    ang2 = t.astype(f)[None] * inv2[d % 32][:, None]
    return np.stack([np.cos(ang), np.sin(ang), np.cos(ang2), np.sin(ang2)]).astype(f)


def kernel(**inputs):
    import concourse.bacc as _bacc
    from concourse.bass_utils import run_bass_kernel_spmd as _launch

    i = {k: np.asarray(v) for k, v in inputs.items()}
    up = zeros(32, 2, S)
    up[0:16, 0] = i["gla_w_gate_up"][0, 0]
    up[16:32, 1] = i["gla_w_gate_up"][0, 1]
    rel = i["rel_table_2"][0]
    rel_rows = np.concatenate([np.repeat(rel[:, 256:], 127, 1), rel[:, 1:][:, ::-1]], 1)
    rel_tile = np.lib.stride_tricks.sliding_window_view(rel_rows, 2 * P, 1)[:, ::-1].transpose(1, 0, 2)
    ada = i["w_ada_2"][0]
    arrays = {
        "xT": np.ascontiguousarray(i["x"][0].T),
        "wb": weight_blocks(i),
        "ada": np.stack([pack_block(ada[:, 256 * j:256 * j + 256]) for j in range(N_ADA)]),
        "prm": small_parameters(i), "con": constants(), "rope": rope_tables(), "gup": up,
        "rel": np.ascontiguousarray(rel_tile),
    }
    nc = _bacc.Bacc("TRN2", target_bir_lowering=False, num_devices=1)
    args = [nc.dram_tensor("in_" + k, v.shape, mybir.dt.from_np(v.dtype), kind="ExternalInput").ap() for k, v in arrays.items()]
    out = nc.dram_tensor("out_T", (D, S), F32, kind="ExternalOutput").ap()
    build(nc, *args, out)
    r = _launch(nc, [{"in_" + k: v for k, v in arrays.items()}], core_ids=[0])
    return np.ascontiguousarray(r.results[0]["out_T"].T)[None]
```

```python
from contextlib import ExitStack

import numpy as np

import concourse.bass as bass
import concourse.mybir as mybir

F32 = mybir.dt.float32
F32R = mybir.dt.float32r
ALU = mybir.AluOpType
ACT = mybir.ActivationFunctionType
AX = mybir.AxisListType.X

P = 128
S = 512
D = 1024
KT = D // P
TT = S // P
EPS = 1e-6
NEG = -1e30
TAKEN = -3e38

HD = 64
D_FF = 4096
MLP_UNITS = D_FF // 256
GLA_H = 4
GLA_DK = 128
GLA_DV = 256
CH = 64
NCH = S // CH
TOPK = 128
D_FF2 = 2816
FFN_UNITS = D_FF2 // 256
TAPS = 3

N_QKV, N_PROJ, N_MLP, N_GLA, N_MIX, N_GATE = 6, 4, 2 * MLP_UNITS, 13, 10, 16
N_FFN = 3 * FFN_UNITS
B_QKV = 0
B_WO0 = B_QKV + N_QKV
B_MLP0 = B_WO0 + N_PROJ
B_GLA = B_MLP0 + N_MLP
B_WO1 = B_GLA + N_GLA
B_MLP1 = B_WO1 + N_PROJ
B_MIX = B_MLP1 + N_MLP
B_GATE = B_MIX + N_MIX
B_WOUT = B_GATE + N_GATE
B_FFN = B_WOUT + N_PROJ
N_BLOCKS = B_FFN + N_FFN
N_ADA = 6 * D // 256
HALF_ADA = N_ADA // 2

PRM = {}
_at = 0
for _name, _n in (("norm_mix", 16), ("norm_mlp", 16), ("final", 8), ("qg", 1), ("kg", 1), ("gla_b", 8), ("out_g", 2),
                  ("b_ada", 48), ("norm_g", 32), ("b_gate", 24), ("b_forget", 1), ("conv", 4 * 2 * FFN_UNITS), ("c", 8),
                  ("eps", 1), ("rel_far", 4)):
    PRM[_name] = _at
    _at += _n
N_PRM = _at
IDENT, HALVES, ROT_A, ROT_B, CAUSAL, ADMIT = (P * i for i in range(6))
RESET = 6 * P
N_CON = RESET + S


def build(nc, xT_d, wb_d, ada_d, prm_d, con_d, rope_d, gup_d, rel_d, sel_d, out_d):
    with ExitStack() as ctx:
        def sb(name, shape, dt=F32, scope=ctx):
            return scope.enter_context(nc.sbuf_tensor(name, shape, dt))

        def sem(name):
            return ctx.enter_context(nc.semaphore(name))

        x = sb("x", [P, KT, S])
        h_hi = sb("h_hi", [P, KT, S], F32R)
        h_lo = sb("h_lo", [P, KT, S], F32R)
        w_raw = sb("w_raw", [P, 2, 2048])
        w_hi = sb("w_hi", [P, 2, 2048], F32R)
        w_lo = sb("w_lo", [P, 2, 2048], F32R)
        con = sb("con", [P, N_CON])
        prm = sb("prm", [P, N_PRM])
        ones = sb("ones", [P, P])
        modT = sb("modT", [P, 48])
        gain2 = sb("gain2", [P, 4, KT])
        sq = sb("sq", [P, 2, 1024])
        rstd = sb("rstd", [P, S])
        cact = sb("cact", [P, KT])
        identr = sb("identr", [P, P], F32R)
        ps = ctx.enter_context(nc.psum_tensor("ps", [P, 8, S], F32))
        trow = sq[:].rearrange("p a (b s) -> p (a b) s", s=S)

        def pc(name, i=0, n=1):
            return prm[:, PRM[name] + i:PRM[name] + i + n]

        def mat(at):
            return con[:, at:at + P]

        def scoped(specs):
            with ExitStack() as scope:
                return {n: sb(n, s, d, scope) for n, s, d in specs}

        p_s = trow[:, 0:3]
        with ExitStack() as scope:
            at_ = {n: sb(n, s, d, scope) for n, s, d in [
                ("a_kh", [P, 2, S], F32R), ("a_kl", [P, 2, S], F32R), ("a_qh", [P, 8, S], F32R), ("a_ql", [P, 8, S], F32R),
                ("a_vh", [P, TT, 256], F32R), ("a_vl", [P, TT, 256], F32R),
                ("a_ph", [P, 2, S], F32R), ("a_pl", [P, 2, S], F32R),
                ("a_nmax", [P, 64], F32), ("a_sum", [P, 64], F32), ("a_rinv", [P, 64], F32)]}
            with ExitStack() as s2:
                at_.update({n: sb(n, s, F32, s2) for n, s in [
                    ("a_sq", [P, 2, 1024]), ("a_g", [P, 2, 1024]), ("a_rs", [P, 1024]), ("a_rot", [P, 1024]),
                    ("a_cos", [P, S]), ("a_sin", [P, S])]})
            with ExitStack() as s2:
                at_.update({n: sb(n, s, F32R, s2) for n, s in [("a_th", [P, 2, TT, S]), ("a_tl", [P, 2, TT, S])]})
        ml = scoped([
            ("m_hi", [P, 2, 2, S], F32R), ("m_lo", [P, 2, 2, S], F32R), ("m_r", [P, 2, 1024], F32),
            ("ada_w", [P, 2, 2048], F32), ("ada_t", [P, 2, 256], F32), ("ada_acc", [P, HALF_ADA, 256], F32)])
        with ExitStack() as scope:
            gl = {n: sb(n, s, F32, scope) for n, s in [
                ("g_q", [P, 2, GLA_H, S]), ("g_k", [P, 2, GLA_H, S]), ("g_v", [P, TT, D]), ("g_r", [P, KT, S]),
                ("g_a", [P, 2, TT, P]), ("g_dec", [P, 2, GLA_H, NCH]), ("g_tot", [P, GLA_H, NCH])]}
            with ExitStack() as s2:
                gl.update({n: sb(n, s, F32, s2) for n, s in [
                    ("g_x", [P, GLA_H, S]), ("g_t", [P, GLA_H, S]), ("g_z", [32, S]), ("g_up", [32, 2, S])]})
            with ExitStack() as s2:
                gl.update({n: sb(n, s, F32, s2) for n, s in [
                    ("g_s", [P, 2, NCH, GLA_DV]), ("g_kd", [P, 2, S]), ("g_kt", [P, 2, TT, P])]})
        with ExitStack() as scope:
            mx = {n: sb(n, s, d, scope) for n, s, d in [("x_yhi", [P, 6, S], F32R), ("x_ylo", [P, 6, S], F32R)]}
            with ExitStack() as s2:
                mx.update({n: sb(n, s, d, s2) for n, s, d in [
                    ("c_qh", [P, 2, S], F32R), ("c_ql", [P, 2, S], F32R), ("c_kh", [P, 1, S], F32R), ("c_kl", [P, 1, S], F32R),
                    ("c_vh", [P, TT, P], F32R), ("c_vl", [P, TT, P], F32R), ("c_wi", [P, TT, 4], F32),
                    ("x_ph", [P, 7 * P], F32R), ("x_pl", [P, 7 * P], F32R), ("x_th", [P, 10 * P], F32R), ("x_tl", [P, 10 * P], F32R),
                    ("x_m8", [P, 16], F32),
                    ("x_nmax", [P, 48], F32), ("x_sum", [P, 48], F32), ("x_rinv", [P, 48], F32)]})
                mx["x_mask"] = sb("x_mask", [P, 9 * P], F32, s2)
                with ExitStack() as s3:
                    mx["x_bias"] = sb("x_bias", [P, 4, 256], F32, s3)
                with ExitStack() as s3:
                    mx["x_neg"] = sb("x_neg", [P, 4, S], F32, s3)
                with ExitStack() as s3:
                    mx["pad"] = sb("x_pad", [P, 4 * S], F32, s3)
                    mx.update({n: sb(n, s, F32, s3) for n, s in [
                        ("x_qi", [P, 2, S]), ("x_ki", [P, 1, S]), ("x_rot", [P, 1024]), ("x_g", [P, 1024]),
                        ("x_cos", [P, S]), ("x_sin", [P, S])]})
                with ExitStack() as s3:
                    mx["pad2"] = sb("x_pad2", [P, 4 * S], F32, s3)
                    mx.update({n: sb(n, s, F32R, s3) for n, s in [
                        ("b_qh", [P, 2, S]), ("b_ql", [P, 2, S]), ("b_kh", [P, 2, S]), ("b_kl", [P, 2, S]),
                        ("b_vh", [P, TT, 256]), ("b_vl", [P, TT, 256])]})
            with ExitStack() as s2:
                mx.update({n: sb(n, s, d, s2) for n, s, d in [
                    ("x_mhi", [P, KT, S], F32R), ("x_mlo", [P, KT, S], F32R), ("x_gate", [P, 3, 1024], F32),
                    ("x_m", [P, 2, 1024], F32)]})
        ff = scoped([
            ("y", [P, KT, S], F32), ("f_hi", [P, 2, 2, S], F32R), ("f_lo", [P, 2, 2, S], F32R),
            ("f_c", [P, 2, 1024], F32), ("f_r", [P, 2, 1024], F32), ("f_prm", [P, 2, 8], F32)])
        y = ff["y"]

        x_in = [sem(f"x_in{c}") for c in range(4)]
        prm_in, con_in, rope_in, rope2_in, gup_in = map(sem, ("prm_in", "con_in", "rope_in", "rope2_in", "gup_in"))
        ones_set, ident_set = sem("ones_set"), sem("ident_set")
        w_in = [sem("w_in0"), sem("w_in1")]
        hi_done, split_done = sem("hi_done"), sem("split_done")
        block_done = sem("block_done")
        n_sq, n_ssq, n_std = sem("n_sq"), sem("n_ssq"), sem("n_std")
        n_row, n_hi, n_app = sem("n_row"), sem("n_hi"), sem("n_app")
        chain = sem("dve_chain")
        achain = sem("act_chain")
        out_st = sem("out_st")

        links = {"d": 0, "a": 0}

        def link(dve, ins):
            links["d"] += 1
            ins.then_inc(chain, 1)
            dve.wait_ge(chain, links["d"])

        def alink(act, ins):
            links["a"] += 1
            ins.then_inc(achain, 1)
            act.wait_ge(achain, links["a"])

        def split_hi(act, b, slot):
            act.wait_ge(w_in[slot], _land(b, slot))
            if not (isinstance(b, int) and b < 2):
                act.wait_ge(block_done, b - 1)
            act.activation(w_hi[:, slot], w_raw[:, slot], ACT.Copy).then_inc(hi_done, 1)

        def _land(b, slot):
            return 16 * (b // 2 + 1) if isinstance(b, int) else (b - slot) * 8 + 16

        def split_lo(dve, b, slot):
            dve.wait_ge(hi_done, b + 1)
            dve.tensor_tensor(w_lo[:, slot], w_raw[:, slot], w_hi[:, slot].bitcast(F32), ALU.subtract).then_inc(split_done, 1)

        def next_hi(act, b, slot):
            if not (isinstance(b, int) and b >= N_BLOCKS):
                split_hi(act, b, slot)

        def next_lo(dve, b, slot):
            if not (isinstance(b, int) and b >= N_BLOCKS):
                split_lo(dve, b, slot)

        def three(pe, out, w, h, start, stop):
            pe.matmul(out, w[0], h[0], start=start, stop=False)
            pe.matmul(out, w[0], h[1], start=False, stop=False)
            return pe.matmul(out, w[1], h[0], start=False, stop=stop)

        def wtile(slot, at):
            return w_hi[:, slot, at:at + P], w_lo[:, slot, at:at + P]

        def pe_block(pe, b, slot, hh, pair, rows=None, ntiles=2, each=None, tiles=range(KT)):
            pe.wait_ge(split_done, b + 1)
            for k in tiles:
                if rows is not None:
                    pe.wait_ge(n_app, rows + k + 1)
                if each is not None:
                    each(k)
                for n in range(ntiles):
                    last = three(pe, ps[:, 2 * pair + n, :], wtile(slot, k * 256 + n * P),
                                 (hh[0][:, k, :], hh[1][:, k, :]), k == 0, k == KT - 1)
            return last.then_inc(block_done, 1) if KT - 1 in tiles else last

        def pe_token_block(pe, b, slot, pair, width=256, count=True):
            pe.wait_ge(split_done, b + 1)
            for t in range(TT):
                out = ps[:, 2 * pair + t // 2, (t % 2) * 256:(t % 2) * 256 + width]
                for k in range(KT):
                    rows = slice(t * P, (t + 1) * P)
                    w = slice(k * 256, k * 256 + width)
                    pe.matmul(out, h_hi[:, k, rows], w_hi[:, slot, w], start=k == 0, stop=False)
                    pe.matmul(out, h_lo[:, k, rows], w_hi[:, slot, w], start=False, stop=False)
                    last = pe.matmul(out, h_hi[:, k, rows], w_lo[:, slot, w], start=False, stop=k == KT - 1)
            return last.then_inc(block_done, 1) if count else last

        def pair_(i):
            return ps[:, 2 * i:2 * i + 2, :]

        HH = (h_hi, h_lo)

        def squares(n):
            return ff["f_c"] if n == 7 else sq

        def act_square(act, n, j, src):
            if j >= 2:
                act.wait_ge(n_ssq, 4 * n + j - 1)
            elif n in (5, 7):
                act.wait_ge(n_app, 8 * (n - 1))
            elif n > 0:
                act.wait_ge(n_app, 8 * n)
            act.activation(squares(n)[:, j % 2].rearrange("p (a s) -> p a s", a=2), src[:, 2 * j:2 * j + 2, :], ACT.Square).then_inc(n_sq, 1)

        def pe_ssq(pe, n, j, bank):
            pe.wait_ge(n_sq, 4 * n + j + 1)
            for i in range(2):
                last = pe.matmul(ps[:, bank, :], ones[:], squares(n)[:, j % 2, i * S:(i + 1) * S],
                                 start=(j == 0 and i == 0), stop=(j == 3 and i == 1))
            last.then_inc(n_ssq, 1)

        def act_std(act, n, bank):
            act.wait_ge(n_ssq, 4 * n + 4)
            alink(act, act.activation(rstd[:], ps[:, bank, :], ACT.Ln, bias=pc("eps"), scale=1.0 / D))
            act.activation(rstd[:], rstd[:], ACT.Exp, scale=-0.5).then_inc(n_std, 1)

        def dve_rstd(dve, n):
            dve.wait_ge(n_std, n + 1)

        def act_norm_h(act, n, m, bank, shift=None):
            act_std(act, n, bank)
            for k in range(KT):
                act.wait_ge(n_row, 8 * m + k + 1)
                if shift is None:
                    act.activation(h_hi[:, k, :], trow[:, k % 4], ACT.Copy).then_inc(n_hi, 1)
                else:
                    act.activation(h_hi[:, k, :], trow[:, k % 4], ACT.Identity, bias=shift[:, k:k + 1]).then_inc(n_hi, 1)

        def dve_norm_h(dve, n, m, gain, shift=None):
            dve_rstd(dve, n)
            for k in range(KT + 2):
                if k < KT:
                    if k >= 4:
                        dve.wait_ge(n_app, 8 * n + k - 3)
                    dve.scalar_tensor_tensor(out=trow[:, k % 4], in0=x[:, k, :], scalar=gain[:, k:k + 1], in1=rstd[:],
                                             op0=ALU.mult, op1=ALU.mult).then_inc(n_row, 1)
                if k >= 2:
                    i = k - 2
                    dve.wait_ge(n_hi, 8 * m + i + 1)
                    dve.wait_ge(n_row, 8 * m + i + 1)
                    hi = h_hi[:, i, :].bitcast(F32)
                    if shift is None:
                        dve.tensor_tensor(h_lo[:, i, :], trow[:, i % 4], hi, ALU.subtract).then_inc(n_app, 1)
                    else:
                        dve.scalar_tensor_tensor(out=h_lo[:, i, :], in0=trow[:, i % 4], scalar=shift[:, i:i + 1], in1=hi,
                                                 op0=ALU.add, op1=ALU.subtract).then_inc(n_app, 1)

        def dve_norm_x(dve, n, gain):
            dve_rstd(dve, n)
            for k in range(KT):
                dve.scalar_tensor_tensor(out=x[:, k, :], in0=x[:, k, :], scalar=gain[:, k:k + 1], in1=rstd[:],
                                         op0=ALU.mult, op1=ALU.mult).then_inc(n_app, 1)

        def dve_norm_add(dve, n, gain):
            dve_rstd(dve, n)
            for k in range(KT + 1):
                if k < KT:
                    if k >= 4:
                        dve.wait_ge(n_app, 8 * n + k - 3)
                    dve.scalar_tensor_tensor(out=trow[:, k % 4], in0=y[:, k, :], scalar=gain[:, k:k + 1], in1=rstd[:],
                                             op0=ALU.mult, op1=ALU.mult).then_inc(y_row, 1)
                if k >= 1:
                    i = k - 1
                    dve.wait_ge(y_row, 8 * ynorms[n] + i + 1)
                    dve.tensor_tensor(x[:, i, :], x[:, i, :], trow[:, i % 4], ALU.add).then_inc(n_app, 1)
        y_row = sem("y_row")
        ynorms = {6: 0, 8: 1}

        proj_ev = sem("proj_ev")

        def proj_pair(i, j):
            return 3 if (i, j) == (0, 0) else j % 2

        def pe_proj(pe, i, b0, hh, n, bank, each, tiles=range(KT)):
            for j in range(4):
                b = b0 + j
                if j >= 2:
                    pe.wait_ge(proj_ev, 4 * i + j - 1)
                pe_block(pe, b, b % 2, hh, proj_pair(i, j), each=each if j == 0 else None, tiles=tiles if j == 0 else range(KT))
                if j >= 1:
                    pe_ssq(pe, n, j - 1, bank)
            pe_ssq(pe, n, 3, bank)

        def act_proj(act, i, b0, n, src, bank):
            for j in range(4):
                b = b0 + j
                if j < 3:
                    next_hi(act, b + 2, b % 2)
                act.wait_ge(proj_ev, 4 * i + j + 1)
                act_square(act, n, j, src)
                if j == 3:
                    next_hi(act, b + 2, b % 2)

        def dve_proj(dve, i, b0, dst, add):
            for j in range(4):
                b = b0 + j
                dve.wait_ge(block_done, b + 1)
                d = dst[:, 2 * j:2 * j + 2, :]
                if add:
                    dve.tensor_tensor(d, d, pair_(proj_pair(i, j)), ALU.add).then_inc(proj_ev, 1)
                else:
                    dve.tensor_copy(d, pair_(proj_pair(i, j))).then_inc(proj_ev, 1)
                next_lo(dve, b + 2, b % 2)

        class Attention:

            def __init__(self, name, heads, causal, wide, nmax, total, rinv, ph, pl, th, tl):
                self.heads, self.causal, self.wide = heads, causal, wide
                self.nmax, self.total, self.rinv, self.ph, self.pl, self.th, self.tl = nmax, total, rinv, ph, pl, th, tl
                self.n = TT * heads
                self.S, self.top, self.exp, self.ri, self.hi, self.lo, self.T, self.th_c, self.tl_c, self.PV, self.oh, self.ol = (
                    sem(name + k) for k in ("_scores", "_max", "_exp", "_rinv", "_p_hi", "_p_lo", "_turned", "_t_hi", "_t_lo", "_pv", "_o_hi", "_o_lo"))

            def part(self, ap, u):
                n = self.tiles(u) * P
                return ap[:, u % 2 * 3 * P:u % 2 * 3 * P + n] if self.causal else ap[:, u % 2, 0:n]

            def tiles(self, u):
                return u % TT + 1 if self.causal else TT

        def pair_block(half, k):
            base, last = (0, 1) if half == 0 else (3 * P, 3)
            return base + 2 * P * k, P if k == last else 2 * P

        def turned_places(A, th, u):
            qt, n = u % TT, A.tiles(u)
            if A.wide:
                return [(th[:, (u // TT) % 2, :, qt * P:(qt + 1) * P], 0, n)]
            if qt < 2:
                return [(th[:, (0, P)[qt]:(P, 3 * P)[qt]].rearrange("p (c q) -> p c q", q=P), 0, n)]
            body = th[:, 3 * P:9 * P].rearrange("p (c q) -> p c q", q=2 * P)[:, :, (qt - 2) * P:(qt - 1) * P]
            return [(body, 0, 3)] + ([(th[:, 9 * P:10 * P].rearrange("p (c q) -> p c q", q=P), 3, 1)] if qt == 3 else [])

        def wait_turned(engine, A, u):
            head, qt = divmod(u, TT)
            if A.wide and qt == 0 and head >= 2:
                engine.wait_ge(A.PV, TT * (head - 1))
            if A.causal and head >= 1:
                engine.wait_ge(A.PV, 2 * head + qt // 2 - 1)

        def pe_attend(pe, A, u0, u1, operands, values_of, first, second=None, third=None, fill=None):
            def scores(u):
                head, qt = divmod(u, TT)
                if u == u0:
                    first()
                if u >= 2:
                    pe.wait_ge(A.exp if not A.causal else A.top, u - 1)
                r = slice(64 * (head % 2), 64 * (head % 2) + 64)
                qh, ql, kh, kl = operands(head)
                q, nk = slice(qt * P, (qt + 1) * P), A.tiles(u) * P
                three(pe, ps[:, 6 + u % 2, 0:nk], (qh[r, q], ql[r, q]), (kh[r, 0:nk], kl[r, 0:nk]), True, True).then_inc(A.S, 1)

            def turn(u):
                pe.wait_ge(A.lo, u + 1)
                if u >= 2:
                    pe.wait_ge(A.th_c, u - 1)
                    pe.wait_ge(A.tl_c, u - 1)
                for src, bank in ((A.ph, 2), (A.pl, 4)):
                    for c in range(A.tiles(u)):
                        w = slice(c * P, (c + 1) * P)
                        last = pe.transpose(ps[:, bank + u % 2, w].bitcast(F32R), A.part(src, u)[:, w], identr[:])
                last.then_inc(A.T, 1)

            def values(u):
                head, c = divmod(u, TT)
                if u == u0 + (0 if A.wide else 1) and third is not None:
                    third()
                if c < 2 and head >= 2:
                    pe.wait_ge(A.ol, head - 1)
                if A.wide:
                    if c == 0:
                        pe.wait_ge(A.th_c, TT * head + TT)
                        pe.wait_ge(A.tl_c, TT * head + TT)
                    last = three(pe, ps[:, head % 2, :], values_of(head, c), (A.th[:, head % 2, c, :], A.tl[:, head % 2, c, :]),
                                 c == 0, c == TT - 1)
                else:
                    pe.wait_ge(A.th_c, u + 1)
                    pe.wait_ge(A.tl_c, u + 1)
                    for k in range(c + 1):
                        at, n = pair_block(c // 2, k)
                        last = three(pe, ps[:, head % 2, (c + 1) * P - n:(c + 1) * P], values_of(head, k),
                                     (A.th[:, at:at + n], A.tl[:, at:at + n]), k == 0, k == c)
                last.then_inc(A.PV, 1)

            lag = 8 if A.wide else 5
            for s in range(u0, u1 + lag):
                if s < u1:
                    scores(s)
                if s == u0 + 1 and second is not None:
                    second()
                if u0 <= s - 3 < u1:
                    turn(s - 3)
                if s == u1 + 2 and fill is not None:
                    fill()
                if u0 <= s - lag < u1 and (A.wide or (s - lag) % 2):
                    values(s - lag)

        def act_attend(act, A, u0, u1, source, dst, beside=None):
            def probs(u):
                act.wait_ge(A.top, u + 1)
                if u >= 3 and not A.causal:
                    act.wait_ge(A.lo, u - 2)
                n = A.tiles(u) * P
                act.activation(p_s[:, u % 3, 0:n], source(u), ACT.Exp, bias=A.nmax[:, u:u + 1],
                               accum_out=A.total[:, u:u + 1]).then_inc(A.exp, 1)

            def hi(u):
                act.wait_ge(A.ri, u + 1)
                if u >= 2:
                    act.wait_ge(A.T, u - 1)
                n = A.tiles(u) * P
                act.activation(A.part(A.ph, u), p_s[:, u % 3, 0:n], ACT.Copy, scale=A.rinv[:, u:u + 1]).then_inc(A.hi, 1)

            def turned(u):
                act.wait_ge(A.T, u + 1)
                wait_turned(act, A, u)
                src = ps[:, 2 + u % 2, :].rearrange("p (c q) -> p c q", q=P)
                for dst_, c, n in turned_places(A, A.th, u):
                    ins = act.activation(dst_, src[:, c:c + n, :], ACT.Copy)
                ins.then_inc(A.th_c, 1)
                if A.causal:
                    src = ps[:, 4 + u % 2, :].rearrange("p (c q) -> p c q", q=P)
                    for dst_, c, n in turned_places(A, A.tl, u):
                        ins = act.activation(dst_, src[:, c:c + n, :], ACT.Copy)
                    ins.then_inc(A.tl_c, 1)

            def out(head):
                r = slice(64 * (head % 2), 64 * (head % 2) + 64)
                act.wait_ge(A.PV, (TT if A.wide else 2) * (head + 1))
                act.activation(dst(head)[0][r], ps[r, head % 2, :], ACT.Copy).then_inc(A.oh, 1)

            lag = 9 if A.wide else 6
            for s in range(u0, u1 + lag):
                if u0 <= s - 4 < u1:
                    turned(s - 4)
                if u0 <= s - 1 < u1:
                    hi(s - 1)
                if s < u1:
                    probs(s)
                if u0 <= s - lag < u1 and (s - lag) % TT == TT - 1:
                    out((s - lag) // TT)
                if beside is not None:
                    beside(s)

        def dve_attend(dve, A, u0, u1, top, dst, beside=None):
            def rinv(u):
                dve.wait_ge(A.exp, u + 1)
                dve.reciprocal(A.rinv[:, u:u + 1], A.total[:, u:u + 1]).then_inc(A.ri, 1)

            def lo(u):
                dve.wait_ge(A.hi, u + 1)
                dve.wait_ge(A.ri, u + 1)
                if u >= 2:
                    dve.wait_ge(A.T, u - 1)
                n = A.tiles(u) * P
                dve.scalar_tensor_tensor(out=A.part(A.pl, u), in0=p_s[:, u % 3, 0:n], scalar=A.rinv[:, u:u + 1],
                                         in1=A.part(A.ph, u).bitcast(F32), op0=ALU.mult, op1=ALU.subtract).then_inc(A.lo, 1)

            def turned(u):
                if A.causal:
                    return
                dve.wait_ge(A.T, u + 1)
                wait_turned(dve, A, u)
                src = ps[:, 4 + u % 2, :].rearrange("p (c q) -> p c q", q=P)
                for dst_, c, n in turned_places(A, A.tl, u):
                    ins = dve.tensor_copy(dst_, src[:, c:c + n, :])
                ins.then_inc(A.tl_c, 1)

            def out(head):
                r = slice(64 * (head % 2), 64 * (head % 2) + 64)
                dve.wait_ge(A.oh, head + 1)
                hi, low = dst(head)
                dve.tensor_tensor(low[r], ps[r, head % 2, :], hi[r].bitcast(F32), ALU.subtract).then_inc(A.ol, 1)

            lag = 9 if A.wide else 6
            for s in range(u0, u1 + lag):
                if u0 <= s - 2 < u1:
                    lo(s - 2)
                if u0 <= s - 4 < u1:
                    turned(s - 4)
                if u0 <= s - 1 < u1:
                    rinv(s - 1)
                if s < u1:
                    top(s)
                if u0 <= s - lag < u1 and (s - lag) % TT == TT - 1:
                    out((s - lag) // TT)
                if beside is not None:
                    beside(s)

        A1 = Attention("a", 16, False, True, at_["a_nmax"], at_["a_sum"], at_["a_rinv"], at_["a_ph"], at_["a_pl"], at_["a_th"], at_["a_tl"])
        a_v_hi, a_v_lo, a_raw, a_aux, a_rs, a_rows, a_qhi, a_ready = map(sem, (
            "a_v_hi", "a_v_lo", "a_raw", "a_aux", "a_rs_s", "a_rows", "a_qhi", "a_ready"))
        V_BLOCK = N_QKV - 1
        two = lambda ap: ap.rearrange("p (a s) -> p a s", a=2)

        def attn_pe(pe):
            def aux(j):
                a = j
                if a == 0:
                    pe.wait_ge(con_in, 16)
                pe.wait_ge(a_raw, a + 1)
                if a >= 1:
                    pe.wait_ge(a_rows, a)
                for i in range(2):
                    pe.matmul(ps[:, 4 + i, :], mat(HALVES), at_["a_sq"][:, a % 2, i * S:(i + 1) * S], start=True, stop=True)
                for i in range(2):
                    last = pe.matmul(ps[:, 6 + i, :], mat(ROT_A), at_["a_g"][:, a % 2, i * S:(i + 1) * S], start=True, stop=True)
                last.then_inc(a_aux, 1)

            for j in range(N_QKV):
                b = B_QKV + j
                if j >= 2:
                    pe.wait_ge(a_raw, j - 1)
                if j == V_BLOCK:
                    pe_token_block(pe, b, b % 2, j % 2)
                else:
                    pe_block(pe, b, b % 2, HH, j % 2, rows=0 if j == 0 else None)
                if j >= 1:
                    aux(j - 1)
            pe.wait_ge(ident_set, 1)
            pe.wait_ge(a_v_lo, 1)
            pe.wait_ge(a_rows, V_BLOCK)

            def operands(h):
                if h == 4:
                    pe.wait_ge(a_ready, V_BLOCK)
                return at_["a_qh"][:, h // 2], at_["a_ql"][:, h // 2], at_["a_kh"][:, h // 8], at_["a_kl"][:, h // 8]

            def project():
                pe_block(pe, B_WO0, B_WO0 % 2, HH, proj_pair(0, 0), each=lambda k: pe.wait_ge(A1.ol, 2 * k + 2), tiles=range(KT - 1))

            pe_attend(pe, A1, 0, A1.n, operands,
                      lambda h, c: (at_["a_vh"][:, c, P * (h // 8):P * (h // 8) + P], at_["a_vl"][:, c, P * (h // 8):P * (h // 8) + P]),
                      first=lambda: pe.wait_ge(a_ready, 2), fill=project)

        def attn_act(act):
            def root(j):
                a = j
                act.wait_ge(a_aux, a + 1)
                if a >= 1:
                    act.wait_ge(a_rows, a)
                alink(act, act.activation(two(at_["a_rs"][:]), ps[:, 4:6, :], ACT.Ln, bias=pc("eps"), scale=1.0 / HD))
                act.activation(at_["a_rs"][:], at_["a_rs"][:], ACT.Exp, scale=-0.5).then_inc(a_rs, 1)

            def q_hi(j):
                a = j
                act.wait_ge(a_rows, a + 1)
                dst = at_["a_kh"][:] if a == 0 else at_["a_qh"][:, 2 * a - 2:2 * a]
                act.activation(dst, two(at_["a_rot"][:]), ACT.Copy).then_inc(a_qhi, 1)

            for j in range(N_QKV):
                b = B_QKV + j
                act.wait_ge(block_done, b + 1)
                if j == V_BLOCK:
                    act.activation(at_["a_vh"][:], ps[:, 2:4, :].rearrange("p a (b n) -> p (a b) n", n=256), ACT.Copy).then_inc(a_v_hi, 1)
                else:
                    a = j
                    if a >= 2:
                        act.wait_ge(a_aux, a - 1)
                        act.wait_ge(a_ready, a - 1)
                    act.activation(two(at_["a_sq"][:, a % 2]), pair_(j % 2), ACT.Square)
                    act.activation(two(at_["a_g"][:, a % 2]), pair_(j % 2), ACT.Copy,
                                   scale=pc("kg" if j == 0 else "qg")).then_inc(a_raw, 1)
                if j < V_BLOCK:
                    next_hi(act, b + 2, b % 2)
                if j >= 1:
                    root(j - 1)
                    q_hi(j - 1)
            act_attend(act, A1, 0, A1.n, lambda u: ps[:, 6 + u % 2, :], lambda h: (h_hi[:, h // 2], h_lo[:, h // 2]),
                       lambda s: next_hi(act, B_WO0 + 1, (B_WO0 + 1) % 2) if s == 6 else None)

        def attn_dve(dve):
            def rope(j):
                a = j
                dve.wait_ge(a_aux, a + 1)
                if a == 0:
                    dve.wait_ge(rope_in, 32)
                if a >= 1:
                    dve.wait_ge(a_qhi, a)
                for i in range(2):
                    g = at_["a_g"][:, a % 2, i * S:(i + 1) * S]
                    dve.tensor_tensor(g, g, at_["a_cos"][:], ALU.mult)
                    ins = dve.tensor_tensor(at_["a_rot"][:, i * S:(i + 1) * S], ps[:, 6 + i, :], at_["a_sin"][:], ALU.mult)
                link(dve, ins)
                link(dve, dve.tensor_tensor(at_["a_rot"][:], at_["a_rot"][:], at_["a_g"][:, a % 2], ALU.add))
                dve.wait_ge(a_rs, a + 1)
                dve.scalar_tensor_tensor(out=at_["a_rot"][:], in0=at_["a_rot"][:], scalar=1.0 if j == 0 else HD ** -0.5,
                                         in1=at_["a_rs"][:], op0=ALU.mult, op1=ALU.mult).then_inc(a_rows, 1)
                dve.wait_ge(a_rows, a + 1)
                dve.wait_ge(a_qhi, a + 1)
                hi = at_["a_kh"][:] if a == 0 else at_["a_qh"][:, 2 * a - 2:2 * a]
                lo = at_["a_kl"][:] if a == 0 else at_["a_ql"][:, 2 * a - 2:2 * a]
                dve.tensor_tensor(lo, two(at_["a_rot"][:]), hi.bitcast(F32), ALU.subtract).then_inc(a_ready, 1)
                dve.wait_ge(a_ready, a + 1)

            for j in range(N_QKV):
                b = B_QKV + j
                if j == V_BLOCK:
                    dve.wait_ge(a_v_hi, 1)
                    dve.tensor_tensor(at_["a_vl"][:], ps[:, 2:4, :].rearrange("p a (b n) -> p (a b) n", n=256),
                                      at_["a_vh"][:].bitcast(F32), ALU.subtract).then_inc(a_v_lo, 1)
                if j < V_BLOCK:
                    next_lo(dve, b + 2, b % 2)
                if j >= 1:
                    rope(j - 1)

            def top(u):
                dve.wait_ge(A1.S, u + 1)
                dve.tensor_reduce(A1.nmax[:, u:u + 1], ps[:, 6 + u % 2, :], AX, ALU.max, negate=True).then_inc(A1.top, 1)
            dve_attend(dve, A1, 0, A1.n, top, lambda h: (h_hi[:, h // 2], h_lo[:, h // 2]),
                       lambda s: next_lo(dve, B_WO0 + 1, (B_WO0 + 1) % 2) if s == 6 else None)

        m_relu, m_sq, m_hi, m_lo, m_out, m_add = map(sem, ("m_relu", "m_sq", "m_hi_s", "m_lo_s", "m_out", "m_add"))

        def mlp_in(pe, i, u, par, b, slot, rows=None):
            c = MLP_UNITS * i + u
            if not (isinstance(u, int) and u < 2):
                pe.wait_ge(m_relu, c - 1)
            pe_block(pe, b, slot, HH, par, rows=rows)

        def mlp_out(pe, i, u, par, b, slot, after=None):
            c = MLP_UNITS * i + u
            pe.wait_ge(m_lo, c + 1)
            pe.wait_ge(split_done, b + 1)
            for q in range(4):
                if not (isinstance(u, int) and u == 0 and q < 2):
                    pe.wait_ge(m_add, 4 * c + q - 1)
                for k in range(2):
                    for n in range(2):
                        last = three(pe, ps[:, 4 + 2 * (q % 2) + n, :], wtile(slot, k * 1024 + (2 * q + n) * P),
                                     (ml["m_hi"][:, par, k, :], ml["m_lo"][:, par, k, :]), k == 0, k == 1)
                last.then_inc(m_out if q < 3 else block_done, 1)
                if after is not None:
                    after(q)

        def mlp_pe(pe, i, b0, n, after_norm=None):
            mlp_in(pe, i, 0, 0, b0, b0 % 2, rows=8 * (n - 1))

            def turn(it):
                for d in (1, 2):
                    mlp_in(pe, i, it * 2 + d, d % 2, it * 4 + (b0 + 2 * d - 1), (b0 + 1) % 2)
                    mlp_out(pe, i, it * 2 + (d - 1), (d - 1) % 2, it * 4 + (b0 + 2 * d), b0 % 2)

            turn(0)
            with pe.Fori(1, (MLP_UNITS - 2) // 2) as it:
                turn(it)
            u = MLP_UNITS - 1
            mlp_in(pe, i, u, u % 2, b0 + 2 * u - 1, (b0 + 1) % 2)
            mlp_out(pe, i, u - 1, (u - 1) % 2, b0 + 2 * u, b0 % 2)

            def after(q):
                if q >= 2:
                    pe_ssq(pe, n, q - 2, 2 * 1)
            mlp_out(pe, i, u, u % 2, b0 + 2 * u + 1, (b0 + 1) % 2, after=after)
            pe_ssq(pe, n, 2, 2)
            pe_ssq(pe, n, 3, 2)

        def mlp_act_in(act, i, u, par, b, slot, more=True):
            c = MLP_UNITS * i + u
            act.wait_ge(block_done, b + 1)
            if not (isinstance(u, int) and i == 0 and u < 2):
                act.wait_ge(m_lo, c - 1)
            act.activation(ml["m_r"][:, par].rearrange("p (a s) -> p a s", a=2), pair_(par), ACT.Relu).then_inc(m_relu, 1)
            split_hi(act, b + 2, slot)
            act.wait_ge(m_sq, c + 1)
            act.activation(ml["m_hi"][:, par], ml["m_r"][:, par].rearrange("p (a s) -> p a s", a=2), ACT.Copy).then_inc(m_hi, 1)
            if more:
                split_hi(act, b + 3, 1 - slot)

        def mlp_act(act, i, b0, n):
            mlp_act_in(act, i, 0, 0, b0, b0 % 2, more=False)

            def turn(it):
                for d in (1, 2):
                    mlp_act_in(act, i, it * 2 + d, d % 2, it * 4 + (b0 + 2 * d - 1), (b0 + 1) % 2)

            turn(0)
            with act.Fori(1, (MLP_UNITS - 2) // 2) as it:
                turn(it)
            u = MLP_UNITS - 1
            mlp_act_in(act, i, u, u % 2, b0 + 2 * u - 1, (b0 + 1) % 2)
            for q in range(4):
                act.wait_ge(m_add, 4 * (MLP_UNITS * i + u) + q + 1)
                act_square(act, n, q, x)
            next_hi(act, b0 + 2 * u + 3, (b0 + 1) % 2)

        def mlp_dve_add(dve, i, u, q, b):
            c = MLP_UNITS * i + u
            if q < 3:
                dve.wait_ge(m_out, 3 * c + q + 1)
            else:
                dve.wait_ge(block_done, b + 1)
            if not (isinstance(u, int) and u == 0 and i == 0):
                dve.wait_ge(m_add, 4 * c + q - 3)
            xd = x[:, 2 * q:2 * q + 2, :]
            dve.tensor_tensor(xd, xd, pair_(2 + q % 2), ALU.add).then_inc(m_add, 1)

        def mlp_dve_in(dve, i, u, par, b, slot, prev=True):
            c = MLP_UNITS * i + u
            dve.wait_ge(m_relu, c + 1)
            r = ml["m_r"][:, par]
            dve.tensor_tensor(r, r, r, ALU.mult).then_inc(m_sq, 1)
            if prev:
                mlp_dve_add(dve, i, u - 1, 0, b + 1)
            split_lo(dve, b + 2, slot)
            if prev:
                mlp_dve_add(dve, i, u - 1, 1, b + 1)
            dve.wait_ge(m_hi, c + 1)
            dve.tensor_tensor(ml["m_lo"][:, par], r.rearrange("p (a s) -> p a s", a=2), ml["m_hi"][:, par].bitcast(F32),
                              ALU.subtract).then_inc(m_lo, 1)
            if prev:
                mlp_dve_add(dve, i, u - 1, 2, b + 1)
                mlp_dve_add(dve, i, u - 1, 3, b + 1)
                split_lo(dve, b + 3, 1 - slot)

        def mlp_dve(dve, i, b0):
            mlp_dve_in(dve, i, 0, 0, b0, b0 % 2, prev=False)

            def turn(it):
                for d in (1, 2):
                    mlp_dve_in(dve, i, it * 2 + d, d % 2, it * 4 + (b0 + 2 * d - 1), (b0 + 1) % 2)

            turn(0)
            with dve.Fori(1, (MLP_UNITS - 2) // 2) as it:
                turn(it)
            u = MLP_UNITS - 1
            mlp_dve_in(dve, i, u, u % 2, b0 + 2 * u - 1, (b0 + 1) % 2)
            for q in range(4):
                mlp_dve_add(dve, i, u, q, b0 + 2 * u + 1)
            next_lo(dve, b0 + 2 * u + 3, (b0 + 1) % 2)

        g_ev, g_ev2, g_log, g_xr, g_x2, g_b, g_e1, g_e2, g_qk = map(sem, (
            "g_ev", "g_ev2", "g_logits", "g_x_ready", "g_soft", "g_cum", "g_exp", "g_expn", "g_qk"))
        g_aT, g_ac, g_az, g_am, g_kd, g_kT, g_kc, g_ckv, g_st, g_O, g_sq, g_ss, g_rt, g_oh, g_ol, g_row = map(sem, (
            "g_aT", "g_a_copied", "g_a_zero", "g_a_masked", "g_kd_s", "g_kT", "g_kt_s", "g_ckv", "g_states", "g_O", "g_sq",
            "g_ss", "g_root", "g_o_hi", "g_o_lo", "g_row"))
        g_or = sem("g_o_rooted")
        INV_TAU = 1.0 / 16.0
        chunks = lambda ap: ap.rearrange("p h (n c) -> p (h n) c", c=CH)

        def qk(t, d):
            return gl[t][:, 1 - d]

        def chunks_of(d):
            return list(range(NCH - 1)) if d == 0 else list(range(NCH - 1, 0, -1))

        def half_of(h, d=0):
            return 4 * ((h + d) % 2)

        def chunk_bank(h, d, n):
            return ps[:, half_of(h, d) + 2 * (n % 2) + n // 4, ((n // 2) % 2) * 256:((n // 2) % 2) * 256 + 256]

        def gla_pe(pe, b0, rows):
            def logits(d):
                if d == 0:
                    pe.wait_ge(gup_in, 16)
                    pe.wait_ge(g_ev, 1)
                else:
                    pe.wait_ge(g_xr, GLA_H)
                for h in range(GLA_H):
                    last = pe.matmul(ps[:, 4 + h, :], gl["g_up"][:, d, h * P:(h + 1) * P], gl["g_z"][:], start=True, stop=True)
                last.then_inc(g_log, 1)

            for j in range(N_GLA):
                b = b0 + j
                if j == 1:
                    pe.wait_ge(mod_set, 1)
                if j >= 2:
                    pe.wait_ge(g_ev, j - 1)
                if 5 <= j < 9:
                    pe_token_block(pe, b, b % 2, j % 2)
                else:
                    pe_block(pe, b, b % 2, HH, j % 2, rows=rows if j == 0 else None, ntiles=1 if j == 0 else 2)
                if j == 1:
                    logits(0)
                if j == 3:
                    logits(1)
            pe.wait_ge(g_ev, N_GLA)

            def within(h):
                for d in range(2):
                    e, bank = 2 * h + d, half_of(h) + 2 * d
                    pe.wait_ge(g_qk, 2)
                    if h >= 1:
                        pe.wait_ge(g_st, 2 * h)
                    for t in range(TT):
                        w = slice(t * P, (t + 1) * P)
                        last = pe.matmul(ps[:, bank, w], qk("g_k", d)[:, h, w], qk("g_q", d)[:, h, w], start=True, stop=True)
                    last.then_inc(g_aT, 1)
                    pe.wait_ge(g_kd, e + 1)
                    for t in range(TT):
                        w = slice(t * P, (t + 1) * P)
                        last = pe.transpose(ps[:, bank + 1, w], gl["g_kd"][:, d, w], mat(IDENT))
                    last.then_inc(g_kT, 1)

            within(0)
            for h in range(GLA_H):
                for d in range(2):
                    if d == 0:
                        pe.wait_ge(g_kc, 2 * h + 2)
                        pe.wait_ge(g_ac, 2 * h + 2)
                    elif h >= 1:
                        pe.wait_ge(g_or, h)
                    for i, n in enumerate(chunks_of(d)):
                        r = slice(CH * (n % 2), CH * (n % 2) + CH)
                        last = pe.matmul(chunk_bank(h, d, n),
                                         gl["g_kt"][r, d, n // 2, :], gl["g_v"][r, n // 2, h * 256:h * 256 + 256], start=True, stop=True)
                        if i in (NCH // 2 - 1, NCH - 2):
                            last.then_inc(g_ckv, 1)
                bank = half_of(h)
                pe.wait_ge(g_am, 2 * (h + 1))
                pe.wait_ge(g_st, 2 * h + 1)
                for i in range(2):
                    vcol = slice(h * 256 + i * P, h * 256 + (i + 1) * P)
                    for t in range(TT):
                        for d in range(2):
                            pe.matmul(ps[:, bank + i, t * P:(t + 1) * P], gl["g_v"][:, t, vcol], gl["g_a"][:, d, t, :],
                                      start=t == 0 and d == 0, stop=False)
                pe.wait_ge(g_st, 2 * h + 2)
                for i in range(2):
                    for n in range(NCH):
                        todo = [d for d in range(2) if n != (0 if d == 0 else NCH - 1)]
                        for d in todo:
                            last = pe.matmul(ps[:, bank + i, n * CH:(n + 1) * CH], gl["g_s"][:, d, n, i * P:(i + 1) * P],
                                             qk("g_q", d)[:, h, n * CH:(n + 1) * CH], start=False, stop=n == NCH - 1)
                last.then_inc(g_O, 1)
                if h + 1 < GLA_H:
                    within(h + 1)
                pe.wait_ge(g_sq, h + 1)
                for i in range(2):
                    last = pe.matmul(ps[:, bank + 2, :], ones[:], sq[:, 0, i * S:(i + 1) * S], start=i == 0, stop=i == 1)
                last.then_inc(g_ss, 1)

        def gla_act(act, b0):
            def gates(d):
                for h in range(GLA_H):
                    if h == 0:
                        act.wait_ge(g_log, d + 1)
                        if d == 1:
                            act.wait_ge(g_qk, 1)
                    act.activation(gl["g_x"][:, h, :], ps[:, 4 + h, :], ACT.Identity, bias=pc("gla_b", 4 * d + h)).then_inc(g_xr, 1)
                act.wait_ge(g_xr, GLA_H * (d + 1))
                t = gl["g_t"][:]
                alink(act, act.activation(t, gl["g_x"][:], ACT.Abs))
                alink(act, act.activation(t, t, ACT.Exp, scale=-1.0))
                act.activation(t, t, ACT.Ln, bias=1.0).then_inc(g_x2, 1)

            def exps(d):
                act.wait_ge(g_b, d + 1)
                act.activation(gl["g_dec"][:, d], gl["g_tot"][:], ACT.Exp, scale=INV_TAU)
                act.activation(gl["g_x"][:], gl["g_t"][:], ACT.Exp, scale=INV_TAU).then_inc(g_e1, 1)
                act.wait_ge(g_e1, d + 1)
                act.activation(gl["g_t"][:], gl["g_t"][:], ACT.Exp, scale=-INV_TAU).then_inc(g_e2, 1)

            for j in range(N_GLA):
                b = b0 + j
                act.wait_ge(block_done, b + 1)
                if j == 0:
                    act.activation(gl["g_z"][:], ps[0:32, 0, :], ACT.Copy).then_inc(g_ev, 1)
                elif j < 5:
                    t, i = ("g_q", 2 * (j - 1)) if j < 3 else ("g_k", 2 * (j - 3))
                    act.activation(gl[t][:, 0, i:i + 2, :], pair_(j % 2), ACT.Copy, scale=GLA_DK ** -0.5 if j < 3 else 1.0).then_inc(g_ev, 1)
                elif j < 9:
                    c = 256 * (j - 5)
                    act.activation(gl["g_v"][:, :, c:c + 256], pair_(j % 2).rearrange("p a (b n) -> p (a b) n", n=256), ACT.Copy).then_inc(g_ev, 1)
                else:
                    i = 2 * (j - 9)
                    act.activation(gl["g_r"][:, i:i + 2, :], pair_(j % 2), ACT.Silu).then_inc(g_ev, 1)
                next_hi(act, b + 2, b % 2)
                if j == 1:
                    gates(0)
                if j == 4:
                    exps(0)
                if j == 5:
                    gates(1)
                if j == 7:
                    exps(1)
            act.preload_act_table_set("natural_log_exp_and_others")

            def turned(h):
                for d in range(2):
                    act.wait_ge(g_kT, 2 * h + d + 1)
                    if h >= 1:
                        act.wait_ge(g_ckv, 4 * h)
                    act.activation(gl["g_kt"][:, d], ps[:, half_of(h) + 2 * d + 1, :].rearrange("p (t k) -> p t k", t=TT), ACT.Copy).then_inc(g_kc, 1)

            turned(0)
            for h in range(GLA_H):
                act.wait_ge(g_O, h + 1)
                if h == 0:
                    act.wait_ge(n_app, 8 * 3)
                else:
                    act.wait_ge(g_ss, h)
                act.activation(two(sq[:, 0]), ps[:, half_of(h):half_of(h) + 2, :], ACT.Square).then_inc(g_sq, 1)
                if h + 1 < GLA_H:
                    turned(h + 1)
                act.wait_ge(g_ss, h + 1)
                if h >= 1:
                    act.wait_ge(g_or, h)
                alink(act, act.activation(rstd[:], ps[:, half_of(h) + 2, :], ACT.Ln, bias=pc("eps"), scale=1.0 / GLA_DV))
                act.activation(rstd[:], rstd[:], ACT.Exp, scale=-0.5).then_inc(g_rt, 1)
                for i in range(2):
                    act.wait_ge(g_row, 2 * h + i + 1)
                    act.activation(h_hi[:, 2 * h + i, :], gl["g_r"][:, 2 * h + i, :], ACT.Copy).then_inc(g_oh, 1)

        def gla_dve(dve, b0):
            def cumulate(d):
                dve.wait_ge(g_x2, d + 1)
                x_, t = gl["g_x"][:], gl["g_t"][:]
                link(dve, dve.scalar_tensor_tensor(out=x_, in0=x_, scalar=0.0, in1=t, op0=ALU.min, op1=ALU.subtract))
                for h in range(GLA_H):
                    ins = dve.tensor_tensor_scan(gl["g_t"][:, h, :], con[:, RESET:RESET + S], gl["g_x"][:, h, :], 0.0, ALU.mult, ALU.add)
                link(dve, ins)
                ends = gl["g_t"][:].rearrange("p h (n c) -> p h n c", c=CH)[:, :, :, CH - 1]
                if d == 1:
                    dve.wait_ge(g_e1, 1)
                ins = dve.tensor_copy(gl["g_tot"][:], ends)
                if d == 0:
                    ins.then_inc(g_b, 1)
                else:
                    link(dve, ins)
                    link(dve, dve.tensor_tensor(t, x_, t, ALU.subtract))
                    tot = gl["g_tot"][:].rearrange("p h n -> p (h n)").unsqueeze(2).to_broadcast([P, GLA_H * NCH, CH])
                    dve.tensor_tensor(chunks(gl["g_t"][:]), chunks(gl["g_t"][:]), tot, ALU.add).then_inc(g_b, 1)

            def scaled(d):
                dve.wait_ge(g_e2, d + 1)
                dve.tensor_tensor(qk("g_q", d), gl["g_q"][:, 0], gl["g_x"][:], ALU.mult)
                dve.tensor_tensor(qk("g_k", d), gl["g_k"][:, 0], gl["g_t"][:], ALU.mult).then_inc(g_qk, 1)

            for j in range(N_GLA):
                b = b0 + j
                next_lo(dve, b + 2, b % 2)
                if j == 1:
                    cumulate(0)
                if j == 4:
                    dve.wait_ge(g_ev, 5)
                    scaled(0)
                if j == 5:
                    cumulate(1)
                if j == 7:
                    dve.wait_ge(g_qk, 1)
                    scaled(1)
            dve.wait_ge(g_qk, 2)
            dve.memset(gl["g_a"][:], 0.0).then_inc(g_az, 1)
            dve.wait_ge(g_az, 1)

            def decayed(h):
                for d in range(2):
                    if h >= 1:
                        dve.wait_ge(g_kT, 2 * h)
                    dec = gl["g_dec"][:, d, h, :].unsqueeze(2).to_broadcast([P, NCH, CH])
                    dve.tensor_tensor(gl["g_kd"][:, d].rearrange("p (n c) -> p n c", c=CH),
                                      qk("g_k", d)[:, h, :].rearrange("p (n c) -> p n c", c=CH), dec, ALU.mult).then_inc(g_kd, 1)

            def within(h):
                for d in range(2):
                    dve.wait_ge(g_aT, 2 * h + d + 1)
                    if h >= 1:
                        dve.wait_ge(g_O, h)
                        dve.wait_ge(g_am, 2 * h)
                    for r in (slice(0, CH), slice(CH, P)):
                        ins = dve.tensor_copy(gl["g_a"][r, d, :, r], ps[r, half_of(h) + 2 * d, :].rearrange("p (t c) -> p t c", t=TT)[:, :, r])
                    ins.then_inc(g_ac, 1)

            def states(h, d):
                prev = None
                for i, n in enumerate(chunks_of(d)):
                    to = n + 1 if d == 0 else n - 1
                    if i in (0, NCH // 2):
                        dve.wait_ge(g_ckv, 4 * h + 2 * d + (1 if i == 0 else 2))
                    if prev is None:
                        ins = dve.tensor_copy(gl["g_s"][:, d, to, :], chunk_bank(h, d, n))
                    else:
                        ins = dve.scalar_tensor_tensor(out=gl["g_s"][:, d, to, :], in0=gl["g_s"][:, d, prev, :],
                                                       scalar=gl["g_dec"][:, d, h, n:n + 1], in1=chunk_bank(h, d, n), op0=ALU.mult, op1=ALU.add)
                    prev = to
                    if i == NCH - 2:
                        ins.then_inc(g_st, 1)
                    else:
                        link(dve, ins)

            def root(h):
                dve.wait_ge(g_rt, h + 1)
                for i in range(2):
                    if h == 0 and i == 0:
                        dve.wait_ge(n_app, 24)
                    ins = dve.scalar_tensor_tensor(out=sq[:, 1, i * S:(i + 1) * S], in0=ps[:, half_of(h) + i, :], scalar=pc("out_g", i),
                                                   in1=rstd[:], op0=ALU.mult, op1=ALU.mult)
                ins.then_inc(g_or, 1)

            def gated(h):
                dve.wait_ge(g_or, h + 1)
                for i in range(2):
                    r = gl["g_r"][:, 2 * h + i, :]
                    dve.tensor_tensor(r, r, sq[:, 1, i * S:(i + 1) * S], ALU.mult).then_inc(g_row, 1)
                for i in range(2):
                    f = 2 * h + i
                    dve.wait_ge(g_oh, f + 1)
                    dve.wait_ge(g_row, f + 1)
                    dve.tensor_tensor(h_lo[:, f, :], gl["g_r"][:, f, :], h_hi[:, f, :].bitcast(F32), ALU.subtract).then_inc(g_ol, 1)

            decayed(0)
            within(0)
            for h in range(GLA_H):
                if h >= 1:
                    dve.wait_ge(g_O, h)
                states(h, 0)
                states(h, 1)
                if h >= 1:
                    gated(h - 1)
                if h + 1 < GLA_H:
                    decayed(h + 1)
                    within(h + 1)
                root(h)
            gated(GLA_H - 1)

        def gla_pool(pool):
            for h in range(GLA_H):
                for d in range(2):
                    pool.wait_ge(g_ac, 2 * h + d + 1)
                    sign = 1 if d == 0 else -1
                    v = gl["g_a"][:, d]
                    pool.affine_select(out=v, in_=v, compare_op=ALU.is_ge, fill=0.0, base=0, pattern=[[0, TT], [sign, P]],
                                       channel_multiplier=-sign).then_inc(g_am, 1)

        ada_in, ada_row, ada_used, ada_sum, mod_set = [sem("ada_in0"), sem("ada_in1")], sem("ada_row"), sem("ada_used"), sem("ada_sum"), sem("mod_set")
        c_set, ada_acc_s = sem("c_set"), sem("ada_acc_s")

        def ada_pool(pool, half):
            def fetch(j):
                pool.dma_start(ml["ada_w"][:, j % 2], ada_d[j]).then_inc(ada_in[j % 2], 16)

            pool.wait_ge(c_set, 1)
            j0 = HALF_ADA * half
            fetch(j0)
            fetch(j0 + 1)
            for j in range(j0, j0 + HALF_ADA):
                pool.wait_ge(ada_in[j % 2], 16 * (j // 2 + 1))
                for k in range(KT):
                    w = ml["ada_w"][:, j % 2, k * 256:(k + 1) * 256]
                    i = KT * j + k
                    if i >= 2:
                        pool.wait_ge(ada_acc_s, i - 1)
                    pool.tensor_scalar(ml["ada_t"][:, k % 2], w, cact[:, k:k + 1], None, ALU.mult).then_inc(ada_row, 1)
                    pool.wait_ge(ada_row, i + 1)
                    acc = ml["ada_acc"][:, j - j0]
                    if k == 0:
                        ins = pool.tensor_copy(acc, ml["ada_t"][:, k % 2])
                    else:
                        pool.wait_ge(ada_acc_s, i)
                        ins = pool.tensor_tensor(acc, acc, ml["ada_t"][:, k % 2], ALU.add)
                    ins.then_inc(ada_acc_s, 1)
                if j + 2 < j0 + HALF_ADA:
                    fetch(j + 2)

        def ada_pe(pe, half):
            pe.wait_ge(ada_acc_s, KT * HALF_ADA * (half + 1))
            for j in range(2 * HALF_ADA):
                last = pe.matmul(ps[:, 3, j:j + 1], ml["ada_acc"][:, j // 2, (j % 2) * P:(j % 2) * P + P], ones[:, 0:1], start=True, stop=True)
            last.then_inc(ada_sum, 1)

        def ada_dve(dve, half):
            dve.wait_ge(ada_sum, half + 1)
            n = 2 * HALF_ADA
            link(dve, dve.tensor_tensor(modT[:, n * half:n * half + n], ps[:, 3, 0:n], pc("b_ada", n * half, n), ALU.add))
            for i, (at, one) in enumerate(((8, 1.0), (16, 0.0))):
                last = dve.scalar_tensor_tensor(out=gain2[:, 2 * half + i, :], in0=modT[:, n * half + at:n * half + at + 8], scalar=one,
                                                in1=pc("norm_g", 8 * (2 * half + i), 8), op0=ALU.add, op1=ALU.mult)
            last.then_inc(mod_set, 1)
            dve.wait_ge(mod_set, half + 1)

        X = Attention("x", 12, True, False, mx["x_nmax"], mx["x_sum"], mx["x_rinv"], mx["x_ph"], mx["x_pl"], mx["x_th"], mx["x_tl"])
        x_raw, x_aux, x_rot, x_chi, x_ready, x_hi, x_ev = map(sem, ("x_raw", "x_aux", "x_rot_s", "x_c_hi", "x_c_ready", "x_hi_ev", "x_ev"))
        i_S, i_relu, i_acc, f_raw, f_soft, f_row, f_pe, f_neg, bias_in, sel_in = map(sem, (
            "i_scores", "i_relu", "i_acc", "f_raw", "f_soft", "f_row", "f_pe", "f_neg", "bias_in", "sel_in"))
        SCORES = [(qt, h) for qt in range(1, TT) for h in range(4)]
        X_PAIR = {7: 3, 9: 0, 8: 1}
        TURNS = [(3, 1)] * 8 + [(3, 2)] * 8 + [(1, 2)] * 8
        CUM = trow[0:4, 3]
        F_LOG = rstd[0:4, :]
        mask_of = lambda qt: mx["x_mask"][:, (0, 2 * P, 5 * P)[qt - 1]:][:, 0:(qt + 1) * P]

        def x_operands(head):
            t = (head % 4) // 2
            if head >= 8:
                return mx["c_qh"][:, t], mx["c_ql"][:, t], mx["c_kh"][:, 0], mx["c_kl"][:, 0]
            return mx["b_qh"][:, t], mx["b_ql"][:, t], mx["b_kh"][:, t], mx["b_kl"][:, t]

        def x_values(head, c):
            if head >= 8:
                return mx["c_vh"][:, c], mx["c_vl"][:, c]
            w = slice(P * ((head % 4) // 2), P * ((head % 4) // 2) + P)
            return mx["b_vh"][:, c, w], mx["b_vl"][:, c, w]

        def x_dst(head):
            t = (head % 4) // 2 + 2 * (head // 4)
            return mx["x_yhi"][:, t], mx["x_ylo"][:, t]

        def mix_pe(pe, b0):
            def rotate(a):
                pe.wait_ge(x_raw, a + 1)
                if a >= 1:
                    pe.wait_ge(x_rot, a)
                for i in range(2):
                    last = pe.matmul(ps[:, 4 + i, :], mat(ROT_B), mx["x_g"][:, i * S:(i + 1) * S], start=True, stop=True)
                last.then_inc(x_aux, 1)

            def blk(j):
                b, pair = b0 + j, X_PAIR.get(j, j % 2)
                if 2 <= j < 5:
                    pe.wait_ge(x_raw, j - 1)
                elif j == 7:
                    pe.wait_ge(X.top, 4 * TT)
                elif j == 9:
                    pe.wait_ge(X.ol, 4)
                elif j >= 5:
                    pe.wait_ge(x_ev, j - 4)
                if j == 3:
                    pe_token_block(pe, b, b % 2, 1, width=136, count=False)
                    for k in range(KT):
                        last = three(pe, ps[:, 6, :], wtile(b % 2, k * 256 + P), (h_hi[:, k, :], h_lo[:, k, :]), k == 0, k == KT - 1)
                    last.then_inc(block_done, 1)
                elif j in (6, 9):
                    pe_token_block(pe, b, b % 2, pair)
                else:
                    pe_block(pe, b, b % 2, HH, pair, rows=40 if j == 0 else None)

            def negatives():
                pe.wait_ge(sel_in, 16)
                pe.wait_ge(f_row, 1)
                for h in range(4):
                    pe.matmul(ps[:, 4 + h, :], con[0:4, RESET + h * P:RESET + (h + 1) * P], CUM, start=True, stop=True).then_inc(f_pe, 1)

            blk(0)
            blk(1)
            rotate(0)
            blk(2)
            rotate(1)
            blk(3)
            rotate(2)
            pe.wait_ge(x_rot, 3)
            pe.wait_ge(f_raw, 1)
            for i, (qt, h) in enumerate(SCORES):
                if i >= 4:
                    pe.wait_ge(i_relu, i - 3)
                r = slice(64 * (h % 2), 64 * (h % 2) + 64)
                pe.matmul(ps[:, 4 + i % 4, 0:(qt + 1) * P], mx["x_qi"][r, h // 2, qt * P:(qt + 1) * P], mx["x_ki"][r, 0, 0:(qt + 1) * P],
                          start=True, stop=True).then_inc(i_S, 1)
            blk(4)
            blk(5)
            pe.wait_ge(i_relu, len(SCORES))
            pe_attend(pe, X, 0, 4 * TT, x_operands, x_values, first=lambda: pe.wait_ge(x_ev, 3), second=lambda: blk(6),
                      third=lambda: pe.wait_ge(x_ev, 4), fill=lambda: blk(7))
            pe.wait_ge(X.ol, 4)
            pe.wait_ge(x_ev, 5)
            negatives()
            blk(8)
            pe.wait_ge(x_ready, 2)
            pe.wait_ge(f_neg, 4)
            pe_attend(pe, X, 4 * TT, 12 * TT, x_operands, x_values, first=lambda: pe.wait_ge(x_ev, 6), second=lambda: blk(9),
                      third=lambda: pe.wait_ge(x_ev, 7))

        def mix_act(act, b0):
            def tokens(i, n0, n1):
                return pair_(i).rearrange("p a (b n) -> p (a b) n", n=256)[:, :, n0:n1]

            def take(j):
                b = b0 + j
                act.wait_ge(block_done, b + 1)
                if j < 3:
                    if j >= 1:
                        act.wait_ge(x_rot, j)
                    act.activation(two(mx["x_g"][:]), pair_(X_PAIR.get(j, j % 2)), ACT.Copy).then_inc(x_raw, 1)
                elif j == 3:
                    act.activation(mx["c_vh"][:], tokens(1, 0, P), ACT.Copy)
                    act.activation(mx["c_wi"][:], tokens(1, 132, 136), ACT.Copy, scale=0.5).then_inc(x_hi, 1)
                    act.activation(F_LOG, ps[0:4, 6, :], ACT.Identity, bias=pc("b_forget")[0:4]).then_inc(f_raw, 1)
                    act.wait_ge(f_raw, 1)
                    alink(act, act.activation(CUM, F_LOG, ACT.Abs))
                    alink(act, act.activation(CUM, CUM, ACT.Exp, scale=-1.0))
                    act.activation(CUM, CUM, ACT.Ln, bias=1.0).then_inc(f_soft, 1)
                elif j in (6, 9):
                    act.activation(mx["b_vh"][:], tokens(X_PAIR.get(j, j % 2), 0, 256), ACT.Copy).then_inc(x_hi, 1)
                else:
                    if j == 4:
                        act.wait_ge(x_ready, 2)
                    act.activation(mx["b_kh" if j in (4, 7) else "b_qh"][:], pair_(X_PAIR.get(j, j % 2)), ACT.Copy).then_inc(x_hi, 1)
                if j not in (6, 9):
                    next_hi(act, b + 2, b % 2)
                if j in (1, 3):
                    a = 0 if j == 1 else 2
                    act.wait_ge(x_rot, a + 1)
                    act.activation(mx["c_kh"][:] if a == 0 else mx["c_qh"][:],
                                   two(mx["x_rot"][:])[:, 0:1 if a == 0 else 2, :], ACT.Copy).then_inc(x_chi, 1)
                if j == 3:
                    for i, (qt, h) in enumerate(SCORES):
                        act.wait_ge(i_S, i + 1)
                        if i >= 3:
                            act.wait_ge(i_acc, i - 2)
                        n = (qt + 1) * P
                        act.activation(trow[:, i % 3, 0:n], ps[:, 4 + i % 4, 0:n], ACT.Relu, scale=HD ** -0.5).then_inc(i_relu, 1)
                if j == 7:
                    for h in range(4):
                        act.wait_ge(f_pe, h + 1)
                        act.activation(mx["x_neg"][:, h, :], ps[:, 4 + h, :], ACT.Copy, scale=-1.0).then_inc(f_neg, 1)
            def beside(u0, j):
                def work(s):
                    if s == u0 + 1:
                        take(j)
                    if s == u0 + 3:
                        next_hi(act, b0 + j + 2, (b0 + j) % 2)
                return work

            source = lambda u: p_s[:, u % 3, 0:X.tiles(u) * P]
            for j in range(6):
                take(j)
            act_attend(act, X, 0, 4 * TT, source, x_dst, beside(0, 6))
            take(7)
            take(8)
            act_attend(act, X, 4 * TT, 12 * TT, source, x_dst, beside(4 * TT, 9))

        def mix_dve(dve, b0):
            def tokens(i, n0, n1):
                return pair_(i).rearrange("p a (b n) -> p (a b) n", n=256)[:, :, n0:n1]

            def rope(a):
                dve.wait_ge(x_aux, a + 1)
                if a == 0:
                    dve.wait_ge(rope2_in, 32)
                if a == 2:
                    dve.wait_ge(x_ready, 1)
                for i in range(2):
                    g = mx["x_g"][:, i * S:(i + 1) * S]
                    dve.tensor_tensor(g, g, mx["x_cos"][:], ALU.mult)
                    ins = dve.tensor_tensor(mx["x_rot"][:, i * S:(i + 1) * S], ps[:, 4 + i, :], mx["x_sin"][:], ALU.mult)
                link(dve, ins)
                dst = mx["x_qi"][:] if a == 1 else two(mx["x_rot"][:])
                dve.tensor_tensor(dst, two(mx["x_rot"][:]), two(mx["x_g"][:]), ALU.add).then_inc(x_rot, 1)
                dve.wait_ge(x_rot, a + 1)
                if a != 1:
                    if a == 0:
                        link(dve, dve.tensor_copy(mx["x_ki"][:, 0, :], mx["x_rot"][:, S:2 * S]))
                    dve.wait_ge(x_chi, 1 if a == 0 else 2)
                    hi, lo, n = (mx["c_kh"], mx["c_kl"], 1) if a == 0 else (mx["c_qh"], mx["c_ql"], 2)
                    dve.tensor_tensor(lo[:], two(mx["x_rot"][:])[:, 0:n, :], hi[:].bitcast(F32), ALU.subtract).then_inc(x_ready, 1)
                    dve.wait_ge(x_ready, 1 if a == 0 else 2)

            def index_scores():
                for i, (qt, h) in enumerate(SCORES):
                    n = (qt + 1) * P
                    sc = mask_of(qt)
                    w = mx["c_wi"][:, qt, h:h + 1]
                    dve.wait_ge(i_relu, i + 1)
                    if h == 0:
                        dve.tensor_scalar(sc, trow[:, i % 3, 0:n], w, None, ALU.mult).then_inc(i_acc, 1)
                    else:
                        dve.scalar_tensor_tensor(out=sc, in0=trow[:, i % 3, 0:n], scalar=w, in1=sc, op0=ALU.mult, op1=ALU.add).then_inc(i_acc, 1)
                    dve.wait_ge(i_acc, i + 1)
                    if h == 3:
                        link(dve, dve.tensor_tensor(sc[:, n - P:n], sc[:, n - P:n], mat(ADMIT), ALU.add))

            def top_k(r0, r1):
                for r in range(r0, r1):
                    at = [0, 0]
                    for i, qt in enumerate(TURNS[r]):
                        dve.max(mx["x_m8"][:, 8 * i:8 * i + 8], mask_of(qt)).then_inc(chain, 1)
                        links["d"] += 1
                        at[i] = links["d"]
                    for i, qt in enumerate(TURNS[r]):
                        dve.wait_ge(chain, at[i])
                        dve.match_replace(mask_of(qt), mx["x_m8"][:, 8 * i:8 * i + 8], mask_of(qt), TAKEN).then_inc(chain, 1)
                        links["d"] += 1
                    dve.wait_ge(chain, links["d"])
                    for qt in TURNS[r]:
                        if sum(turn.count(qt) for turn in TURNS[:r + 1]) == TOPK // 8:
                            link(dve, dve.tensor_scalar(mask_of(qt), mask_of(qt), TAKEN, NEG, ALU.not_equal, ALU.mult))

            def top(u):
                head, qt = divmod(u, TT)
                h, n = head % 4, X.tiles(u) * P
                s_, sc = ps[:, 6 + u % 2, 0:n], p_s[:, u % 3, 0:n]
                dve.wait_ge(X.S, u + 1)
                if u >= 3:
                    dve.wait_ge(X.lo, u - 2)
                scaled = lambda lo, hi, add: dve.scalar_tensor_tensor(out=sc[:, lo:hi], in0=s_[:, lo:hi], scalar=HD ** -0.5, in1=add,
                                                                      op0=ALU.mult, op1=ALU.add)
                if head >= 8:
                    ins = scaled(0, n, mat(ADMIT) if qt == 0 else mask_of(qt))
                elif head < 4:
                    if qt == 0:
                        ins = scaled(0, n, mx["x_bias"][:, h, P:2 * P])
                    else:
                        ins = scaled(n - 2 * P, n, mx["x_bias"][:, h, :])
                        if n > 2 * P:
                            ins = dve.tensor_scalar(sc[:, 0:n - 2 * P], s_[:, 0:n - 2 * P], HD ** -0.5, pc("rel_far", h), ALU.mult, ALU.add)
                else:
                    link(dve, scaled(0, n, mx["x_neg"][:, h, 0:n]))
                    ins = dve.tensor_tensor(sc[:, n - P:n], sc[:, n - P:n], mat(CAUSAL), ALU.add)
                link(dve, ins)
                dve.tensor_reduce(X.nmax[:, u:u + 1], sc, AX, ALU.max, negate=True).then_inc(X.top, 1)

            def take(j):
                b = b0 + j
                if j < 3:
                    pass
                elif j == 3:
                    dve.wait_ge(x_hi, 1)
                    dve.tensor_tensor(mx["c_vl"][:], tokens(1, 0, P), mx["c_vh"][:].bitcast(F32), ALU.subtract).then_inc(x_ev, 1)
                else:
                    dve.wait_ge(x_hi, j - 2)
                    if j in (6, 9):
                        dve.tensor_tensor(mx["b_vl"][:], tokens(X_PAIR.get(j, j % 2), 0, 256), mx["b_vh"][:].bitcast(F32), ALU.subtract).then_inc(x_ev, 1)
                    else:
                        k = "b_k" if j in (4, 7) else "b_q"
                        dve.tensor_tensor(mx[k + "l"][:], pair_(X_PAIR.get(j, j % 2)), mx[k + "h"][:].bitcast(F32), ALU.subtract).then_inc(x_ev, 1)
                if j in (1, 2, 3):
                    rope(j - 1)
                if j not in (6, 9):
                    next_lo(dve, b + 2, b % 2)
                if j == 3:
                    dve.wait_ge(f_soft, 1)
                    f = F_LOG
                    link(dve, dve.scalar_tensor_tensor(out=f, in0=f, scalar=0.0, in1=CUM, op0=ALU.min, op1=ALU.subtract))
                    for t in range(TT):
                        w = slice(t * P, (t + 1) * P)
                        ins = dve.tensor_tensor_scan(CUM[:, w], ones[0:4, :], f[:, w], 0.0 if t == 0 else CUM[:, t * P - 1:t * P], ALU.mult, ALU.add)
                        if t < TT - 1:
                            link(dve, ins)
                    ins.then_inc(f_row, 1)
                    index_scores()
                if j in ROUNDS:
                    top_k(*ROUNDS[j])
            ROUNDS = {3: (0, 4), 4: (4, 7), 5: (7, 10), 7: (14, 17), 8: (17, 19)}
            BESIDE = {4 * TT + i: (10 + i, 11 + i) for i in range(4)}
            BESIDE_B = {4 * TT + 5 + 2 * i: (19 + i, 20 + i) for i in range(5)}

            def beside(u0, j, turns):
                def work(s):
                    if s == u0 + 1:
                        take(j)
                    if s == u0 + 3:
                        next_lo(dve, b0 + j + 2, (b0 + j) % 2)
                    if s in turns:
                        top_k(*turns[s])
                return work

            for j in range(6):
                take(j)
            dve.wait_ge(bias_in, 16)
            for h in range(4):
                ins = dve.tensor_tensor(mx["x_bias"][:, h, P:2 * P], mx["x_bias"][:, h, P:2 * P], mat(ADMIT), ALU.add)
            link(dve, ins)
            dve_attend(dve, X, 0, 4 * TT, top, x_dst, beside(0, 6, BESIDE))
            take(7)
            take(8)
            dve_attend(dve, X, 4 * TT, 12 * TT, top, x_dst, beside(4 * TT, 9, BESIDE_B))

        t_sig, t_use, t_sum, t_hi, t_lo = map(sem, ("t_gate", "t_used", "t_merged", "t_hi", "t_lo"))

        def merge_pe(pe, b0):
            pe.wait_ge(X.ol, 12)
            for p in range(4):
                for br in range(3):
                    b, i = b0 + 4 * p + br, 6 * p + br
                    if i >= 2:
                        if br < 2:
                            pe.wait_ge(t_use, 3 * p - 1 + br)
                        else:
                            pe.wait_ge(t_sig, 3 * p + 1)
                    pe_block(pe, b, b % 2, HH, i % 2)
                b = b0 + 4 * p + 3
                pe.wait_ge(split_done, b + 1)
                for br in range(3):
                    i = 6 * p + 3 + br
                    if br < 2:
                        pe.wait_ge(t_sig, 3 * p + 2 + br)
                    else:
                        pe.wait_ge(t_use, 3 * p + 1)
                    for k in range(2):
                        for n in range(2):
                            last = three(pe, ps[:, 2 * (i % 2) + n, :], wtile(b % 2, (2 * br + k) * 256 + n * P),
                                         (mx["x_yhi"][:, 2 * br + k, :], mx["x_ylo"][:, 2 * br + k, :]), k == 0, k == 1)
                    last.then_inc(t_br if br < 2 else block_done, 1)
        t_br = sem("t_branch")

        def merge_act(act, b0):
            for p in range(4):
                for br in range(3):
                    b = b0 + 4 * p + br
                    act.wait_ge(block_done, b + 1)
                    if p >= 1:
                        act.wait_ge(t_sum, p)
                    for n in range(2):
                        ins = act.activation(mx["x_gate"][:, br, n * S:(n + 1) * S], ps[:, 2 * (br % 2) + n, :], ACT.Sigmoid,
                                             bias=pc("b_gate", 8 * br + 2 * p + n))
                    ins.then_inc(t_sig, 1)
                    next_hi(act, b + 2, b % 2)
                act.wait_ge(t_sum, p + 1)
                act.activation(mx["x_mhi"][:, 2 * p:2 * p + 2, :], two(mx["x_m"][:, p % 2]), ACT.Copy).then_inc(t_hi, 1)
                next_hi(act, b0 + 4 * p + 5, (b0 + 1) % 2)

        def merge_dve(dve, b0):
            for p in range(4):
                for br in range(3):
                    next_lo(dve, b0 + 4 * p + br + 2, (b0 + br) % 2)
                m = mx["x_m"][:, p % 2]
                for br in range(3):
                    if br < 2:
                        dve.wait_ge(t_br, 2 * p + br + 1)
                    else:
                        dve.wait_ge(block_done, b0 + 4 * p + 4)
                    dve.wait_ge(t_sig, 3 * p + br + 1)
                    if br == 0 and p >= 2:
                        dve.wait_ge(t_lo, p - 1)
                        dve.wait_ge(t_hi, p - 1)
                    g = mx["x_gate"][:, br]
                    out = m if br == 0 else g
                    dve.tensor_tensor(two(out), two(g), pair_((br + 1) % 2), ALU.mult).then_inc(t_use, 1)
                    dve.wait_ge(t_use, 3 * p + br + 1)
                    if br >= 1:
                        ins = dve.tensor_tensor(m, m, g, ALU.add)
                        if br == 1:
                            link(dve, ins)
                ins.then_inc(t_sum, 1)
                dve.wait_ge(t_hi, p + 1)
                dve.tensor_tensor(mx["x_mlo"][:, 2 * p:2 * p + 2, :], two(m), mx["x_mhi"][:, 2 * p:2 * p + 2, :].bitcast(F32),
                                  ALU.subtract).then_inc(t_lo, 1)
                next_lo(dve, b0 + 4 * p + 5, (b0 + 1) % 2)

        f_pr, f_ce, f_t1, f_conv, f_ge, f_gm, f_hs, f_ls, f_out, f_add, y_zero = map(sem, (
            "f_params", "f_current", "f_tap1", "f_conv", "f_gelu", "f_gated", "f_h_hi", "f_h_lo", "f_out", "f_added", "y_zero"))

        def ffn_up(pe, u, b, slot, rows=None):
            for which, pair in ((0, 0), (1, 1)):
                if not (isinstance(u, int) and u == 0):
                    pe.wait_ge((f_conv, f_gm)[which], u)
                pe_block(pe, b + which, (slot + which) % 2, HH, pair, rows=rows if which == 0 else None)

        def ffn_down(pe, u, b, slot, after=None):
            pe.wait_ge(f_ls, u + 1)
            pe.wait_ge(split_done, b + 1)
            for q in range(4):
                if not (isinstance(u, int) and u == 0 and q < 2):
                    pe.wait_ge(f_add, u * 4 + (q - 1))
                for k in range(2):
                    for n in range(2):
                        last = three(pe, ps[:, 4 + 2 * (q % 2) + n, :], wtile(slot, k * 1024 + (2 * q + n) * P),
                                     (ff["f_hi"][:, f_par(u), k, :], ff["f_lo"][:, f_par(u), k, :]), k == 0, k == 1)
                last.then_inc(f_out if q < 3 else block_done, 1)
                if after is not None:
                    after(q)

        par_now = [0]

        def f_par(u):
            return u % 2 if isinstance(u, int) else par_now[0]

        LOOPED = FFN_UNITS - 3

        def ffn_pe(pe, b0, n):
            ffn_up(pe, 0, b0, b0 % 2, rows=56)

            def unit(u, b, d):
                ffn_up(pe, u, b, (b0 + 3 * d - 1) % 2)
                par_now[0] = (d - 1) % 2
                ffn_down(pe, u - 1, b + 2, (b0 + 3 * d + 1) % 2)

            unit(1, b0 + 2, 1)
            with pe.Fori(0, LOOPED // 2) as it:
                for d in (2, 3):
                    unit(it * 2 + d, it * 6 + (b0 + 3 * d - 1), d)
            unit(FFN_UNITS - 1, b0 + 3 * FFN_UNITS - 4, FFN_UNITS - 1)
            ffn_down(pe, FFN_UNITS - 1, b0 + 3 * FFN_UNITS - 1, (b0 + 3 * FFN_UNITS - 1) % 2,
                     after=lambda q: pe_ssq(pe, n, q - 2, 2) if q >= 2 else None)
            pe_ssq(pe, n, 2, 2)
            pe_ssq(pe, n, 3, 2)

        def ffn_act(act, b0, n):
            def unit(u, b, d, first=False, last=False):
                slot = (b0 if first else b0 + 3 * d - 1) % 2
                p_ = d % 2
                act.wait_ge(block_done, b + 1)
                act.wait_ge(f_pr, u + 1)
                if not (isinstance(u, int) and u < 2):
                    act.wait_ge(f_gm, u - 1)
                for i in range(2):
                    ins = act.activation(ff["f_c"][:, p_, i * S:(i + 1) * S], ps[:, i, :], ACT.Identity,
                                         bias=ff["f_prm"][:, p_, 4 * i + 3:4 * i + 4], scale=ff["f_prm"][:, p_, 4 * i + 2:4 * i + 3])
                ins.then_inc(f_ce, 1)
                split_hi(act, b + 2, slot)
                act.wait_ge(f_conv, u + 1)
                act.activation(ff["f_c"][:, p_], ff["f_c"][:, p_], ACT.Gelu_apprx_tanh).then_inc(f_ge, 1)
                split_hi(act, b + 3, 1 - slot)
                act.wait_ge(f_gm, u + 1)
                act.activation(ff["f_hi"][:, p_], two(ff["f_r"][:, p_]), ACT.Copy).then_inc(f_hs, 1)
                if not first and not last:
                    split_hi(act, b + 4, slot)

            unit(0, b0, 0, first=True)
            unit(1, b0 + 2, 1)
            with act.Fori(0, LOOPED // 2) as it:
                for d in (2, 3):
                    unit(it * 2 + d, it * 6 + (b0 + 3 * d - 1), d)
            u = FFN_UNITS - 1
            unit(u, b0 + 3 * u - 1, u, last=True)
            for q in range(4):
                act.wait_ge(f_add, 4 * u + q + 1)
                act_square(act, n, q, y)

        def ffn_dve(dve, b0):
            def params(u, d):
                at = PRM["conv"]
                src = prm[:, at + 8 * u:at + 8 * u + 8] if isinstance(u, int) else prm[:, bass.ds(u * 8 + at, 8)]
                dve.tensor_scalar(ff["f_prm"][:, d % 2, :], src, 1.0, None, ALU.mult).then_inc(f_pr, 1)

            def add(u, q, b):
                if q < 3:
                    dve.wait_ge(f_out, u * 3 + (q + 1))
                else:
                    dve.wait_ge(block_done, b + 1)
                if not (isinstance(u, int) and u == 0):
                    dve.wait_ge(f_add, u * 4 + (q - 3))
                yd = y[:, 2 * q:2 * q + 2, :]
                dve.tensor_tensor(yd, yd, pair_(2 + q % 2), ALU.add).then_inc(f_add, 1)

            def unit(u, b, d, first=False, last=False):
                slot = (b0 if first else b0 + 3 * d - 1) % 2
                p_ = d % 2
                dve.wait_ge(f_ce, u + 1)
                for tap, shift, s_ in ((1, 1, f_t1), (0, 2, f_conv)):
                    for i in range(2):
                        c = ff["f_c"][:, p_, i * S + shift:(i + 1) * S]
                        ins = dve.scalar_tensor_tensor(out=c, in0=ps[:, i, 0:S - shift], scalar=ff["f_prm"][:, p_, 4 * i + tap:4 * i + tap + 1],
                                                       in1=c, op0=ALU.mult, op1=ALU.add)
                    ins.then_inc(s_, 1)
                    dve.wait_ge(s_, u + 1)
                if not last:
                    params(u + 1, d + 1)
                    dve.wait_ge(f_pr, u + 2)
                split_lo(dve, b + 2, slot)
                dve.wait_ge(block_done, b + 2)
                dve.wait_ge(f_ge, u + 1)
                if not (isinstance(u, int) and u < 2):
                    dve.wait_ge(f_ls, u - 1)
                dve.tensor_tensor(two(ff["f_r"][:, p_]), two(ff["f_c"][:, p_]), pair_(1), ALU.mult).then_inc(f_gm, 1)
                if not first:
                    add(u - 1, 0, b + 2)
                split_lo(dve, b + 3, 1 - slot)
                if not first:
                    add(u - 1, 1, b + 2)
                dve.wait_ge(f_hs, u + 1)
                dve.wait_ge(f_gm, u + 1)
                dve.tensor_tensor(ff["f_lo"][:, p_], two(ff["f_r"][:, p_]), ff["f_hi"][:, p_].bitcast(F32), ALU.subtract).then_inc(f_ls, 1)
                if not first:
                    add(u - 1, 2, b + 2)
                    add(u - 1, 3, b + 2)
                    if not last:
                        split_lo(dve, b + 4, slot)

            params(0, 0)
            dve.wait_ge(f_pr, 1)
            dve.memset(y[:], 0.0).then_inc(y_zero, 1)
            dve.wait_ge(y_zero, 1)
            unit(0, b0, 0, first=True)
            unit(1, b0 + 2, 1)
            with dve.Fori(0, LOOPED // 2) as it:
                for d in (2, 3):
                    unit(it * 2 + d, it * 6 + (b0 + 3 * d - 1), d)
            u = FFN_UNITS - 1
            unit(u, b0 + 3 * u - 1, u, last=True)
            for q in range(4):
                add(u, q, b0 + 3 * u + 2)

        def renorm_squares(act, n, src):
            for j in range(4):
                act.wait_ge(n_app, 8 * (n - 1) + 2 * j + 2)
                act_square(act, n, j, src)

        def pe_sums(pe, n, bank):
            for j in range(4):
                pe_ssq(pe, n, j, bank)

        env = dict(locals())
        block = ctx.enter_context(nc.Block())
        program(nc, block, env)


def program(nc, block, e):
    x, out_d = e["x"], e["out_d"]
    gain = lambda name, i: e["prm"][:, PRM[name] + 8 * i:PRM[name] + 8 * i + 8]
    shift = lambda i: e["modT"][:, 24 * i:24 * i + 8]

    @block.sync
    def _(sp):
        xt = e["xT_d"].rearrange("(k p) s -> p k s", p=P)
        sp.dma_start(e["prm"][:], e["prm_d"]).then_inc(e["prm_in"], 16)
        for c in range(4):
            sp.dma_start(x[:, 2 * c:2 * c + 2, :], xt[:, 2 * c:2 * c + 2, :]).then_inc(e["x_in"][c], 16)
        for b in range(2):
            sp.dma_start(e["w_raw"][:, b], e["wb_d"][b]).then_inc(e["w_in"][b], 16)
        sp.dma_start(e["con"][:], e["con_d"]).then_inc(e["con_in"], 16)
        sp.dma_start(e["at_"]["a_cos"][:], e["rope_d"][0]).then_inc(e["rope_in"], 16)
        sp.dma_start(e["at_"]["a_sin"][:], e["rope_d"][1]).then_inc(e["rope_in"], 16)

        def load(b, slot):
            sp.wait_ge(e["split_done"], b - 1)
            sp.dma_start(e["w_raw"][:, slot], e["wb_d"][b]).then_inc(e["w_in"][slot], 16)

        def loads(b0, b1):
            with sp.Fori(0, (b1 - b0) // 2) as it:
                load(it * 2 + b0, b0 % 2)
                load(it * 2 + (b0 + 1), (b0 + 1) % 2)
            if (b1 - b0) % 2:
                load(b1 - 1, (b1 - 1) % 2)
        loads(2, B_MLP0 + 2)
        loads(B_MLP0 + 2, B_GLA + 2)
        sp.wait_ge(e["m_add"], 4 * MLP_UNITS)
        sp.wait_ge(e["ada_sum"], 1)
        sp.dma_start(e["gl"]["g_up"][:], e["gup_d"]).then_inc(e["gup_in"], 16)
        loads(B_GLA + 2, B_MLP1 + 2)
        loads(B_MLP1 + 2, B_MIX + 2)
        sp.wait_ge(e["n_app"], 40)
        sp.dma_start(e["mx"]["x_cos"][:], e["rope_d"][2]).then_inc(e["rope2_in"], 16)
        sp.dma_start(e["mx"]["x_sin"][:], e["rope_d"][3]).then_inc(e["rope2_in"], 16)
        sp.dma_start(e["mx"]["x_bias"][:], e["rel_d"]).then_inc(e["bias_in"], 16)
        sp.dma_start(e["con"][0:4, RESET:RESET + 4 * P], e["sel_d"]).then_inc(e["sel_in"], 16)
        loads(B_MIX + 2, B_FFN + 2)
        loads(B_FFN + 2, N_BLOCKS)
        od = out_d.rearrange("(k p) s -> p k s", p=P)
        for j in range(4):
            sp.wait_ge(e["n_app"], 8 * 8 + 2 * j + 2)
            sp.dma_start(od[:, 2 * j:2 * j + 2, :], x[:, 2 * j:2 * j + 2, :]).then_inc(e["out_st"], 16)
        sp.wait_ge(e["out_st"], 64)

    @block.gpsimd
    def _(pool):
        pool.memset(e["ones"][:], 1.0).then_inc(e["ones_set"], 1)
        pool.wait_ge(e["A1"].ol, 16)
        e["ada_pool"](pool, 0)
        e["gla_pool"](pool)
        pool.wait_ge(e["g_ol"], 8)
        e["ada_pool"](pool, 1)

    @block.scalar
    def _(act):
        act.wait_ge(e["prm_in"], 16)
        act.activation(e["cact"][:], e["pc"]("c", 0, 8), ACT.Silu).then_inc(e["c_set"], 1)
        act.preload_act_table_set("natural_log_exp_and_others")
        for j in range(4):
            act.wait_ge(e["x_in"][j], 16)
            e["act_square"](act, 0, j, x)
        e["split_hi"](act, 0, 0)
        e["act_norm_h"](act, 0, 0, 2)
        e["split_hi"](act, 1, 1)
        e["attn_act"](act)
        e["act_proj"](act, 0, B_WO0, 1, x, 6)
        e["act_norm_h"](act, 1, 1, 6)
        e["mlp_act"](act, 0, B_MLP0, 2)
        act.preload_act_table_set("natural_log_exp_and_others")
        e["act_norm_h"](act, 2, 2, 2)
        e["gla_act"](act, B_GLA)
        e["act_proj"](act, 1, B_WO1, 3, x, 6)
        e["act_norm_h"](act, 3, 3, 6)
        e["mlp_act"](act, 1, B_MLP1, 4)
        act.preload_act_table_set("natural_log_exp_and_others")
        e["act_std"](act, 4, 2)
        e["renorm_squares"](act, 5, x)
        e["act_norm_h"](act, 5, 4, 2, shift(0))
        e["mix_act"](act, B_MIX)
        e["merge_act"](act, B_GATE)
        e["act_proj"](act, 2, B_WOUT, 6, e["y"], 6)
        act.preload_act_table_set("natural_log_exp_and_others")
        e["act_std"](act, 6, 6)
        e["renorm_squares"](act, 7, x)
        e["act_norm_h"](act, 7, 5, 2, shift(1))
        e["ffn_act"](act, B_FFN, 8)
        e["act_std"](act, 8, 2)

    @block.vector
    def _(dve):
        e["split_lo"](dve, 0, 0)
        for j in range(4):
            dve.wait_ge(e["x_in"][j], 16)
        e["dve_norm_h"](dve, 0, 0, gain("norm_mix", 0))
        e["split_lo"](dve, 1, 1)
        dve.wait_ge(e["con_in"], 16)
        dve.tensor_copy(e["identr"][:], e["mat"](IDENT)).then_inc(e["ident_set"], 1)
        e["attn_dve"](dve)
        e["dve_proj"](dve, 0, B_WO0, x, True)
        e["dve_norm_h"](dve, 1, 1, gain("norm_mlp", 0))
        e["mlp_dve"](dve, 0, B_MLP0)
        e["dve_norm_h"](dve, 2, 2, gain("norm_mix", 1))
        e["ada_dve"](dve, 0)
        e["gla_dve"](dve, B_GLA)
        e["dve_proj"](dve, 1, B_WO1, x, True)
        e["dve_norm_h"](dve, 3, 3, gain("norm_mlp", 1))
        e["mlp_dve"](dve, 1, B_MLP1)
        e["dve_norm_x"](dve, 4, gain("final", 0))
        e["ada_dve"](dve, 1)
        e["dve_norm_h"](dve, 5, 4, e["gain2"][:, 0], shift(0))
        e["mix_dve"](dve, B_MIX)
        e["merge_dve"](dve, B_GATE)
        e["dve_proj"](dve, 2, B_WOUT, e["y"], False)
        e["dve_norm_add"](dve, 6, e["gain2"][:, 1])
        e["dve_norm_h"](dve, 7, 5, e["gain2"][:, 2], shift(1))
        e["ffn_dve"](dve, B_FFN)
        e["dve_norm_add"](dve, 8, e["gain2"][:, 3])

    @block.tensor
    def _(pe):
        pe.wait_ge(e["ones_set"], 1)
        e["pe_sums"](pe, 0, 2)
        e["attn_pe"](pe)
        e["pe_proj"](pe, 0, B_WO0, e["HH"], 1, 6, lambda k: pe.wait_ge(e["A1"].ol, 2 * k + 2), tiles=(KT - 1,))
        e["mlp_pe"](pe, 0, B_MLP0, 2)
        e["ada_pe"](pe, 0)
        e["gla_pe"](pe, B_GLA, 16)
        e["pe_proj"](pe, 1, B_WO1, e["HH"], 3, 6, lambda k: pe.wait_ge(e["g_ol"], k + 1))
        e["mlp_pe"](pe, 1, B_MLP1, 4)
        e["ada_pe"](pe, 1)
        e["pe_sums"](pe, 5, 2)
        e["mix_pe"](pe, B_MIX)
        e["merge_pe"](pe, B_GATE)
        pe.wait_ge(e["t_use"], 12)
        e["pe_proj"](pe, 2, B_WOUT, (e["mx"]["x_mhi"], e["mx"]["x_mlo"]), 6, 6, lambda k: pe.wait_ge(e["t_lo"], k // 2 + 1))
        e["pe_sums"](pe, 7, 2)
        e["ffn_pe"](pe, B_FFN, 8)


def pack_block(w):
    return w.reshape(KT, P, 256).transpose(1, 0, 2).reshape(P, 2048)


def pack_wide(w):
    return w.reshape(2, P, 1024).transpose(1, 0, 2).reshape(P, 2048)


def columns(v):
    return v.reshape(-1, P).T


def zeros(*shape):
    return np.zeros(shape, np.float32)


def weight_blocks(i):
    out = []
    cols = lambda w, order=None: [pack_block(w[:, 256 * j:256 * j + 256]) for j in range(w.shape[1] // 256)]
    w = i["attn_w_qkv"][0]
    heads = [8 * (t // 4) + 4 * par + t % 4 for t in range(8) for par in range(2)]
    wq = np.concatenate([w[:, 64 * h:64 * h + 64] for h in heads], 1)
    out += [pack_block(w[:, 1024:1280])] + cols(wq) + [pack_block(w[:, 1280:1536])]
    out += cols(i["attn_w_o"][0].reshape(16, HD, D)[heads].reshape(D, D))

    def mlp(w1, w2):
        a = cols(w1)
        b = [pack_wide(w2[256 * u:256 * u + 256]) for u in range(MLP_UNITS)]
        seq = [a[0]]
        for u in range(1, MLP_UNITS):
            seq += [a[u], b[u - 1]]
        return seq + [b[-1]]

    out += mlp(i["mlp_w_in"][0], i["mlp_w_out"][0])
    w = i["gla_w_in"][0]
    z = np.concatenate([w[:, 3072:3104], zeros(D, 224)], 1)
    out += [pack_block(z)] + cols(w[:, 0:1024]) + cols(w[:, 1024:2048]) + cols(w[:, 2048:3072])
    out += cols(i["gla_w_o"][0])
    out += mlp(i["mlp_w_in"][1], i["mlp_w_out"][1])
    w = i["w_in_2"][0]
    c = lambda a, n=256: w[:, a:a + n]
    small = np.concatenate([c(1860, 64), c(1860, 64), c(1536, 4), c(2244, 4), zeros(D, 120)], 1)
    dup = np.concatenate([c(1796, 64)] * 2 + [c(2180, 64)] * 2, 1)
    out += [pack_block(v) for v in (dup, c(1924), c(1540), small, c(256), c(0), c(512), c(1024), c(768), c(1280))]
    for p in range(4):
        for br in range(3):
            out.append(pack_block(c(2248 + 1024 * br + 256 * p)))
        wbr = np.concatenate([i["w_branch_2"][0, br][:, 256 * p:256 * p + 256] for br in range(3)] + [zeros(256, 256)], 0)
        out.append(pack_block(wbr))
    out += cols(i["w_out_2"][0])
    up = i["w_up_2"][0]
    a, g = cols(up[:, :D_FF2]), cols(up[:, D_FF2:])
    dn = [pack_wide(i["w_down_2"][0][256 * u:256 * u + 256]) for u in range(FFN_UNITS)]
    out += [a[0], g[0]]
    for u in range(1, FFN_UNITS):
        out += [a[u], g[u], dn[u - 1]]
    out.append(dn[-1])
    return np.stack(out)


def small_parameters(i):
    halves = lambda v: np.concatenate([v, v])[:, None]
    pad = lambda v: np.concatenate([v, zeros(P - len(v))])[:, None]
    conv = np.concatenate([i["conv_w_2"][0], i["conv_b_2"]], 0)
    conv = conv.reshape(4, FFN_UNITS, 2, P).transpose(3, 1, 2, 0).reshape(P, -1)
    parts = [columns(i["norm_mix"].reshape(-1)), columns(i["norm_mlp"].reshape(-1)), columns(i["final_norm"]),
             halves(i["attn_q_norm"][0]), halves(i["attn_k_norm"][0]), columns(i["gla_b_gate"].reshape(-1)),
             columns(i["gla_out_norm"].reshape(-1)), columns(i["b_ada_2"].reshape(-1)), columns(i["norm_g_2"].reshape(-1)),
             columns(i["b_gate_2"].reshape(-1)), pad(i["b_forget_2"][0]), conv, columns(i["c_2"].reshape(-1)),
             np.full((P, 1), EPS, np.float32), np.tile(i["rel_table_2"][0, :, -1][None], (P, 1))]
    return np.ascontiguousarray(np.concatenate(parts, 1))


def constants():
    con = zeros(P, N_CON)
    r = np.arange(P)
    con[:, IDENT:IDENT + P] = np.eye(P)
    con[:, HALVES:HALVES + P] = (r[:, None] // 64 == r[None] // 64)
    for at, half in ((ROT_A, 16), (ROT_B, 32)):
        for m in range(P):
            if m % (2 * half) < half:
                con[m + half, at + m] = -1.0
            else:
                con[m - half, at + m] = 1.0
    con[:, CAUSAL:CAUSAL + P] = np.where(r[None] <= r[:, None], 0.0, NEG)
    con[:, ADMIT:ADMIT + P] = np.where(r[None] // CH <= r[:, None] // CH, 0.0, NEG)
    con[:, RESET:RESET + S] = (np.arange(S) % CH != 0)
    return con


def rope_tables():
    f = np.float32
    theta = f(10000.0)
    t, d = np.arange(S), np.arange(P) % 64
    inv = theta ** (-np.arange(0, 32, 2, dtype=f) / f(32))
    pos = np.where((d < 32)[:, None], (t // 64)[None], (t % 64)[None]).astype(f)
    ang = pos * inv[d % 16][:, None]
    inv2 = theta ** (-np.arange(0, 64, 2, dtype=f) / f(64))
    ang2 = t.astype(f)[None] * inv2[d % 32][:, None]
    return np.stack([np.cos(ang), np.sin(ang), np.cos(ang2), np.sin(ang2)]).astype(f)


def kernel(**inputs):
    import concourse.bacc as _bacc
    from concourse.bass_utils import run_bass_kernel_spmd as _launch

    i = {k: np.asarray(v) for k, v in inputs.items()}
    up = zeros(32, 2, S)
    up[0:16, 0] = i["gla_w_gate_up"][0, 0]
    up[16:32, 1] = i["gla_w_gate_up"][0, 1]
    rel = i["rel_table_2"][0]
    rel_rows = np.concatenate([np.repeat(rel[:, 256:], 127, 1), rel[:, 1:][:, ::-1]], 1)
    rel_tile = np.lib.stride_tricks.sliding_window_view(rel_rows, 2 * P, 1)[:, ::-1].transpose(1, 0, 2)
    ada = i["w_ada_2"][0]
    arrays = {
        "xT": np.ascontiguousarray(i["x"][0].T),
        "wb": weight_blocks(i),
        "ada": np.stack([pack_block(ada[:, 256 * j:256 * j + 256]) for j in range(N_ADA)]),
        "prm": small_parameters(i), "con": constants(), "rope": rope_tables(), "gup": up,
        "rel": np.ascontiguousarray(rel_tile),
        "sel": np.repeat(np.eye(4, dtype=np.float32), P, 1),
    }
    nc = _bacc.Bacc("TRN2", target_bir_lowering=False, num_devices=1)
    args = [nc.dram_tensor("in_" + k, v.shape, mybir.dt.from_np(v.dtype), kind="ExternalInput").ap() for k, v in arrays.items()]
    out = nc.dram_tensor("out_T", (D, S), F32, kind="ExternalOutput").ap()
    build(nc, *args, out)
    r = _launch(nc, [{"in_" + k: v for k, v in arrays.items()}], core_ids=[0])
    return np.ascontiguousarray(r.results[0]["out_T"].T)[None]
```
